# Optimizing a Trainium2 kernel written in Bass

```python
import math, functools
import jax, jax.numpy as jnp
from jax import lax
import numpy as np

D_MODEL = 1024
BATCH = 1
SEQ = 1024
DEPTH = 1
DEC_BATCH = 8
DEC_SEQ = 4
PAST_LEN = 8192
PAGE_SIZE = 128

POOL_WIDTH = D_MODEL // 2
POOL_WINDOWS = (2, 4, 8, 16)
N_POOL_GROUPS = len(POOL_WINDOWS)
POOL_GROUP = POOL_WIDTH // N_POOL_GROUPS
POOL_PAD = max(POOL_WINDOWS) - 1
N_HEADS = 8
N_KV_HEADS = 2
HEAD_DIM = 64
GQA_GROUP = N_HEADS // N_KV_HEADS
ATTN_WIDTH = N_HEADS * HEAD_DIM
WINDOW = 128
ATTN_BLOCK = 128
D_FF = 4 * D_MODEL
RMS_EPS = 1e-6
NEG_INF = -1e30
IN_SIZES = (POOL_WIDTH, ATTN_WIDTH, N_KV_HEADS * HEAD_DIM, N_KV_HEADS * HEAD_DIM, D_MODEL, D_MODEL)
IN_SPLITS = tuple(int(s) for s in np.cumsum(IN_SIZES)[:-1])
IN_WIDTH = int(sum(IN_SIZES))

kernel_name = "hybrid_pool_swa_gated_decoder_step"

def rms_norm(x, g):
    xf = x.astype(jnp.float32)
    y = xf * lax.rsqrt(jnp.mean(xf * xf, axis=-1, keepdims=True) + RMS_EPS)
    return (y * g.astype(jnp.float32)).astype(x.dtype)

def alibi_slopes():
    s = 2.0 ** (-8.0 * (np.arange(N_HEADS) + 1) / N_HEADS)
    return jnp.asarray(s, dtype=jnp.float32).reshape(N_KV_HEADS, GQA_GROUP)

def attend(q, k, v, dist, valid, sinks):
    scale = HEAD_DIM ** -0.5
    s = jnp.einsum('...qhgd,...khd->...hgqk', q, k, preferred_element_type=jnp.float32) * scale
    d = dist[..., None, None, :, :].astype(jnp.float32)
    s = s - alibi_slopes()[:, :, None, None] * d
    s = jnp.where(valid[..., None, None, :, :], s, NEG_INF)
    sink = sinks.astype(jnp.float32).reshape(N_KV_HEADS, GQA_GROUP)[:, :, None, None]
    m = jnp.maximum(jnp.max(s, axis=-1, keepdims=True), sink)
    p = jnp.exp(s - m)
    den = jnp.sum(p, axis=-1, keepdims=True) + jnp.exp(sink - m)
    return jnp.einsum('...hgqk,...khd->...qhgd', (p / den).astype(v.dtype), v)

def swa_prompt(q, k, v, sinks):
    B, T = q.shape[0], q.shape[1]
    nb = T // ATTN_BLOCK
    qb = q.reshape(B, nb, ATTN_BLOCK, N_KV_HEADS, GQA_GROUP, HEAD_DIM)
    kb = k.reshape(B, nb, ATTN_BLOCK, N_KV_HEADS, HEAD_DIM)
    vb = v.reshape(B, nb, ATTN_BLOCK, N_KV_HEADS, HEAD_DIM)
    kc = jnp.concatenate([jnp.concatenate([jnp.zeros_like(kb[:, :1]), kb[:, :-1]], axis=1), kb], axis=2)
    vc = jnp.concatenate([jnp.concatenate([jnp.zeros_like(vb[:, :1]), vb[:, :-1]], axis=1), vb], axis=2)
    blk = jnp.arange(nb)[:, None] * ATTN_BLOCK
    pos_q = blk + jnp.arange(ATTN_BLOCK)[None, :]
    pos_k = blk - ATTN_BLOCK + jnp.arange(2 * ATTN_BLOCK)[None, :]
    dist = pos_q[:, :, None] - pos_k[:, None, :]
    valid = (dist >= 0) & (dist < WINDOW) & (pos_k[:, None, :] >= 0)
    o = attend(qb, kc, vc, dist, valid, sinks)
    o = o.reshape(B, T, N_KV_HEADS, GQA_GROUP, HEAD_DIM)
    return o, k[:, -WINDOW:], v[:, -WINDOW:]

def swa_sample(q, k, v, sinks, cache_k, cache_v):
    Tn = q.shape[1]
    kc = jnp.concatenate([cache_k.astype(k.dtype), k], axis=1)
    vc = jnp.concatenate([cache_v.astype(v.dtype), v], axis=1)
    pos_q = jnp.arange(Tn)
    pos_k = jnp.arange(WINDOW + Tn) - WINDOW
    dist = pos_q[:, None] - pos_k[None, :]
    valid = (dist >= 0) & (dist < WINDOW)
    o = attend(q, kc, vc, dist, valid, sinks)
    return o, kc[:, -WINDOW:], vc[:, -WINDOW:]

def pool_mix(u, prefix, pos, w_pool, pool_scale):
    B, T, P = u.shape
    up = jnp.concatenate([prefix.astype(u.dtype), u], axis=1)
    upf = up.astype(jnp.float32)
    csum = jnp.concatenate([jnp.zeros((B, 1, P), jnp.float32), jnp.cumsum(upf, axis=1)], axis=1)
    uf = upf[:, POOL_PAD:]
    outs = []
    for g, w in enumerate(POOL_WINDOWS):
        lo, hi = g * POOL_GROUP, (g + 1) * POOL_GROUP
        wsum = csum[:, POOL_PAD + 1:POOL_PAD + 1 + T, lo:hi] - csum[:, POOL_PAD + 1 - w:POOL_PAD + 1 - w + T, lo:hi]
        cnt = jnp.minimum(w, pos + 1).astype(jnp.float32)[None, :, None]
        outs.append(wsum / cnt - uf[:, :, lo:hi])
    d = jnp.stack(outs, axis=2).astype(u.dtype)
    y = jnp.einsum('btgc,gcd->btgd', d, w_pool).reshape(B, T, P) * pool_scale
    return y, up[:, -POOL_PAD:]

def block(x, c, w_ada, b_ada, g1, w_in, w_pool, pool_scale, sinks, w_a, w_b, w_out,
          g2, w_up, w_down, pool_prefix, pos, attn_fn):
    B, T, _ = x.shape
    mod = (jax.nn.silu(c) @ w_ada + b_ada)[:, None, :]
    sh1, sc1, gt1, sh2, sc2, gt2 = jnp.split(mod, 6, axis=-1)
    h = rms_norm(x, g1) * (1 + sc1) + sh1
    z = h @ w_in
    u, q, k, v, ga, gb = jnp.split(z, IN_SPLITS, axis=-1)
    a, new_pool = pool_mix(u, pool_prefix, pos, w_pool, pool_scale)
    q = q.reshape(B, T, N_KV_HEADS, GQA_GROUP, HEAD_DIM)
    k = k.reshape(B, T, N_KV_HEADS, HEAD_DIM)
    v = v.reshape(B, T, N_KV_HEADS, HEAD_DIM)
    o, new_k, new_v = attn_fn(q, k, v, sinks)
    br_a = a @ w_a
    br_b = o.reshape(B, T, ATTN_WIDTH) @ w_b
    merged = jax.nn.sigmoid(ga) * br_a + jax.nn.sigmoid(gb) * br_b
    x = x + gt1 * (merged @ w_out)
    h2 = rms_norm(x, g2) * (1 + sc2) + sh2
    x = x + gt2 * (jnp.square(jax.nn.relu(h2 @ w_up)) @ w_down)
    return x, new_k, new_v, new_pool

def setup_inputs(seed: int = 0) -> dict:
    key = jax.random.key(seed)
    ks = jax.random.split(key, 24)
    f32 = jnp.float32
    nrm = lambda k, shape, s: jax.random.normal(k, shape, f32) * s
    return {
        "x_prompt": nrm(ks[0], (BATCH, SEQ, D_MODEL), 1.0),
        "x_sample": nrm(ks[1], (DEC_BATCH, DEC_SEQ, D_MODEL), 1.0),
        "cache_k": nrm(ks[2], (DEPTH, DEC_BATCH, WINDOW, N_KV_HEADS, HEAD_DIM), 1.0),
        "cache_v": nrm(ks[3], (DEPTH, DEC_BATCH, WINDOW, N_KV_HEADS, HEAD_DIM), 1.0),
        "state_pool": nrm(ks[4], (DEPTH, DEC_BATCH, POOL_PAD, POOL_WIDTH), 1.0),
        "c_prompt": nrm(ks[5], (BATCH, D_MODEL), 1.0),
        "c_sample": nrm(ks[6], (DEC_BATCH, D_MODEL), 1.0),
        "w_ada": nrm(ks[7], (DEPTH, D_MODEL, 6 * D_MODEL), 0.5 * D_MODEL ** -0.5),
        "b_ada": nrm(ks[8], (DEPTH, 6 * D_MODEL), 0.01),
        "norm1_g": 1.0 + nrm(ks[9], (DEPTH, D_MODEL), 0.05),
        "w_in": nrm(ks[10], (DEPTH, D_MODEL, IN_WIDTH), D_MODEL ** -0.5),
        "w_pool": nrm(ks[11], (DEPTH, N_POOL_GROUPS, POOL_GROUP, POOL_GROUP), POOL_GROUP ** -0.5),
        "pool_scale": 1.0 + nrm(ks[12], (DEPTH, POOL_WIDTH), 0.1),
        "attn_sinks": nrm(ks[13], (DEPTH, N_HEADS), 1.0),
        "w_a": nrm(ks[14], (DEPTH, POOL_WIDTH, D_MODEL), POOL_WIDTH ** -0.5),
        "w_b": nrm(ks[15], (DEPTH, ATTN_WIDTH, D_MODEL), ATTN_WIDTH ** -0.5),
        "w_out": nrm(ks[16], (DEPTH, D_MODEL, D_MODEL), D_MODEL ** -0.5),
        "norm2_g": 1.0 + nrm(ks[17], (DEPTH, D_MODEL), 0.05),
        "w_up": nrm(ks[18], (DEPTH, D_MODEL, D_FF), D_MODEL ** -0.5),
        "w_down": nrm(ks[19], (DEPTH, D_FF, D_MODEL), D_FF ** -0.5),
        "final_g": 1.0 + nrm(ks[20], (D_MODEL,), 0.05),
    }

def reference(x_prompt, x_sample, cache_k, cache_v, state_pool, c_prompt, c_sample,
              w_ada, b_ada, norm1_g, w_in, w_pool, pool_scale, attn_sinks, w_a, w_b,
              w_out, norm2_g, w_up, w_down, final_g):
    T, Tn = x_prompt.shape[1], x_sample.shape[1]
    pos_p = jnp.arange(T)
    pos_s = PAST_LEN + jnp.arange(Tn)
    xp, xs = x_prompt, x_sample
    kp_l, vp_l, pp_l, ks_l, vs_l, ps_l = [], [], [], [], [], []
    for l in range(DEPTH):
        lw = (w_ada[l], b_ada[l], norm1_g[l], w_in[l], w_pool[l], pool_scale[l], attn_sinks[l],
              w_a[l], w_b[l], w_out[l], norm2_g[l], w_up[l], w_down[l])
        prefix_p = jnp.zeros((xp.shape[0], POOL_PAD, POOL_WIDTH), xp.dtype)
        xp, kp, vp, pp = block(xp, c_prompt, *lw, prefix_p, pos_p, swa_prompt)
        attn_s = functools.partial(swa_sample, cache_k=cache_k[l], cache_v=cache_v[l])
        xs, k_s, v_s, p_s = block(xs, c_sample, *lw, state_pool[l], pos_s, attn_s)
        kp_l.append(kp); vp_l.append(vp); pp_l.append(pp)
        ks_l.append(k_s); vs_l.append(v_s); ps_l.append(p_s)
    y_prompt = rms_norm(xp, final_g)
    y_sample = rms_norm(xs, final_g)
    new_k_prompt = jnp.stack(kp_l, axis=0)
    new_v_prompt = jnp.stack(vp_l, axis=0)
    new_pool_prompt = jnp.stack(pp_l, axis=0)
    new_k_sample = jnp.stack(ks_l, axis=0)
    new_v_sample = jnp.stack(vs_l, axis=0)
    new_pool_sample = jnp.stack(ps_l, axis=0)
    return (y_prompt, y_sample, new_k_prompt, new_v_prompt, new_pool_prompt, new_k_sample, new_v_sample, new_pool_sample)


_drawn_inputs = setup_inputs


def setup_inputs(seed=0):
    import zlib

    import numpy as np

    out = dict(_drawn_inputs(seed))
    spreads = {}
    factors = {'b_ada': 3.522, 'pool_scale': 3.581, 'attn_sinks': 8.0, 'norm2_g': 2.732}
    for name, (base, spread) in spreads.items():
        noise = np.random.default_rng([zlib.crc32(name.encode()), seed]).standard_normal(out[name].shape)
        drawn = base * np.exp(spread * noise) if base else spread * noise
        out[name] = __import__('jax').numpy.asarray(drawn.astype(out[name].dtype))
    for name, factor in factors.items():
        out[name] = (out[name] * factor).astype(out[name].dtype)
    return out
```

```python
import concourse.bass as bass
from concourse import mybir
from contextlib import ExitStack

F32 = mybir.dt.float32
F32R = mybir.dt.float32r
ALU = mybir.AluOpType
ACT = mybir.ActivationFunctionType
AX = mybir.AxisListType

P = 128
D = 1024
DK = D // P
TP = 1024
NB, NT = 8, 4
TS = NB * NT
T = TP + TS
TT = T // 3
BLK = TP // P
HD, NH, NKV = 64, 8, 2
G = NH // NKV
WIN = 128
DFF = 4 * D
PW = D // 2
NG = 4
PAD = 15
NMOD = 6 * DK
NC = 1 + NB
SK = NB * WIN + TS
EPS = 1e-6
SCALE = HD ** -0.5

U_Z, N_Z = 0, 10
U_G, N_G = 10, 16
U_AB, N_AB = 26, 8
U_O, N_O = 34, 8
U_F = 42
N_U = U_F + 64
USE_R1 = 0
USE_Z = 1
USE_SS = 27
USE_POOL = 29
USE_AB = 33
USE_O = 41
USE_R2 = 49
USE_F = 50


LOADS_AB = 16 * (U_AB // 2) + 32
LOADS_O = LOADS_AB + 48 * (N_AB // 2)


def use_of(u):
    if u < U_AB:
        return USE_Z + u
    return USE_AB + (u - U_AB) if u < U_F else USE_F + (u - U_F)


def loads_of(u):
    if u < U_AB:
        return 16 * (u // 2 + 1) + 16 * min(u // 2, 2)
    if u < U_O:
        return LOADS_AB + 48 * ((u - U_AB) // 2 + 1)
    return LOADS_O + 16 * ((u - U_O) // 2 + 1)


def wait(eng, sem, value):
    if isinstance(value, int) and value <= 0:
        return
    eng.wait_ge(sem, value)


class Chain:

    def __init__(self, eng, sem):
        self.eng, self.sem, self.base, self.k = eng, sem, 0, 0

    def step(self, ins):
        self.k += 1
        ins.then_inc(self.sem, 1)
        self.eng.wait_ge(self.sem, self.base + self.k)

    def enter(self, i, first, per):
        self.start = self.base + self.k
        self.base = self.start + (i - first) * per
        self.k = 0

    def leave(self, turns, per):
        assert self.k == per, (self.k, per)
        self.base, self.k = self.start + turns * per, 0


def hybrid_decoder_step(nc, a, outs):
    y_p, y_s, nk_p, nv_p, npool_p, nk_s, nv_s, npool_s = outs
    ctx = ExitStack()
    with ctx:
        def sem(name):
            return ctx.enter_context(nc.semaphore(name))

        arena_bytes = 212800
        arena = ctx.enter_context(nc.sbuf_tensor("arena", [P, arena_bytes // 4], F32))
        arena_at = 16512

        def at(name, offset, shape, dt=F32):
            size = 4
            for s in shape[1:]:
                size *= s
            assert offset % 32 == 0 and offset + size <= arena_bytes, (name, offset, size)
            return nc.alloc_sbuf_tensor_at(name, shape, dt, offset=arena_at + offset)

        ROW = 4 * T
        RA, RB, RC, RD = 0, 8 * ROW, 16 * ROW, 32 * ROW
        RE = RC + 10 * ROW
        RW = RD + 8 * ROW
        RM = RW + 6 * 4096

        w_raw = [at(f"w_raw{s}", RW + 4096 * s, [P, DK, P]) for s in range(2)]
        w_hi = [at(f"w_hi{s}", RW + 8192 + 4096 * s, [P, DK, P], F32R) for s in range(2)]
        w_lo = [at(f"w_lo{s}", RW + 16384 + 4096 * s, [P, DK, P], F32R) for s in range(2)]
        m = RM

        def small(name, shape, dt=F32):
            nonlocal m
            size = 4
            for s in shape[1:]:
                size *= s
            t = at(name, m, shape, dt)
            m += (size + 31) // 32 * 32
            return t

        mod = small("mod", [P, NMOD, NC])
        vec = small("vec", [P, 68])
        ident = small("ident", [P, P])
        ones = small("ones", [P, P])
        gain1 = small("gain1", [P, DK, NC])
        gain2 = small("gain2", [P, DK, NC])
        cT = small("cT", [P, DK, NC])
        pool_s = small("pool_s", [P, NG, NB, PAD + NT])
        inv_cnt = small("inv_cnt", [P, NG, 16])
        sink_p = small("sink_p", [P, NH])
        sink_s = small("sink_s", [P, NKV])
        ssq = small("ssq", [P, 9])
        rms = small("rms", [P, 9])
        half = small("half", [P, 9])
        mx = small("mx", [P, 2, G])
        nmx = small("nmx", [P, 2, G])
        dsk = small("dsk", [P, 2, G])
        esk = small("esk", [P, 2, G])
        rsum = small("rsum", [P, 2, G])
        rden = small("rden", [P, 2, G])
        fin_ss = small("fin_ss", [P, 2, 1])
        fin_r = small("fin_r", [P, 2, 1])
        v_st = small("v_st", [P, 2, P])
        smp_t = small("smp_t", [P, DK, NB, NT])
        pool_last = small("pool_last", [P, NG, PAD])
        m_pool = m
        assert m + 8448 + 1216 <= arena_bytes
        R = small("R", [P, T])
        acc = small("acc", [P, T])
        win_a = at("win_a", m_pool, [P, TP])
        win_b = at("win_b", m_pool + 4096, [P, TP])
        win_sa = at("win_sa", m_pool + 8192, [P, NB, PAD + NT])
        win_sb = at("win_sb", m_pool + 8192 + 608, [P, NB, PAD + NT])
        kv_out = at("kv_out", m_pool, [P, 512])
        poolp_out = at("poolp_out", m_pool + 2048, [P, 512])
        pool_tail = at("pool_tail", m_pool + 6144, [P, NG, NB * PAD])
        pools_out = at("pools_out", m_pool + 4096, [P, 512])

        h_hi = at("h_hi", RA, [P, DK, T], F32R)
        h_lo = at("h_lo", RB, [P, DK, T], F32R)
        o_hi = at("o_hi", RA, [P, 4, T], F32R)
        o_lo = at("o_lo", RA + 4 * ROW, [P, 4, T], F32R)
        a_hi = at("a_hi", RB, [P, 4, T], F32R)
        a_lo = at("a_lo", RB + 4 * ROW, [P, 4, T], F32R)
        x1 = at("x1", RA, [P, DK, T])
        ff_hi = at("ff_hi", RB, [P, DK, T], F32R)
        c_row = at("c_row", RB, [P, D])
        c_sil = at("c_sil", RB + 4096, [P, D])
        v_row = at("v_row", RB + 8192, [P, P])
        s_row = at("s_row", RB + 8704, [P, PW])
        diag1 = at("diag1", RB + 12288, [P, 9, P])
        sq_x = at("sq_x", RB + 17408, [P, D])
        xT = at("xT", RC, [P, DK, T])
        z = at("z", RC, [P, 10, T])
        mg_hi = at("mg_hi", RC, [P, DK, T], F32R)
        mg_lo = at("mg_lo", RC + 8 * ROW, [P, DK, T], F32R)
        h2_hi = at("h2_hi", RC, [P, DK, T], F32R)
        h2_lo = at("h2_lo", RC + 8 * ROW, [P, DK, T], F32R)
        x_in = at("x_in", RE, [P, 4, D])
        ada_row = at("ada_row", RE + 16384, [P, 2, 512])
        nrm_t = at("nrm_t", RE + 20480, [P, 2, 512])
        bias_p = at("bias_p", RE, [P, NH, 2 * P])
        pr = at("pr", RE + 8192, [P, 2, G, 2 * P])
        pt_hi = at("pt_hi", RE + 16384, [P, 2, G * P], F32R)
        pt_lo = at("pt_lo", RE + 20480, [P, 2, G * P], F32R)
        ks_hi = at("ks_hi", RE, [P, SK], F32R)
        ks_lo = at("ks_lo", RE + 4224, [P, SK], F32R)
        ps = at("ps", RE + 8448, [P, 2, SK])
        pst_hi = at("pst_hi", RE + 16896, [P, 9, P], F32R)
        ada_w = at("ada_w", RD, [P, 2, DK, 512])
        q_hi = at("q_hi", RD, [P, 4, P], F32R)
        q_lo = at("q_lo", RD + 2048, [P, 4, P], F32R)
        k_hi = at("k_hi", RD + 4096, [P, 2 * P], F32R)
        k_lo = at("k_lo", RD + 5120, [P, 2 * P], F32R)
        v_hi = at("v_hi", RD + 6144, [P, 2, P], F32R)
        v_lo = at("v_lo", RD + 7168, [P, 2, P], F32R)
        g_out = at("g_out", RD + 8192, [P, 2, T])
        kc = at("kc", RD + 16640, [P, NB, P])
        vc = at("vc", RD + 20736, [P, NB, P])
        bias_s = at("bias_s", RD + 24832, [P, NKV, SK])
        vs_hi = at("vs_hi", RD, [P, 9, P], F32R)
        vs_lo = at("vs_lo", RD + 4608, [P, 9, P], F32R)
        pst_lo = at("pst_lo", RD + 9216, [P, 9, P], F32R)
        qs_hi = at("qs_hi", RD + 13824, [P, 4, TS], F32R)
        qs_lo = at("qs_lo", RD + 14336, [P, 4, TS], F32R)
        d_hi = [at(f"d_hi{s}", RD + ROW * (4 + 2 * s), [P, T], F32R) for s in range(2)]
        d_lo = [at(f"d_lo{s}", RD + ROW * (5 + 2 * s), [P, T], F32R) for s in range(2)]
        wp_raw = at("wp_raw", RE + 21504, [P, NG, P])
        wp_hi = at("wp_hi", RC, [P, NG, P], F32R)
        wp_lo = at("wp_lo", RC + 2048, [P, NG, P], F32R)
        a_t = at("a_t", RC + ROW, [P, 2, TT])
        g_in = at("g_in", RD, [P, 2, T])
        mt = at("mt", RD + 4 * ROW, [P, 2, 3, TT])
        x_res = at("x_res", RD, [P, 2, T])
        sq_t = at("sq_t", RD + 2 * ROW, [P, 3, TT])
        diag2 = at("diag2", RD, [P, 9, P])
        nrm_t2 = at("nrm_t2", RD + 4608, [P, 2, 512])
        ff_lo = at("ff_lo", RD, [P, DK, T], F32R)
        r_t = at("r_t", m_pool, [P, 2, TT])
        f_t = at("f_t", m_pool + 8 * TT, [P, 2, TT])
        y_st = at("y_st", RC, [P, 2, DK, P])
        y_sq = at("y_sq", RC + 8192, [P, D])
        y_out = at("y_out", RC + 12288, [P, 2, D])
        fin_g = at("fin_g", RC + 20480, [P, D])

        psum = ctx.enter_context(nc.psum_tensor("psum", [P, 8, 512], F32))

        gates_d = nc.dram_tensor("gates_scratch", [8, P, 2, T], F32, kind="Internal").ap()
        xT_d = nc.dram_tensor("xT_scratch", [P, DK, T], F32, kind="Internal").ap()

        w_in = [sem("w_in0"), sem("w_in1")]
        w_hi_done, w_lo_done = sem("w_hi_done"), sem("w_lo_done")
        ready = [sem(f"ready{t}") for t in range(3)]
        free = [sem(f"free{t}") for t in range(3)]
        readyB = [sem(f"readyB{t}") for t in range(3)]
        freeB = [sem(f"freeB{t}") for t in range(3)]
        c_in, v_in, s_in, tab_in = sem("c_in"), sem("v_in"), sem("s_in"), sem("tab_in")
        x_land = [sem(f"x_land{s}") for s in range(4)]
        x_sq, xt_ready, xt_read, xt_saved = sem("x_sq"), sem("xt_ready"), sem("xt_read"), sem("xt_saved")
        const_done, c_sig, c_silu = sem("const_done"), sem("c_sig"), sem("c_silu")
        cvt_ready, cvt_read, st_ready, st_read = sem("cvt_ready"), sem("cvt_read"), sem("st_ready"), sem("st_read")
        ada_in = [sem("ada_in0"), sem("ada_in1")]
        row_ready, row_read, modt_ready, mod_done = sem("row_ready"), sem("row_read"), sem("modt_ready"), sem("mod_done")
        ms_done, rms_done, diag_done = sem("ms_done"), sem("rms_done"), sem("diag_done")
        n_tmp, n_hi, h_done = sem("n_tmp"), sem("n_hi"), sem("h_done")
        pool_done = sem("pool_done")
        stage_done, vt_ready, v_hi_done, v_lo_done = sem("stage_done"), sem("vt_ready"), sem("v_hi_done"), sem("v_lo_done")
        s_ready, nmax_done, exp_done, p_done = sem("s_ready"), sem("nmax_done"), sem("exp_done"), sem("p_done")
        pt_ready, pt_hi_done, pt_lo_done, o_ready, o_read = sem("pt_ready"), sem("pt_hi_done"), sem("pt_lo_done"), sem("o_ready"), sem("o_read")
        g_saved, kvc_in, bs_in, bp_in = sem("g_saved"), sem("kvc_in"), sem("bs_in"), sem("bp_in")
        out_t_ready, out_t_read, kct_ready, kct_hi, ks_done, vs_done, qs_done = (
            sem("out_t_ready"), sem("out_t_read"), sem("kct_ready"), sem("kct_hi"), sem("ks_done"), sem("vs_done"), sem("qs_done"))
        sst_ready, sst_hi, sst_lo, so_ready, so_read = sem("sst_ready"), sem("sst_hi"), sem("sst_lo"), sem("so_ready"), sem("so_read")
        ss_nmax, ss_exp, ss_p = sem("ss_nmax"), sem("ss_exp"), sem("ss_p")
        d_hi_done, d_lo_done, o_hi_done, o_lo_done = sem("d_hi_done"), sem("d_lo_done"), sem("o_hi_done"), sem("o_lo_done")
        a_hi_done, a_lo_done = sem("a_hi_done"), sem("a_lo_done")
        g_in_sem, sig_done, sum_done, mg_hi_done, mg_lo_done = (
            sem("g_in_sem"), sem("sig_done"), sem("sum_done"), sem("mg_hi_done"), sem("mg_lo_done"))
        xr_in, x1_done, sq_done, acc_done = [sem("xr_in0"), sem("xr_in1")], sem("x1_done"), sem("sq_done"), sem("acc_done")
        ss_ready = sem("ss_ready")
        ff_sq, ff_hi_done, ff_lo_done = sem("ff_sq"), sem("ff_hi_done"), sem("ff_lo_done")
        y_staged, yt_ready, yss_done, yms_done, yr_done, y_done, fg_in = (
            sem("y_staged"), sem("yt_ready"), sem("yss_done"), sem("yms_done"), sem("yr_done"), sem("y_done"), sem("fg_in"))
        y_sent = [sem("y_sent0"), sem("y_sent1")]
        qk_lo_done = sem("qk_lo_done")
        wp_in, wp_done = sem("wp_in"), sem("wp_done")
        sent = sem("sent")
        act_c, dve_c, pool_c = sem("act_chain"), sem("dve_chain"), sem("pool_chain")

        def cols(t):
            return slice(t * TT, (t + 1) * TT)

        ada_col = [0, 2, 1, 3] + list(range(4, 12))

        block = ctx.enter_context(nc.Block())

        @block.sync
        def _(sp):
            def load_x(b):
                rows = P if b < BLK else TS
                if b >= 4:
                    sp.wait_ge(x_sq, b - 3)
                    sp.wait_ge(xt_ready, b - 3)
                src = a["x_prompt"][0, b * P:(b + 1) * P, :] if b < BLK else a["x_sample"].rearrange("b t d -> (b t) d")
                sp.dma_start(x_in[0:rows, b % 4, :], src).then_inc(x_land[b % 4], 16)

            def load_ada(n, col):
                wait(sp, row_ready, n - 1)
                sp.dma_start(ada_w[:, n % 2, :, :], a["w_ada"][0, :, col].rearrange("(k p) c -> p k c", p=P))\
                    .then_inc(ada_in[n % 2], 16)

            def load_w(slot, src, free_count):
                wait(sp, w_lo_done, free_count)
                sp.dma_start(w_raw[slot][:, :, :], src.rearrange("(k p) c -> p k c", p=P)).then_inc(w_in[slot], 16)

            w_in_d, z_col = a["w_in"][0], [PW + NH * HD, PW + NH * HD + NKV * HD] + [None] * 4 + [g * P for g in range(NG)]

            def load_z(u):
                if z_col[u] is not None:
                    load_w(u % 2, w_in_d[:, z_col[u]:z_col[u] + P], u - 1)
                    return
                wait(sp, w_lo_done, u - 1)
                c = PW + (u - 2) * HD
                src = w_in_d[:, PW:PW + NH * HD].rearrange("(k p) (v g c) -> p k v g c", p=P, v=NKV, g=G)[:, :, :, u - 2, :]
                sp.dma_start(w_raw[u % 2][:, :, 0:HD], src[:, :, 0, :]).then_inc(w_in[u % 2], 16)
                sp.dma_start(w_raw[u % 2][:, :, HD:P], src[:, :, 1, :]).then_inc(w_in[u % 2], 16)

            for b in range(4):
                load_x(b)
            load_ada(0, slice(ada_col[0] * 512, ada_col[0] * 512 + 512))
            for b in range(4, 9):
                load_x(b)
            load_ada(1, slice(ada_col[1] * 512, ada_col[1] * 512 + 512))
            load_z(0)
            load_z(1)
            for n in (2, 3):
                load_ada(n, slice(ada_col[n] * 512, ada_col[n] * 512 + 512))
            sp.wait_ge(xt_read, 9)
            sp.dma_start(xT_d, xT[:, :, :]).then_inc(xt_saved, 16)
            for p in range(4):
                load_z(2 * p + 2)
                load_ada(4 + 2 * p, slice((4 + 2 * p) * 512, (5 + 2 * p) * 512))
                load_z(2 * p + 3)
                load_ada(5 + 2 * p, slice((5 + 2 * p) * 512, (6 + 2 * p) * 512))
            z0 = 2 * PW + 2 * NKV * HD

            def gate_loads(i, g_from):
                load_w(0, w_in_d[:, bass.ds(z0 + i * P, P)], g_from)
                load_w(1, w_in_d[:, bass.ds(z0 + D + i * P, P)], g_from + 1)

            gate_loads(0, U_G - 1)
            sp.wait_ge(mod_done, 12)
            sp.dma_start(bias_p[:, :, :], a["alibi_prompt"]).then_inc(bp_in, 16)
            sp.dma_start(kc[:, :, :], a["cache_k"][0].rearrange("b w h d -> w b (h d)")).then_inc(kvc_in, 16)
            sp.dma_start(vc[:, :, :], a["cache_v"][0].rearrange("b w h d -> w b (h d)")).then_inc(kvc_in, 16)
            sp.dma_start(bias_s[:, :, :], a["alibi_sample"]).then_inc(bs_in, 16)
            for cache, new in ((a["cache_k"], nk_s), (a["cache_v"], nv_s)):
                sp.dma_start(new[0, :, 0:WIN - NT].rearrange("b w h d -> b w (h d)"),
                             cache[0, :, NT:WIN].rearrange("b w h d -> b w (h d)")).then_inc(sent, 16)
            def gate_store(i):
                for t in range(3):
                    sp.wait_ge(free[t], USE_Z + U_G + 2 * i + 2)
                sp.dma_start(gates_d[bass.ds(i, 1)].rearrange("o p g t -> (o p) g t"), g_out[:, :, :]).then_inc(g_saved, 16)

            with sp.Fori(1, BLK) as i:
                gate_loads(i, U_G - 1 + 2 * i)
                gate_store(i - 1)

            def load_ab(j, slot, free_count):
                wait(sp, w_lo_done, free_count)
                c = bass.ds(j * P, P)
                sp.dma_start(w_raw[slot][:, 0:4, :], a["w_a"][0][:, c].rearrange("(k p) c -> p k c", p=P)).then_inc(w_in[slot], 16)
                w_b = a["w_b"][0][:, c].rearrange("(v g p) c -> v p g c", v=NKV, g=G)
                for v in range(NKV):
                    sp.dma_start(w_raw[slot][v * HD:(v + 1) * HD, 4:8, :], w_b[v]).then_inc(w_in[slot], 16)

            load_ab(0, 0, U_AB - 1)
            load_ab(1, 1, U_AB)
            gate_store(BLK - 1)
            sp.wait_ge(o_ready, 2 * BLK)
            sp.dma_start(wp_raw[:, :, :], a["w_pool"][0].rearrange("g c d -> c g d")).then_inc(wp_in, 16)
            sp.wait_ge(out_t_read, 4)
            sp.dma_start(nk_p[0, 0].rearrange("w h d -> w (h d)"), kv_out[:, 0:P]).then_inc(sent, 16)
            sp.dma_start(nv_p[0, 0].rearrange("w h d -> w (h d)"), kv_out[:, P:2 * P]).then_inc(sent, 16)
            for new, c in ((nk_s, 2 * P), (nv_s, 3 * P)):
                for b in range(NB):
                    sp.dma_start(new[0, b, WIN - NT:WIN].rearrange("w h d -> w (h d)"), kv_out[b * NT:(b + 1) * NT, c:c + P]).then_inc(sent, 16)
            sp.dma_start(npool_p[0, 0], poolp_out[0:PAD, :]).then_inc(sent, 16)
            sp.dma_start(npool_s[0].rearrange("b r c -> (b r) c"), pools_out[0:NB * PAD, :]).then_inc(sent, 16)

            def gates_back(j):
                wait(sp, free[2], USE_AB + j)
                sp.dma_start(g_in[:, :, :], gates_d[bass.ds(j, 1)].rearrange("o p g t -> (o p) g t")).then_inc(g_in_sem, 16)

            sp.wait_ge(g_saved, 16 * BLK)
            sp.wait_ge(so_ready, 2)
            gates_back(0)
            w_out_d = a["w_out"][0]
            with sp.Fori(1, 4) as p:
                load_ab(2 * p, 0, U_AB - 1 + 2 * p)
                gates_back(2 * p - 1)
                load_ab(2 * p + 1, 1, U_AB + 2 * p)
                gates_back(2 * p)
            load_w(0, w_out_d[:, 0:P], U_O - 1)
            gates_back(7)
            load_w(1, w_out_d[:, P:2 * P], U_O)
            sp.wait_ge(xt_saved, 16)

            def load_res(j, slot):
                wait(sp, x1_done, j - 1)
                sp.dma_start(x_res[:, slot, :], xT_d[:, bass.ds(j, 1), :].rearrange("p o t -> p (o t)")).then_inc(xr_in[slot], 16)

            sp.wait_ge(mg_lo_done, 3 * N_AB)
            load_res(0, 0)
            load_res(1, 1)
            with sp.Fori(1, 4) as p:
                load_w(0, w_out_d[:, bass.ds(2 * p * P, P)], U_O - 1 + 2 * p)
                load_res(2 * p, 0)
                load_w(1, w_out_d[:, bass.ds((2 * p + 1) * P, P)], U_O + 2 * p)
                load_res(2 * p + 1, 1)
            w_up_d, w_down_d = a["w_up"][0], a["w_down"][0]
            with sp.Fori(0, 4) as g:
                with sp.Fori(0, 4) as i:
                    for s in range(2):
                        load_w(s, w_up_d[:, bass.ds((8 * g + 2 * i + s) * P, P)], U_F - 1 + 16 * g + 2 * i + s)
                with sp.Fori(0, 4) as i:
                    for s in range(2):
                        load_w(s, w_down_d[bass.ds(g * D, D), bass.ds((2 * i + s) * P, P)], U_F + 7 + 16 * g + 2 * i + s)
            sp.wait_ge(ready[2], USE_F + 64)
            sp.dma_start(fin_g[:, :], a["final_g"].partition_broadcast(P)).then_inc(fg_in, 16)
            with sp.Fori(0, 4) as p:
                for s in range(2):
                    b = 2 * p + s
                    sp.wait_ge(y_done, b + 1)
                    sp.dma_start(y_p[0, bass.ds(b * P, P), :], y_out[:, s, :]).then_inc(y_sent[s], 16)
            sp.wait_ge(y_done, 9)
            sp.dma_start(y_s.rearrange("b t d -> (b t) d"), y_out[0:TS, 0, :]).then_inc(y_sent[0], 16)
            sp.wait_ge(y_sent[0], 16 * 5)
            sp.wait_ge(y_sent[1], 16 * 4)
            sp.wait_ge(sent, 16 * (2 + 2 + 16 + 2))

        @block.tensor
        def _(pe):
            mm = nc.tensor.matmul

            def mm3(out, whi, wlo, rhi, rlo, first, last):
                mm(out, whi, rhi, start=first, stop=False)
                mm(out, whi, rlo, start=False, stop=False)
                return mm(out, wlo, rhi, start=False, stop=last)

            def project(u, use, slot, rhi, rlo, before=None):
                pe.wait_ge(w_lo_done, u + 1)
                for t in range(3):
                    if before:
                        before(t)
                    pe.wait_ge(free[t], use)
                    for k in range(DK):
                        last = mm3(psum[:, t, 0:TT], w_hi[slot][:, k, :], w_lo[slot][:, k, :], rhi[:, k, cols(t)], rlo[:, k, cols(t)], k == 0, k == DK - 1)
                    last.then_inc(ready[t], 1)

            pe.wait_ge(const_done, 4)
            pe.wait_ge(c_silu, 1)
            for j in range(DK):
                nc.tensor.transpose(psum[:, 3, 16 * j:16 * j + NC], c_sil[0:NC, j * P:(j + 1) * P], ident[0:NC, 0:NC])
            pe.wait_ge(v_in, 64)
            nc.tensor.transpose(psum[:, 3, P:P + 68], v_row[0:68, :], ident[0:68, 0:68]).then_inc(cvt_ready, 1)
            pe.wait_ge(s_in, 16)
            for g in range(NG):
                last = nc.tensor.transpose(psum[:, 2, 120 * g:120 * g + 120], s_row[0:120, g * P:(g + 1) * P], ident[0:120, 0:120])
            last.then_inc(st_ready, 1)
            for b in range(BLK + 1):
                rows = P if b < BLK else TS
                pe.wait_ge(x_land[b % 4], 16 * (b // 4 + 1))
                wait(pe, xt_read, b - 1)
                for j in range(DK):
                    bank = 4 + 2 * (b % 2) + j // 4
                    last = nc.tensor.transpose(psum[:, bank, (j % 4) * P:(j % 4) * P + rows], x_in[0:rows, b % 4, j * P:(j + 1) * P], ident[0:rows, 0:rows])
                last.then_inc(xt_ready, 1)

            def ada_rows(n, s):
                pe.wait_ge(ada_in[s], 8 * (n - s) + 16)
                wait(pe, row_read, n - 1)
                for k in range(DK):
                    last = mm(psum[0:NC, 3 + s, :], cT[:, k, :], ada_w[:, s, k, :], start=(k == 0), stop=(k == DK - 1))
                last.then_inc(row_ready, 1)

            def ada_turn(n, s):
                pe.wait_ge(row_read, n + 1)
                wait(pe, mod_done, n - 1)
                for q in range(4):
                    last = mm(psum[:, 5 + s, 16 * q:16 * q + NC], ada_row[:, s, q * P:(q + 1) * P], ident[:, 0:NC], start=True, stop=True)
                last.then_inc(modt_ready, 1)

            pe.wait_ge(cvt_read, 2)
            ada_rows(0, 0)
            pe.wait_ge(st_read, 1)

            def spread_rms(diag, use, n):
                pe.wait_ge(diag_done, 2 * n + 2)
                for t in range(3):
                    wait(pe, free[t], use)
                for t in range(2):
                    mm(psum[:, t, :], ones[:, :], diag[:, 4 * t:4 * t + 4, :], start=True, stop=True).then_inc(ready[t], 1)
                mm(psum[:, 2, 0:TS], ones[0:TS, :], diag[0:TS, 8, 0:TS], start=True, stop=True).then_inc(ready[2], 1)

            pe.wait_ge(xt_read, 9)
            ada_rows(1, 1)
            spread_rms(diag1, USE_R1, 0)
            ada_turn(0, 0)
            ada_rows(2, 0)
            ada_turn(1, 1)
            ada_rows(3, 1)
            ada_turn(2, 0)
            ada_turn(3, 1)

            def h_there(t):
                pe.wait_ge(h_done, (12, 16, 17)[t])

            project(0, USE_Z, 0, h_hi, h_lo, h_there)
            project(1, USE_Z + 1, 1, h_hi, h_lo)
            with pe.Fori(1, 5) as p:
                project(2 * p, USE_Z + 2 * p, 0, h_hi, h_lo)
                ada_rows(2 * p + 2, 0)
                ada_rows(2 * p + 3, 1)
                project(2 * p + 1, USE_Z + 2 * p + 1, 1, h_hi, h_lo)
                ada_turn(2 * p + 2, 0)
                ada_turn(2 * p + 3, 1)

            def gate_tile(use, slot, t):
                pe.wait_ge(free[t], use)
                for k in range(DK):
                    last = mm3(psum[:, t, 0:TT], w_hi[slot][:, k, :], w_lo[slot][:, k, :], h_hi[:, k, cols(t)], h_lo[:, k, cols(t)], k == 0, k == DK - 1)
                last.then_inc(ready[t], 1)

            def attend(i):
                first = isinstance(i, int)
                kks = [1] if first else [0, 1]
                k0 = P if first else 0
                u = U_G + 2 * i

                def scores(kv):
                    wait(pe, nmax_done, 2 * i + kv)
                    h = slice(kv * HD, (kv + 1) * HD)
                    for c in range(G):
                        last = mm3(psum[:, 3 + c // 2, (c % 2) * 256 + k0:(c % 2) * 256 + 256], q_hi[h, c, :], q_lo[h, c, :],
                                   k_hi[h, k0:256], k_lo[h, k0:256], True, True)
                    last.then_inc(s_ready, 1)

                def turn_probs(kv):
                    pe.wait_ge(p_done, 2 * i + kv + 1)
                    wait(pe, pt_lo_done, 2 * i + kv)
                    for kk in kks:
                        for c in range(G):
                            last = nc.tensor.transpose(psum[:, 5 + kk, c * P:(c + 1) * P], pr[:, kv, c, kk * P:(kk + 1) * P], ident[:, :])
                    last.then_inc(pt_ready, 1)

                def weigh(kv):
                    pe.wait_ge(pt_lo_done, 2 * i + kv + 1)
                    pe.wait_ge(v_lo_done, i + 1)
                    wait(pe, o_read, 2 * i + kv)
                    for kk in kks:
                        last = mm3(psum[:, 7, :], v_hi[:, kk, :], v_lo[:, kk, :], pt_hi[:, kk, :], pt_lo[:, kk, :], kk == kks[0], kk == 1)
                    last.then_inc(o_ready, 1)

                pe.wait_ge(stage_done, i + 1)
                wait(pe, o_read, 2 * i)
                for kk in kks:
                    last = nc.tensor.transpose(psum[:, 7, kk * P:(kk + 1) * P], v_st[:, kk, :], ident[:, :])
                last.then_inc(vt_ready, 1)
                pe.wait_ge(qk_lo_done, i + 1)
                scores(0)
                pe.wait_ge(w_lo_done, u + 1)
                gate_tile(USE_Z + u, 0, 0)
                gate_tile(USE_Z + u, 0, 1)
                turn_probs(0)
                scores(1)
                gate_tile(USE_Z + u, 0, 2)
                weigh(0)
                pe.wait_ge(w_lo_done, u + 2)
                gate_tile(USE_Z + u + 1, 1, 0)
                gate_tile(USE_Z + u + 1, 1, 1)
                turn_probs(1)
                gate_tile(USE_Z + u + 1, 1, 2)
                weigh(1)

            attend(0)
            with pe.Fori(1, BLK) as i:
                attend(i)

            pe.wait_ge(o_read, 2 * BLK)
            pe.wait_ge(pt_lo_done, 2 * BLK)
            for q, (chunk, c0, n) in enumerate(((0, TP - P, P), (1, TP - P, P), (0, TP, TS), (1, TP, TS))):
                last = nc.tensor.transpose(psum[0:n, 5, q * P:(q + 1) * P], z[:, chunk, c0:c0 + n], ident[:, :])
            last.then_inc(out_t_ready, 1)
            pe.wait_ge(pool_done, 1)
            for g in range(NG):
                last = nc.tensor.transpose(psum[0:PAD, 6, g * P:(g + 1) * P], pool_last[:, g, :], ident[:, :])
            last.then_inc(out_t_ready, 1)
            for g in range(NG):
                last = nc.tensor.transpose(psum[0:NB * PAD, 7, g * P:(g + 1) * P], pool_tail[:, g, :], ident[:, :])
            last.then_inc(out_t_ready, 1)
            pe.wait_ge(kvc_in, 32)
            for b in range(NB):
                last = nc.tensor.transpose(psum[:, 3 + b // 4, (b % 4) * P:(b % 4 + 1) * P], kc[:, b, :], ident[:, :])
            last.then_inc(kct_ready, 1)
            pe.wait_ge(ks_done, 1)
            pe.wait_ge(qs_done, 1)
            for kv in range(NKV):
                h = slice(kv * HD, (kv + 1) * HD)
                for t in range(3):
                    pe.wait_ge(free[t], USE_SS + kv)
                    mm3(psum[:, t, 0:TT], qs_hi[h, :, :], qs_lo[h, :, :], ks_hi[h, cols(t)], ks_lo[h, cols(t)], True, True)\
                        .then_inc(ready[t], 1)
            pe.wait_ge(vs_done, 1)
            pe.wait_ge(out_t_read, 4)
            for kv in range(NKV):
                pe.wait_ge(ss_p, kv + 1)
                wait(pe, sst_lo, 2 * kv)
                for cc in range(9):
                    n = P if cc < NB else TS
                    bank = (5, 6, 4)[cc // 4]
                    last = nc.tensor.transpose(psum[0:n, bank, (cc % 4) * P:(cc % 4 + 1) * P], ps[:, kv, cc * P:cc * P + n], ident[:, :])
                last.then_inc(sst_ready, 1)
                pe.wait_ge(sst_lo, 2 * kv + 2)
                wait(pe, so_read, kv)
                for cc in range(9):
                    n = P if cc < NB else TS
                    last = mm3(psum[:, 7, 0:P], vs_hi[0:n, cc, :], vs_lo[0:n, cc, :], pst_hi[0:n, cc, :], pst_lo[0:n, cc, :], cc == 0, cc == 8)
                last.then_inc(so_ready, 1)

            pe.wait_ge(wp_done, 1)
            for g in range(NG):
                pe.wait_ge(d_lo_done, g + 1)
                for t in range(3):
                    pe.wait_ge(free[t], USE_POOL + g)
                    mm3(psum[:, t, 0:TT], wp_hi[:, g, :], wp_lo[:, g, :], d_hi[g % 2][:, cols(t)], d_lo[g % 2][:, cols(t)], True, True)\
                        .then_inc(ready[t], 1)

            def branches(j, slot):
                pe.wait_ge(w_lo_done, U_AB + j + 1)
                for t in range(3):
                    wait(pe, freeB[t], j)
                    for k in range(4):
                        last = mm3(psum[:, 3 + t, 0:TT], w_hi[slot][:, 4 + k, :], w_lo[slot][:, 4 + k, :], o_hi[:, k, cols(t)], o_lo[:, k, cols(t)], k == 0, k == 3)
                    last.then_inc(readyB[t], 1)
                    pe.wait_ge(free[t], USE_AB + j)
                    for k in range(4):
                        last = mm3(psum[:, t, 0:TT], w_hi[slot][:, k, :], w_lo[slot][:, k, :], a_hi[:, k, cols(t)], a_lo[:, k, cols(t)], k == 0, k == 3)
                    last.then_inc(ready[t], 1)

            pe.wait_ge(o_lo_done, 4)
            pe.wait_ge(so_read, 2)
            pe.wait_ge(a_lo_done, 12)
            branches(0, 0)
            branches(1, 1)
            with pe.Fori(1, 4) as p:
                branches(2 * p, 0)
                branches(2 * p + 1, 1)

            def merged_there(t):
                pe.wait_ge(mg_lo_done, 3 * (N_AB - 1) + t + 1)

            with pe.Fori(0, 4) as p:
                for s in range(2):
                    project(U_O + 2 * p + s, USE_O + 2 * p + s, s, mg_hi, mg_lo, merged_there)

            pe.wait_ge(acc_done, 3 * N_O + 1)
            for b in range(BLK + 1):
                n = P if b < BLK else TS
                last = mm(psum[0:n, 6, b:b + 1], acc[:, b * P:b * P + n], ones[:, 0:1], start=True, stop=True)
            last.then_inc(ss_ready, 1)
            spread_rms(diag2, USE_R2, 1)

            def h2_there(t):
                pe.wait_ge(h_done, 17 + (8, 16, 17)[t])

            with pe.Fori(0, 4) as g:
                with pe.Fori(0, 4) as i:
                    for s in range(2):
                        n = 16 * g + 2 * i + s
                        project(U_F + n, USE_F + n, s, h2_hi, h2_lo, h2_there)

                def ff_there(t):
                    pe.wait_ge(ff_lo_done, 24 * g + 22 + t)

                with pe.Fori(0, 4) as i:
                    for s in range(2):
                        n = 16 * g + 8 + 2 * i + s
                        project(U_F + n, USE_F + n, s, ff_hi, ff_lo, ff_there)

            def turn_back(b, s, n):
                pe.wait_ge(y_staged, b + 1)
                wait(pe, y_done, b - 1)
                for j in range(DK):
                    last = nc.tensor.transpose(psum[0:n, 3 + 2 * s + j // 4, (j % 4) * P:(j % 4 + 1) * P], y_st[:, s, j, 0:n], ident[:, :])
                last.then_inc(yt_ready, 1)

            turn_back(0, 0, P)
            turn_back(1, 1, P)
            with pe.Fori(1, 4) as p:
                turn_back(2 * p, 0, P)
                turn_back(2 * p + 1, 1, P)
            turn_back(8, 0, TS)

        @block.scalar
        def _(act):
            copy = nc.scalar.copy
            fn = nc.scalar.activation

            act.dma_start(c_row[0:1, :], a["c_prompt"]).then_inc(c_in, 16)
            act.dma_start(c_row[1:NC, :], a["c_sample"]).then_inc(c_in, 16)
            for r0, n, name in ((0, NMOD, "b_ada"), (NMOD, DK, "norm1_g"), (NMOD + DK, DK, "norm2_g"), (NMOD + 2 * DK, NG, "pool_scale")):
                act.dma_start(v_row[r0:r0 + n, :], a[name].rearrange("o (j p) -> (o j) p", p=P)).then_inc(v_in, 16)
            act.dma_start(s_row[0:NB * PAD, :], a["state_pool"][0].rearrange("b r c -> (b r) c")).then_inc(s_in, 16)
            act.dma_start(sink_p[:, :], a["attn_sinks"][0].partition_broadcast(P)).then_inc(tab_in, 16)
            for g in range(G):
                act.dma_start(sink_s[g * TS:(g + 1) * TS, :], a["attn_sinks"][0].rearrange("(v g) -> g v", g=G)[g].partition_broadcast(TS), allow_slow_non_contiguous=True).then_inc(tab_in, 16)
            act.dma_start(inv_cnt[:, :, :].rearrange("p g c -> p (g c)"), a["inv_count"].partition_broadcast(P)).then_inc(tab_in, 16)

            act.wait_ge(c_in, 32)
            fn(c_sil[0:NC, :], c_row[0:NC, :], ACT.Sigmoid).then_inc(c_sig, 1)
            act.wait_ge(cvt_ready, 1)
            fn(cT[:, :, :], psum[:, 3, 0:P].rearrange("p (j c) -> p j c", c=16)[:, :, 0:NC], ACT.Copy).then_inc(cvt_read, 1)
            fn(vec[:, :], psum[:, 3, P:P + 68], ACT.Copy).then_inc(cvt_read, 1)
            act.wait_ge(st_ready, 1)
            fn(pool_s[:, :, :, 0:PAD], psum[:, 2, 0:480].rearrange("p (g b r) -> p g b r", g=NG, b=NB), ACT.Copy).then_inc(st_read, 1)
            for b in range(BLK + 1):
                n = P if b < BLK else TS
                act.wait_ge(xt_ready, b + 1)
                for hf in range(2):
                    last = fn(xT[:, 4 * hf:4 * hf + 4, b * P:b * P + n],
                              psum[:, 4 + 2 * (b % 2) + hf, :].rearrange("p (j c) -> p j c", c=P)[:, :, 0:n], ACT.Copy)
                last.then_inc(xt_read, 1)

            def ada_copy(n, s):
                act.wait_ge(row_ready, n + 1)
                wait(act, modt_ready, n - 1)
                fn(ada_row[0:NC, s, :], psum[0:NC, 3 + s, :], ACT.Copy).then_inc(row_read, 1)

            def split_hi(u, slot, loads, use):
                act.wait_ge(w_in[slot], loads)
                wait(act, ready[2], use)
                fn(w_hi[slot][:, :, :], w_raw[slot][:, :, :], ACT.Copy).then_inc(w_hi_done, 1)

            def rms_copies(use):
                for t in range(2):
                    act.wait_ge(ready[t], use + 1)
                    fn(R[:, 512 * t:512 * t + 512], psum[:, t, :], ACT.Copy).then_inc(free[t], 1)
                act.wait_ge(ready[2], use + 1)
                fn(R[:, TP:T], psum[:, 2, 0:TS], ACT.Copy).then_inc(free[2], 1)

            def norm_hi(m, dst, j, shift, tl, s):
                act.wait_ge(n_tmp, m + 1)
                fn(dst[:, bass.ds(j, 1), 512 * tl:512 * tl + 512].rearrange("p o t -> p (o t)"), (nrm_t if shift == 0 else nrm_t2)[:, s, :],
                   ACT.Identity, bias=mod[:, bass.ds(shift + j, 1), 0:1].rearrange("p o c -> p (o c)")).then_inc(n_hi, 1)

            ada_copy(0, 0)
            ada_copy(1, 1)
            rms_copies(USE_R1)
            for hf in range(2):
                if hf == 1:
                    ada_copy(2, 0)
                    split_hi(1, 1, loads_of(1), 0)
                    ada_copy(3, 1)
                else:
                    split_hi(0, 0, loads_of(0), 0)
                for tl in range(2):
                    act.wait_ge(mod_done, 2 * hf + 2)
                    with act.Fori(0, 2) as q:
                        for s in range(2):
                            norm_hi(8 * hf + 4 * tl + 2 * q + s, h_hi, 4 * hf + 2 * q + s, 0, tl, s)

            def z_tiles(u):
                for t in range(3):
                    act.wait_ge(ready[t], USE_Z + u + 1)
                    fn(z[:, u, cols(t)], psum[:, t, 0:TT], ACT.Copy).then_inc(free[t], 1)

            act.wait_ge(xt_saved, 16)
            for u in range(N_Z):
                if u >= 1:
                    split_hi(u + 1, (u + 1) % 2, loads_of(u + 1), use_of(u - 1) + 1)
                z_tiles(u)
                if u >= 2 and u % 2 == 0:
                    ada_copy(u + 2, 0)
                    ada_copy(u + 3, 1)

            def gate_copy(i, which, t):
                act.wait_ge(ready[t], USE_Z + U_G + 2 * i + which + 1)
                fn(g_out[:, which, cols(t)], psum[:, t, 0:TT], ACT.Copy).then_inc(free[t], 1)

            def attend(i, last_turn=False):
                first = isinstance(i, int) and i == 0
                k0 = P if first else 0
                kks = [1] if first else [0, 1]
                u = U_G + 2 * i

                def exps(kv):
                    act.wait_ge(nmax_done, 2 * i + kv + 1)
                    for c in range(G):
                        fn(pr[:, kv, c, k0:256], pr[:, kv, c, k0:256], ACT.Exp, bias=nmx[:, kv, c:c + 1], accum_out=rsum[:, kv, c:c + 1])
                    fn(esk[:, kv, :], dsk[:, kv, :], ACT.Exp).then_inc(exp_done, 1)

                def pt_halves(kv):
                    act.wait_ge(pt_ready, 2 * i + kv + 1)
                    wait(act, o_ready, 2 * i + kv)
                    fn(pt_hi[:, kks[0]:2, :], psum[:, 5 + kks[0]:7, :], ACT.Copy).then_inc(pt_hi_done, 1)

                def o_copy(kv):
                    act.wait_ge(o_ready, 2 * i + kv + 1)
                    h = slice(kv * HD, (kv + 1) * HD)
                    fn(z[h, 2:6, bass.ds(i * P, P)], psum[h, 7, :].rearrange("p (c t) -> p c t", c=G), ACT.Copy).then_inc(o_read, 1)

                split_hi(u + 1, 1, 16 * (U_G // 2) + 48 + 16 * i, USE_Z + u)
                act.wait_ge(vt_ready, i + 1)
                wait(act, o_ready, 2 * i)
                fn(v_hi[:, kks[0]:2, :], psum[:, 7, kks[0] * P:256].rearrange("p (k c) -> p k c", c=P), ACT.Copy).then_inc(v_hi_done, 1)
                exps(0)
                wait(act, g_saved, 16 * i)
                gate_copy(i, 0, 0)
                gate_copy(i, 0, 1)
                pt_halves(0)
                gate_copy(i, 0, 2)
                split_hi(u + 2, 0, loads_of(U_AB) if last_turn else 16 * (U_G // 2) + 64 + 16 * i, USE_Z + u + 1)
                exps(1)
                o_copy(0)
                gate_copy(i, 1, 0)
                gate_copy(i, 1, 1)
                pt_halves(1)
                gate_copy(i, 1, 2)
                o_copy(1)

            attend(0)
            with act.Fori(1, BLK - 1) as i:
                attend(i)
            attend(BLK - 1, last_turn=True)

            act.wait_ge(out_t_ready, 1)
            fn(kv_out[:, 0:256], psum[:, 5, 0:256], ACT.Copy).then_inc(out_t_read, 1)
            fn(kv_out[0:TS, 256:512], psum[0:TS, 5, 256:512], ACT.Copy).then_inc(out_t_read, 1)
            act.wait_ge(out_t_ready, 2)
            fn(poolp_out[0:PAD, :], psum[0:PAD, 6, :], ACT.Copy).then_inc(out_t_read, 1)
            act.wait_ge(out_t_ready, 3)
            fn(pools_out[0:NB * PAD, :], psum[0:NB * PAD, 7, :], ACT.Copy).then_inc(out_t_read, 1)
            act.wait_ge(kct_ready, 1)
            fn(ks_hi[:, 0:NB * WIN].rearrange("p (b k) -> p b k", b=2), psum[:, 3:5, :], ACT.Copy).then_inc(kct_hi, 1)
            fn(ks_hi[:, NB * WIN:SK], z[:, 0, TP:T], ACT.Copy).then_inc(kct_hi, 1)
            for kv in range(NKV):
                act.wait_ge(ss_nmax, kv + 1)
                fn(ps[:, kv, :], ps[:, kv, :], ACT.Exp, bias=nmx[:, kv, 0:1], accum_out=rsum[:, kv, 0:1])
                fn(esk[:, kv, 0:1], dsk[:, kv, 0:1], ACT.Exp).then_inc(ss_exp, 1)

            def d_half(g):
                act.wait_ge(ready[2], USE_POOL + g - 1 if g >= 2 else USE_SS + 2)
                fn(d_hi[g % 2][:, :], z[:, 6 + g, :], ACT.Copy).then_inc(d_hi_done, 1)

            act.wait_ge(pool_done, 1)
            act.wait_ge(vs_done, 1)
            act.wait_ge(ss_p, 1)
            for kv in range(NKV):
                act.wait_ge(sst_ready, kv + 1)
                wait(act, so_ready, kv)
                fn(pst_hi[:, 0:NB, :].rearrange("p (b k) c -> p b (k c)", b=2), psum[:, 5:7, :], ACT.Copy).then_inc(sst_hi, 1)
                fn(pst_hi[0:TS, NB, :], psum[0:TS, 4, 0:P], ACT.Copy).then_inc(sst_hi, 1)
                d_half(kv)
                act.wait_ge(so_ready, kv + 1)
                h = slice(kv * HD, (kv + 1) * HD)
                fn(z[h, 2:6, TP:T], psum[h, 7, 0:P].rearrange("p (c t) -> p c t", c=G), ACT.Copy).then_inc(so_read, 1)
            act.wait_ge(so_read, 2)
            for g in range(NG):
                fn(o_hi[:, g, :], z[:, 2 + g, :], ACT.Copy).then_inc(o_hi_done, 1)
                if g >= 2:
                    d_half(g)
                for t in range(3):
                    n = 3 * g + t
                    act.wait_ge(ready[t], USE_POOL + g + 1)
                    wait(act, a_lo_done, n - 1)
                    fn(a_t[:, n % 2, :], psum[:, t, 0:TT], ACT.Identity, scale=vec[:, NMOD + 2 * DK + g:NMOD + 2 * DK + g + 1])\
                        .then_inc(free[t], 1)
                    act.wait_ge(free[t], USE_POOL + g + 1)
                    fn(a_hi[:, g, cols(t)], a_t[:, n % 2, :], ACT.Copy).then_inc(a_hi_done, 1)

            def gate_halves(j, slot, loads, use):
                act.wait_ge(g_in_sem, 16 * j + 16)
                fn(g_in[:, :, :], g_in[:, :, :], ACT.Sigmoid).then_inc(sig_done, 1)
                split_hi(0, 1 - slot, loads, use)
                for t in range(3):
                    act.wait_ge(sum_done, 3 * j + t + 1)
                    fn(mg_hi[:, bass.ds(j, 1), cols(t)].rearrange("p o t -> p (o t)"), mt[:, 0, t, :], ACT.Copy).then_inc(mg_hi_done, 1)

            with act.Fori(0, 3) as p:
                gate_halves(2 * p, 0, LOADS_AB + 48 + 48 * p, USE_AB + 2 * p)
                gate_halves(2 * p + 1, 1, LOADS_AB + 96 + 48 * p, USE_AB + 1 + 2 * p)
            gate_halves(6, 0, loads_of(U_AB + 7), USE_AB + 6)
            gate_halves(7, 1, loads_of(U_O), USE_AB + 7)

            with act.Fori(0, 4) as p:
                for s in range(2):
                    j = 2 * p + s
                    split_hi(0, 1 - s, LOADS_O + 16 + 16 * (p + s), USE_O + j)
                    for t in range(3):
                        act.wait_ge(free[t], USE_O + j + 1)
                        if t == 2:
                            act.wait_ge(x1_done, j + 1)
                        act.wait_ge(acc_done, 3 * j + 1)
                        fn(sq_t[:, t, :], x1[:, bass.ds(j, 1), cols(t)].rearrange("p o t -> p (o t)"), ACT.Square).then_inc(sq_done, 1)

            rms_copies(USE_R2)
            for tl in range(2):
                with act.Fori(0, 4) as q:
                    for s in range(2):
                        norm_hi(16 + 8 * tl + 2 * q + s, h2_hi, 2 * q + s, 3 * DK, tl, s)
            act.wait_ge(h_done, 34)

            def ff_tiles(g, j, s):
                for t in range(3):
                    n = 24 * g + 3 * j + t
                    sl = (3 * s + t) % 2
                    act.wait_ge(ready[t], USE_F + 16 * g + j + 1)
                    wait(act, ff_sq, n - 1)
                    wait(act, ff_hi_done, n - 1)
                    fn(r_t[:, sl, :], psum[:, t, 0:TT], ACT.Relu).then_inc(free[t], 1)
                    act.wait_ge(free[t], USE_F + 16 * g + j + 1)
                    fn(ff_hi[:, bass.ds(j, 1), cols(t)].rearrange("p o t -> p (o t)"), r_t[:, sl, :], ACT.Square).then_inc(ff_hi_done, 1)

            def ff_group(g, last_group):
                def up(i):
                    for s in range(2):
                        split_hi(0, 1 - s, LOADS_O + 80 + 128 * g + 16 * i + 16 * s, USE_F + 16 * g + 2 * i + s)
                        ff_tiles(g, 2 * i + s, s)

                def down(i, skip=False):
                    for s in range(2):
                        if not (skip and s == 1):
                            split_hi(0, 1 - s, LOADS_O + 144 + 128 * g + 16 * i + 16 * s, USE_F + 8 + 16 * g + 2 * i + s)

                if isinstance(g, int) and g == 0:
                    up(0)
                    with act.Fori(1, 4) as i:
                        up(i)
                else:
                    with act.Fori(0, 4) as i:
                        up(i)
                with act.Fori(0, 3 if last_group else 4) as i:
                    down(i)
                if last_group:
                    down(3, skip=True)

            ff_group(0, False)
            with act.Fori(1, 3) as g:
                ff_group(g, False)
            ff_group(3, True)

            def y_squares(b, s, n):
                act.wait_ge(yt_ready, b + 1)
                wait(act, yss_done, b)
                fn(y_sq[0:n, :], psum[0:n, 3 + 2 * s:5 + 2 * s, :], ACT.Square, accum_out=fin_ss[0:n, s, :]).then_inc(yss_done, 1)

            y_squares(0, 0, P)
            y_squares(1, 1, P)
            with act.Fori(1, 4) as p:
                for s in range(2):
                    y_squares(2 * p + s, s, P)
            y_squares(8, 0, TS)

        @block.vector
        def _(dve):
            tt, ts_, stt = nc.vector.tensor_tensor, nc.vector.tensor_scalar, nc.vector.scalar_tensor_tensor
            ch = Chain(dve, dve_c)

            def f(t):
                return t.bitcast(F32)

            dve.wait_ge(c_sig, 1)
            tt(c_sil[0:NC, :], c_sil[0:NC, :], c_row[0:NC, :], ALU.mult).then_inc(c_silu, 1)
            for b in range(BLK + 1):
                n = P if b < BLK else TS
                dve.wait_ge(x_land[b % 4], 16 * (b // 4 + 1))
                wait(dve, x_sq, b)
                nc.vector.tensor_tensor_reduce(out=sq_x[0:n, :], in0=x_in[0:n, b % 4, :], in1=x_in[0:n, b % 4, :], scale=1.0, scalar=0.0,
                                               op0=ALU.mult, op1=ALU.add, accum_out=ssq[0:n, b:b + 1]).then_inc(x_sq, 1)

            def mean_squares(src8, src1):
                ts_(rms[:, 0:BLK], src8, 1.0 / D, EPS, ALU.mult, ALU.add)
                ts_(rms[0:TS, BLK:BLK + 1], src1, 1.0 / D, EPS, ALU.mult, ALU.add).then_inc(ms_done, 1)

            def diagonals(diag, n):
                dve.wait_ge(rms_done, 2 * n + 2)
                tt(diag[:, 0:BLK, :], ident[:, :].unsqueeze(1).to_broadcast([P, BLK, P]), ssq[:, 0:BLK].unsqueeze(2).to_broadcast([P, BLK, P]), ALU.mult)\
                    .then_inc(diag_done, 1)
                tt(diag[0:TS, BLK, 0:TS], ident[0:TS, 0:TS], ssq[0:TS, BLK:BLK + 1].to_broadcast([TS, TS]), ALU.mult).then_inc(diag_done, 1)

            dve.wait_ge(x_sq, 9)
            mean_squares(ssq[:, 0:BLK], ssq[0:TS, BLK:BLK + 1])
            dve.wait_ge(const_done, 4)
            diagonals(diag1, 0)

            def ada_add(n, s, col):
                dve.wait_ge(modt_ready, n + 1)
                tt(mod[:, 4 * col:4 * col + 4, :], psum[:, 5 + s, 0:64].rearrange("p (q c) -> p q c", c=16)[:, :, 0:NC],
                   vec[:, 4 * col:4 * col + 4].unsqueeze(2).to_broadcast([P, 4, NC]), ALU.add).then_inc(mod_done, 1)
                dve.wait_ge(mod_done, n + 1)

            def gains(gain, j0, n, scale_chunk, g_chunk):
                ch.step(stt(gain[:, j0:j0 + n, :], mod[:, scale_chunk + j0:scale_chunk + j0 + n, :], 1.0,
                            vec[:, g_chunk + j0:g_chunk + j0 + n].unsqueeze(2).to_broadcast([P, n, NC]), ALU.add, ALU.mult))

            def split_lo(u, slot):
                dve.wait_ge(w_hi_done, u + 1)
                tt(w_lo[slot][:, :, :], w_raw[slot][:, :, :], f(w_hi[slot][:, :, :]), ALU.subtract).then_inc(w_lo_done, 1)

            def norm_pair(m, src, gain, dst_hi, dst_lo, j, shift, tl, first):
                tile = slice(512 * tl, 512 * tl + 512)
                tmp = nrm_t if shift == 0 else nrm_t2
                for s in range(2):
                    if not first:
                        dve.wait_ge(n_hi, m + s - 1)
                        dve.wait_ge(h_done, m + s - 1 + (0 if shift == 0 else 1))
                    stt(tmp[:, s, :], src[:, bass.ds(j + s, 1), tile].rearrange("p o t -> p (o t)"),
                        gain[:, bass.ds(j + s, 1), 0:1].rearrange("p o c -> p (o c)"), R[:, tile], ALU.mult, ALU.mult).then_inc(n_tmp, 1)
                for s in range(2):
                    dve.wait_ge(n_hi, m + s + 1)
                    stt(dst_lo[:, bass.ds(j + s, 1), tile].rearrange("p o t -> p (o t)"), tmp[:, s, :],
                        mod[:, bass.ds(shift + j + s, 1), 0:1].rearrange("p o c -> p (o c)"),
                        f(dst_hi[:, bass.ds(j + s, 1), tile]).rearrange("p o t -> p (o t)"), ALU.add, ALU.subtract).then_inc(h_done, 1)

            def norm_samples(src, gain, dst_hi, dst_lo, shift):
                def v(t):
                    return t.rearrange("p j (b t) -> p j b t", t=NT)

                ch.step(tt(smp_t[:, :, :, :], v(src[:, :, TP:T]), gain[:, :, 1:NC].unsqueeze(3).to_broadcast([P, DK, NB, NT]), ALU.mult))
                flat = smp_t[:, :, :, :].rearrange("p j b t -> p j (b t)")
                ch.step(tt(flat, flat, R[:, TP:T].unsqueeze(1).to_broadcast([P, DK, TS]), ALU.mult))
                ch.step(tt(smp_t[:, :, :, :], smp_t[:, :, :, :], mod[:, shift:shift + DK, 1:NC].unsqueeze(3).to_broadcast([P, DK, NB, NT]), ALU.add))
                ch.step(nc.vector.tensor_copy(dst_hi[:, :, TP:T], flat))
                tt(dst_lo[:, :, TP:T], flat, f(dst_hi[:, :, TP:T]), ALU.subtract).then_inc(h_done, 1)

            ada_add(0, 0, ada_col[0])
            ada_add(1, 1, ada_col[1])
            gains(gain1, 0, 4, DK, NMOD)
            for t in range(3):
                dve.wait_ge(free[t], USE_R1 + 1)
            dve.wait_ge(xt_read, 9)
            split_lo(0, 0)
            for hf in range(2):
                if hf == 1:
                    split_lo(1, 1)
                    ada_add(2, 0, ada_col[2])
                    ada_add(3, 1, ada_col[3])
                    gains(gain1, 4, 4, DK, NMOD)
                for tl in range(2):
                    if hf == 0 and tl == 0:
                        norm_pair(0, xT, gain1, h_hi, h_lo, 0, 0, 0, True)
                        norm_pair(2, xT, gain1, h_hi, h_lo, 2, 0, 0, False)
                        continue
                    with dve.Fori(0, 2) as q:
                        norm_pair(8 * hf + 4 * tl + 2 * q, xT, gain1, h_hi, h_lo, 4 * hf + 2 * q, 0, tl, False)
            norm_samples(xT, gain1, h_hi, h_lo, 0)

            def pool_group(g):
                w = 2 << g
                u = z[:, 6 + g, :]
                for t in range(3):
                    dve.wait_ge(free[t], USE_Z + 6 + g + 1)
                us = u[:, TP:T].rearrange("p (b t) -> p b t", t=NT)
                ch.step(nc.vector.tensor_copy(pool_last[:, g, :], u[:, TP - PAD:TP]))
                ch.step(nc.vector.tensor_copy(pool_s[:, g, :, PAD:PAD + NT], us))
                cur, cur_s, lag = u[:, 0:TP], pool_s[:, g, :, :], 1
                bufs, bufs_s = [win_a, win_b], [win_sa, win_sb]
                while lag < w:
                    new, new_s = bufs[0][:, :], bufs_s[0][:, :, :]
                    bufs.reverse()
                    bufs_s.reverse()
                    tt(new[:, lag:TP], cur[:, lag:TP], cur[:, 0:TP - lag], ALU.add)
                    nc.vector.tensor_copy(new[:, 0:lag], cur[:, 0:lag])
                    ch.step(tt(new_s[:, :, 2 * lag - 1:], cur_s[:, :, 2 * lag - 1:], cur_s[:, :, lag - 1:PAD + NT - lag], ALU.add))
                    cur, cur_s, lag = new, new_s, 2 * lag
                ch.step(tt(cur[:, 0:16], cur[:, 0:16], inv_cnt[:, g, :], ALU.mult))
                tt(u[:, 0:16], cur[:, 0:16], u[:, 0:16], ALU.subtract)
                stt(u[:, 16:TP], cur[:, 16:TP], 1.0 / w, u[:, 16:TP], ALU.mult, ALU.subtract)
                last = stt(us, cur_s[:, :, PAD:PAD + NT], 1.0 / w, us, ALU.mult, ALU.subtract)
                ch.step(last)

            dve.wait_ge(tab_in, 16 * 6)
            for p in range(5):
                for s in range(2):
                    u = 2 * p + s
                    if u >= 1:
                        split_lo(u + 1, (u + 1) % 2)
                    if u >= 7:
                        pool_group(u - 7)
                if p:
                    ada_add(2 * p + 2, 0, 2 * p + 2)
                    ada_add(2 * p + 3, 1, 2 * p + 3)
            gains(gain2, 0, DK, 4 * DK, NMOD + DK)
            pool_group(3)

            nc.vector.tensor_copy(pool_tail[:, :, :].rearrange("p g (b r) -> p g b r", b=NB), pool_s[:, :, :, NT:PAD + NT]).then_inc(pool_done, 1)

            def attend(i):
                first = isinstance(i, int)
                k0 = P if first else 0
                kks = [1] if first else [0, 1]
                nk = 2 * P - k0
                u = U_G + 2 * i

                def soft_a(kv):
                    dve.wait_ge(s_ready, 2 * i + kv + 1)
                    wait(dve, pt_ready, 2 * i + kv - 1 if not first else 0)
                    s_all = psum[:, 3:5, :].rearrange("p b (c k) -> p (b c) k", k=256)
                    ch.step(stt(pr[:, kv, :, k0:256], s_all[:, :, k0:256], SCALE, bias_p[:, G * kv:G * kv + G, k0:256], ALU.mult, ALU.add))
                    ch.step(nc.vector.tensor_reduce(mx[:, kv, :], pr[:, kv, :, k0:256], AX.X, ALU.max))
                    ch.step(tt(mx[:, kv, :], mx[:, kv, :], sink_p[:, G * kv:G * kv + G], ALU.max))
                    ts_(nmx[:, kv, :], mx[:, kv, :], -1.0, None, ALU.mult)
                    tt(dsk[:, kv, :], sink_p[:, G * kv:G * kv + G], mx[:, kv, :], ALU.subtract).then_inc(nmax_done, 1)

                def soft_b(kv):
                    dve.wait_ge(exp_done, 2 * i + kv + 1)
                    ch.step(tt(rden[:, kv, :], rsum[:, kv, :], esk[:, kv, :], ALU.add))
                    ch.step(nc.vector.reciprocal(rden[:, kv, :], rden[:, kv, :]))
                    tt(pr[:, kv, :, k0:256], pr[:, kv, :, k0:256], rden[:, kv, :].unsqueeze(2).to_broadcast([P, G, nk]), ALU.mult).then_inc(p_done, 1)

                def pt_low(kv):
                    dve.wait_ge(pt_hi_done, 2 * i + kv + 1)
                    tt(pt_lo[:, kks[0]:2, :], psum[:, 5 + kks[0]:7, :], f(pt_hi[:, kks[0]:2, :]), ALU.subtract).then_inc(pt_lo_done, 1)

                dve.wait_ge(stage_done, i + 1)
                keys = slice(0, P) if first else bass.ds(i * P - P, 2 * P)
                tt(q_lo[:, :, :], z[:, 2:6, bass.ds(i * P, P)], f(q_hi[:, :, :]), ALU.subtract)
                tt(k_lo[:, k0:256], z[:, 0, keys], f(k_hi[:, k0:256]), ALU.subtract).then_inc(qk_lo_done, 1)
                split_lo(u + 1, 1)
                dve.wait_ge(v_hi_done, i + 1)
                tt(v_lo[:, kks[0]:2, :], psum[:, 7, kks[0] * P:256].rearrange("p (k c) -> p k c", c=P), f(v_hi[:, kks[0]:2, :]), ALU.subtract)\
                    .then_inc(v_lo_done, 1)
                soft_a(0)
                soft_b(0)
                pt_low(0)
                soft_a(1)
                split_lo(u + 2, 0)
                soft_b(1)
                pt_low(1)

            dve.wait_ge(bp_in, 16)
            attend(0)
            per = 2 * 5
            with dve.Fori(1, BLK) as i:
                ch.enter(i, 1, per)
                attend(i)
            ch.leave(BLK - 1, per)

            dve.wait_ge(kct_hi, 2)
            tt(ks_lo[:, 0:NB * WIN].rearrange("p (b k) -> p b k", b=2), psum[:, 3:5, :], f(ks_hi[:, 0:NB * WIN]).rearrange("p (b k) -> p b k", b=2), ALU.subtract)
            tt(ks_lo[:, NB * WIN:SK], z[:, 0, TP:T], f(ks_hi[:, NB * WIN:SK]), ALU.subtract).then_inc(ks_done, 1)
            dve.wait_ge(bs_in, 16)
            for kv in range(NKV):
                for t in range(3):
                    dve.wait_ge(ready[t], USE_SS + kv + 1)
                    ins = stt(ps[:, kv, cols(t)], psum[:, t, 0:TT], SCALE, bias_s[:, kv, cols(t)], ALU.mult, ALU.add)
                    ins.then_inc(free[t], 1)
                for t in range(3):
                    dve.wait_ge(free[t], USE_SS + kv + 1)
                ch.step(nc.vector.tensor_reduce(mx[:, kv, 0:1], ps[:, kv, :], AX.X, ALU.max))
                ch.step(tt(mx[:, kv, 0:1], mx[:, kv, 0:1], sink_s[:, kv:kv + 1], ALU.max))
                ts_(nmx[:, kv, 0:1], mx[:, kv, 0:1], -1.0, None, ALU.mult)
                tt(dsk[:, kv, 0:1], sink_s[:, kv:kv + 1], mx[:, kv, 0:1], ALU.subtract).then_inc(ss_nmax, 1)
            for kv in range(NKV):
                dve.wait_ge(ss_exp, kv + 1)
                ch.step(tt(rden[:, kv, 0:1], rsum[:, kv, 0:1], esk[:, kv, 0:1], ALU.add))
                ch.step(nc.vector.reciprocal(rden[:, kv, 0:1], rden[:, kv, 0:1]))
                ts_(ps[:, kv, :], ps[:, kv, :], rden[:, kv, 0:1], None, ALU.mult).then_inc(ss_p, 1)

            def d_low(g):
                dve.wait_ge(d_hi_done, g + 1)
                tt(d_lo[g % 2][:, :], z[:, 6 + g, :], f(d_hi[g % 2][:, :]), ALU.subtract).then_inc(d_lo_done, 1)

            for kv in range(NKV):
                dve.wait_ge(sst_hi, 2 * kv + 2)
                tt(pst_lo[:, 0:NB, :].rearrange("p (b k) c -> p b (k c)", b=2), psum[:, 5:7, :], f(pst_hi[:, 0:NB, :]).rearrange("p (b k) c -> p b (k c)", b=2), ALU.subtract)\
                    .then_inc(sst_lo, 1)
                tt(pst_lo[0:TS, NB, :], psum[0:TS, 4, 0:P], f(pst_hi[0:TS, NB, :]), ALU.subtract).then_inc(sst_lo, 1)
                d_low(kv)
            for g in range(NG):
                dve.wait_ge(o_hi_done, g + 1)
                tt(o_lo[:, g, :], z[:, 2 + g, :], f(o_hi[:, g, :]), ALU.subtract).then_inc(o_lo_done, 1)
                if g >= 2:
                    d_low(g)
                for t in range(3):
                    n = 3 * g + t
                    dve.wait_ge(a_hi_done, n + 1)
                    tt(a_lo[:, g, cols(t)], a_t[:, n % 2, :], f(a_hi[:, g, cols(t)]), ALU.subtract).then_inc(a_lo_done, 1)

            def gated(j, u, slot):
                def lo(t):
                    dve.wait_ge(mg_hi_done, 3 * j + t + 1)
                    tt(mg_lo[:, bass.ds(j, 1), cols(t)].rearrange("p o t -> p (o t)"), mt[:, 0, t, :],
                       f(mg_hi[:, bass.ds(j, 1), cols(t)]).rearrange("p o t -> p (o t)"), ALU.subtract).then_inc(mg_lo_done, 1)

                split_lo(u + 1, 1 - slot)
                dve.wait_ge(sig_done, j + 1)
                for t in range(3):
                    dve.wait_ge(readyB[t], j + 1)
                    wait(dve, mg_lo_done, 3 * j + t - 2)
                    tt(mt[:, 1, t, :], psum[:, 3 + t, 0:TT], g_in[:, 1, cols(t)], ALU.mult).then_inc(freeB[t], 1)
                    dve.wait_ge(ready[t], USE_AB + j + 1)
                    tt(mt[:, 0, t, :], psum[:, t, 0:TT], g_in[:, 0, cols(t)], ALU.mult).then_inc(free[t], 1)
                    if t:
                        lo(t - 1)
                lo(2)

            gated(0, U_AB, 0)
            gated(1, U_AB + 1, 1)
            with dve.Fori(1, 4) as p:
                for s in range(2):
                    gated(2 * p + s, U_AB + 2 * p + s, s)

            def add_gated(j, t, use, gate_chunk, res, count):
                x = x1[:, bass.ds(j, 1), :].rearrange("p o t -> p (o t)")
                gt = mod[:, bass.ds(gate_chunk + j, 1), :].rearrange("p o c -> p (o c)")
                dve.wait_ge(ready[t], use + 1)
                n = TT if t < 2 else TP - 2 * TT
                c0 = t * TT
                if t == 2:
                    ch.step(tt(smp_t[:, 0, :, :], psum[:, 2, n:TT].rearrange("p (b t) -> p b t", t=NT), gt[:, 1:NC].unsqueeze(2).to_broadcast([P, NB, NT]), ALU.mult))
                ins = stt(x[:, c0:c0 + n], psum[:, t, 0:n], gt[:, 0:1], res[:, c0:c0 + n], ALU.mult, ALU.add)
                ins.then_inc(free[t], 1)
                if t == 2:
                    tt(x[:, TP:T], smp_t[:, 0, :, :].rearrange("p b t -> p (b t)"), res[:, TP:T], ALU.add).then_inc(x1_done, 1)
                    dve.wait_ge(x1_done, count)

            per = 2
            with dve.Fori(0, 4) as p:
                ch.enter(p, 0, per)
                for s in range(2):
                    j = 2 * p + s
                    split_lo(U_O + j + 1, 1 - s)
                    dve.wait_ge(xr_in[s], 16 * p + 16)
                    for t in range(3):
                        add_gated(j, t, USE_O + j, 2 * DK, x_res[:, s, :], j + 1)
            ch.leave(4, per)

            dve.wait_ge(ss_ready, 1)
            mean_squares(psum[:, 6, 0:BLK], psum[0:TS, 6, BLK:BLK + 1])
            diagonals(diag2, 1)
            for t in range(3):
                dve.wait_ge(free[t], USE_R2 + 1)
            for tl in range(2):
                with dve.Fori(0, 4) as q:
                    norm_pair(16 + 8 * tl + 2 * q, x1, gain2, h2_hi, h2_lo, 2 * q, 3 * DK, tl, False)
            norm_samples(x1, gain2, h2_hi, h2_lo, 3 * DK)

            def ff_group(g, last_group):
                def up(i):
                    for s in range(2):
                        j = 2 * i + s
                        split_lo(U_F + 16 * g + j + 1, 1 - s)
                        for t in range(3):
                            n = 24 * g + 3 * j + t
                            sl = (3 * s + t) % 2
                            dve.wait_ge(free[t], USE_F + 16 * g + j + 1)
                            wait(dve, ff_lo_done, n - 1)
                            tt(f_t[:, sl, :], r_t[:, sl, :], r_t[:, sl, :], ALU.mult).then_inc(ff_sq, 1)
                            dve.wait_ge(ff_sq, n + 1)
                            dve.wait_ge(ff_hi_done, n + 1)
                            tt(ff_lo[:, bass.ds(j, 1), cols(t)].rearrange("p o t -> p (o t)"), f_t[:, sl, :],
                               f(ff_hi[:, bass.ds(j, 1), cols(t)]).rearrange("p o t -> p (o t)"), ALU.subtract).then_inc(ff_lo_done, 1)

                if isinstance(g, int) and g == 0:
                    up(0)
                    with dve.Fori(1, 4) as i:
                        up(i)
                else:
                    with dve.Fori(0, 4) as i:
                        up(i)

                def down(i, skip=False):
                    for s in range(2):
                        j = 2 * i + s
                        if not (skip and s == 1):
                            split_lo(U_F + 16 * g + 8 + j + 1, 1 - s)
                        for t in range(3):
                            add_gated(j, t, USE_F + 16 * g + 8 + j, 5 * DK, x1[:, bass.ds(j, 1), :].rearrange("p o t -> p (o t)"), N_O + 8 * g + j + 1)

                per = 2
                turns = 3 if last_group else 4
                with dve.Fori(0, turns) as i:
                    ch.enter(i, 0, per)
                    down(i)
                ch.leave(turns, per)
                if last_group:
                    down(3, skip=True)

            ff_group(0, False)
            outer = ch.base + ch.k
            with dve.Fori(1, 3) as g:
                ch.base, ch.k = outer + (g - 1) * 8, 0
                ff_group(g, False)
            ch.base, ch.k = outer + 2 * 8, 0
            ff_group(3, True)

            def stage(b, s, n):
                wait(dve, yt_ready, b - 1)
                nc.vector.tensor_copy(y_st[:, s, :, 0:n], x1[:, :, bass.ds(b * P, n)]).then_inc(y_staged, 1)

            for t in range(3):
                dve.wait_ge(free[t], USE_F + 64)
            dve.wait_ge(x1_done, N_O + 32)
            dve.wait_ge(fg_in, 16)
            stage(0, 0, P)

            def out_block(b, s, n, turn):
                dve.wait_ge(yss_done, b + 1)
                ts_(fin_r[0:n, s, :], fin_ss[0:n, s, :], 1.0 / D, EPS, ALU.mult, ALU.add).then_inc(yms_done, 1)
                dve.wait_ge(yr_done, b + 1)
                wait(dve, y_sent[s], 16 * turn)
                stt(y_out[0:n, s, :], psum[0:n, 3 + 2 * s:5 + 2 * s, :].rearrange("p b c -> p (b c)"), fin_ss[0:n, s, :], fin_g[0:n, :], ALU.mult, ALU.mult)\
                    .then_inc(y_done, 1)

            stage(1, 1, P)
            out_block(0, 0, P, 0)
            stage(2, 0, P)
            out_block(1, 1, P, 0)
            with dve.Fori(1, 3) as p:
                stage(2 * p + 1, 1, P)
                out_block(2 * p, 0, P, p)
                stage(2 * p + 2, 0, P)
                out_block(2 * p + 1, 1, P, p)
            stage(7, 1, P)
            out_block(6, 0, P, 3)
            stage(8, 0, TS)
            out_block(7, 1, P, 3)
            out_block(8, 0, TS, 4)

        @block.gpsimd
        def _(pool):
            tt = nc.gpsimd.tensor_tensor
            cp = nc.gpsimd.tensor_copy
            ch = Chain(pool, pool_c)

            def f(t):
                return t.bitcast(F32)

            ch.step(nc.gpsimd.memset(ident[:, :], 0.0))
            nc.gpsimd.affine_select(out=ident[:, :], in_=ident[:, :], compare_op=ALU.not_equal, fill=1.0, base=0, pattern=[[-1, P]],
                                    channel_multiplier=1).then_inc(const_done, 1)
            nc.gpsimd.memset(ada_row[:, :, :], 0.0).then_inc(const_done, 1)
            nc.gpsimd.memset(ones[:, :], 1.0).then_inc(const_done, 1)
            nc.gpsimd.memset(half[:, :], -0.5).then_inc(const_done, 1)
            pool.wait_ge(const_done, 4)

            def powers(n):
                pool.wait_ge(ms_done, n + 1)
                tt(ssq[:, 0:BLK], rms[:, 0:BLK], half[:, 0:BLK], ALU.pow).then_inc(rms_done, 1)
                tt(ssq[0:TS, BLK:BLK + 1], rms[0:TS, BLK:BLK + 1], half[0:TS, 0:1], ALU.pow).then_inc(rms_done, 1)

            powers(0)

            def stage(i):
                first = isinstance(i, int)
                k0 = P if first else 0
                keys = slice(0, P) if first else bass.ds(i * P - P, 2 * P)
                blk = bass.ds(i * P, P)
                wait(pool, s_ready, 2 * i)
                wait(pool, vt_ready, i)
                cp(q_hi[:, :, :], z[:, 2:6, blk])
                cp(k_hi[:, k0:256], z[:, 0, keys])
                cp(v_st[:, k0 // P:2, :].rearrange("p k c -> p (k c)"), z[:, 1, keys]).then_inc(stage_done, 1)

            for t in range(3):
                pool.wait_ge(free[t], USE_Z + 6)
            pool.wait_ge(mod_done, 12)
            stage(0)
            with pool.Fori(1, BLK) as i:
                stage(i)

            pool.wait_ge(g_saved, 16 * BLK)
            pool.wait_ge(o_ready, 2 * BLK)
            ch.step(cp(qs_hi[:, :, :], z[:, 2:6, TP:T]))
            tt(qs_lo[:, :, :], z[:, 2:6, TP:T], f(qs_hi[:, :, :]), ALU.subtract).then_inc(qs_done, 1)
            pool.wait_ge(kvc_in, 32)
            ch.step(cp(vs_hi[:, 0:NB, :], vc[:, :, :]))
            tt(vs_lo[:, 0:NB, :], vc[:, :, :], f(vs_hi[:, 0:NB, :]), ALU.subtract)
            pool.wait_ge(out_t_read, 2)
            ch.step(cp(vs_hi[0:TS, NB, :], kv_out[0:TS, 3 * P:4 * P]))
            tt(vs_lo[0:TS, NB, :], kv_out[0:TS, 3 * P:4 * P], f(vs_hi[0:TS, NB, :]), ALU.subtract).then_inc(vs_done, 1)
            pool.wait_ge(ks_done, 1)
            pool.wait_ge(wp_in, 16)
            ch.step(cp(wp_hi[:, :, :], wp_raw[:, :, :]))
            tt(wp_lo[:, :, :], wp_raw[:, :, :], f(wp_hi[:, :, :]), ALU.subtract).then_inc(wp_done, 1)

            with pool.Fori(0, N_AB) as j:
                for t in range(3):
                    pool.wait_ge(free[t], USE_AB + j + 1)
                    tt(mt[:, 0, t, :], mt[:, 0, t, :], mt[:, 1, t, :], ALU.add).then_inc(sum_done, 1)

            pool.wait_ge(sent, 16 * 22)
            nc.gpsimd.memset(acc[:, :], 0.0).then_inc(acc_done, 1)
            with pool.Fori(0, N_O) as j:
                for t in range(3):
                    pool.wait_ge(sq_done, 3 * j + t + 1)
                    pool.wait_ge(acc_done, 3 * j + t + 1)
                    tt(acc[:, cols(t)], acc[:, cols(t)], sq_t[:, t, :], ALU.add).then_inc(acc_done, 1)
            powers(1)

            def y_power(b, s, n):
                pool.wait_ge(yms_done, b + 1)
                tt(fin_ss[0:n, s, :], fin_r[0:n, s, :], half[0:n, 0:1], ALU.pow).then_inc(yr_done, 1)

            with pool.Fori(0, 4) as p:
                y_power(2 * p, 0, P)
                y_power(2 * p + 1, 1, P)
            y_power(8, 0, TS)


_INS = ["x_prompt", "x_sample", "cache_k", "cache_v", "state_pool", "c_prompt", "c_sample", "w_ada", "b_ada", "norm1_g", "w_in", "w_pool",
        "pool_scale", "attn_sinks", "w_a", "w_b", "w_out", "norm2_g", "w_up", "w_down", "final_g"]
_OUTS = [(1, TP, D), (NB, NT, D), (1, 1, WIN, NKV, HD), (1, 1, WIN, NKV, HD), (1, 1, PAD, PW),
         (1, NB, WIN, NKV, HD), (1, NB, WIN, NKV, HD), (1, NB, PAD, PW)]


def _shape_tables(np):
    slopes = 2.0 ** (-8.0 * (np.arange(NH) + 1) / NH)
    dist = np.arange(P)[:, None] + P - np.arange(2 * P)[None, :]
    seen = (dist >= 0) & (dist < WIN)
    prompt = np.where(seen[:, None, :], -slopes[None, :, None] * dist[:, None, :], -1e30).astype(np.float32)
    row = np.arange(P)
    g, seq, tok = row // TS, (row % TS) // NT, row % NT
    key = np.arange(SK)
    new = key >= NB * WIN
    key_seq = np.where(new, (key - NB * WIN) // NT, key // WIN)
    key_pos = np.where(new, (key - NB * WIN) % NT, key % WIN - WIN)
    dist = tok[:, None] - key_pos[None, :]
    seen = (dist >= 0) & (dist < WIN) & (seq[:, None] == key_seq[None, :])
    sample = np.stack([np.where(seen, -slopes[v * G + g][:, None] * dist, -1e30) for v in range(NKV)], axis=1).astype(np.float32)
    pos = np.arange(16)
    inv = np.stack([1.0 / np.minimum(2 << n, pos + 1) for n in range(NG)]).astype(np.float32).reshape(-1)
    return {"alibi_prompt": prompt, "alibi_sample": sample, "inv_count": inv}


def kernel(**inputs):
    import numpy as _np
    import concourse.bacc as _bacc
    from concourse import mybir as _mybir
    from concourse.bass_utils import run_bass_kernel_spmd as _run

    nc = _bacc.Bacc("TRN2", target_bir_lowering=False, num_devices=1)
    arrays, args = {}, {}
    given = {name: _np.ascontiguousarray(inputs[name]) for name in _INS}
    given.update(_shape_tables(_np))
    for name, x in given.items():
        arrays[f"in_{name}_dram"] = x
        args[name] = nc.dram_tensor(f"in_{name}_dram", x.shape, _mybir.dt.from_np(x.dtype), kind="ExternalInput").ap()
    outs = [nc.dram_tensor(f"out_{i}_dram", shape, _mybir.dt.float32, kind="ExternalOutput").ap() for i, shape in enumerate(_OUTS)]
    hybrid_decoder_step(nc, args, outs)
    r = _run(nc, [arrays], core_ids=[0])
    return tuple(r.results[0][f"out_{i}_dram"] for i in range(len(_OUTS)))
```

```python
import concourse.bass as bass
from concourse import mybir
from contextlib import ExitStack

F32 = mybir.dt.float32
F32R = mybir.dt.float32r
ALU = mybir.AluOpType
ACT = mybir.ActivationFunctionType
AX = mybir.AxisListType

P = 128
D = 1024
DK = D // P
TP = 1024
NB, NT = 8, 4
TS = NB * NT
T = TP + TS
TW = (384, 384, 288)
TC = (0, 384, 768)
TM = max(TW)
BLK = TP // P
HD, NH, NKV = 64, 8, 2
G = NH // NKV
WIN = 128
DFF = 4 * D
PW = D // 2
NG = 4
PAD = 15
NMOD = 6 * DK
NC = 1 + NB
SK = NB * WIN + TS
EPS = 1e-6
SCALE = HD ** -0.5

U_Z, N_Z = 0, 10
U_G, N_G = 10, 16
U_AB, N_AB = 26, 8
U_O, N_O = 34, 8
U_F = 42
N_U = U_F + 64
USE_R1 = 0
USE_Z = 1
USE_SS = 27
USE_POOL = 29
USE_AB = 33
USE_O = 41
USE_R2 = 49
USE_F = 49


LOADS_AB = 16 * (U_AB // 2) + 32
LOADS_O = LOADS_AB + 48 * (N_AB // 2)


def use_of(u):
    if u < U_AB:
        return USE_Z + u
    return USE_AB + (u - U_AB) if u < U_F else USE_F + (u - U_F)


def loads_of(u):
    if u < U_AB:
        return 16 * (u // 2 + 1) + 16 * min(u // 2, 2)
    if u < U_O:
        return LOADS_AB + 48 * ((u - U_AB) // 2 + 1)
    return LOADS_O + 16 * ((u - U_O) // 2 + 1)


def wait(eng, sem, value):
    if isinstance(value, int) and value <= 0:
        return
    eng.wait_ge(sem, value)


class Chain:

    def __init__(self, eng, sem):
        self.eng, self.sem, self.base, self.k = eng, sem, 0, 0

    def step(self, ins):
        self.k += 1
        ins.then_inc(self.sem, 1)
        self.eng.wait_ge(self.sem, self.base + self.k)

    def enter(self, i, first, per):
        self.start = self.base + self.k
        self.base = self.start + (i - first) * per
        self.k = 0

    def leave(self, turns, per):
        assert self.k == per, (self.k, per)
        self.base, self.k = self.start + turns * per, 0


def hybrid_decoder_step(nc, a, outs):
    y_p, y_s, nk_p, nv_p, npool_p, nk_s, nv_s, npool_s = outs
    ctx = ExitStack()
    with ctx:
        def sem(name):
            return ctx.enter_context(nc.semaphore(name))

        arena_bytes = 212800
        arena = ctx.enter_context(nc.sbuf_tensor("arena", [P, arena_bytes // 4], F32))
        arena_at = 16512

        def at(name, offset, shape, dt=F32):
            size = 4
            for s in shape[1:]:
                size *= s
            assert offset % 32 == 0 and offset + size <= arena_bytes, (name, offset, size)
            return nc.alloc_sbuf_tensor_at(name, shape, dt, offset=arena_at + offset)

        ROW = 4 * T
        RA, RB, RC, RD = 0, 8 * ROW, 16 * ROW, 32 * ROW
        RE = RC + 10 * ROW
        RW = RD + 8 * ROW
        RM = RW + 6 * 4096

        w_raw = [at(f"w_raw{s}", RW + 4096 * s, [P, DK, P]) for s in range(2)]
        w_hi = [at(f"w_hi{s}", RW + 8192 + 4096 * s, [P, DK, P], F32R) for s in range(2)]
        w_lo = [at(f"w_lo{s}", RW + 16384 + 4096 * s, [P, DK, P], F32R) for s in range(2)]
        m = RM

        def small(name, shape, dt=F32):
            nonlocal m
            size = 4
            for s in shape[1:]:
                size *= s
            t = at(name, m, shape, dt)
            m += (size + 31) // 32 * 32
            return t

        mod = small("mod", [P, NMOD, NC])
        vec = small("vec", [P, 68])
        ident = small("ident", [P, P])
        ones = small("ones", [P, P])
        gain1 = small("gain1", [P, DK, NC])
        gain2 = small("gain2", [P, DK, NC])
        cT = small("cT", [P, DK, NC])
        pool_s = small("pool_s", [P, NG, NB, PAD + NT])
        inv_cnt = small("inv_cnt", [P, NG, 16])
        sink_p = small("sink_p", [P, NH])
        sink_s = small("sink_s", [P, NKV])
        ssq = small("ssq", [P, 9])
        rms = small("rms", [P, 9])
        half = small("half", [P, 9])
        mx = small("mx", [P, 2, G])
        nmx = small("nmx", [P, 2, G])
        dsk = small("dsk", [P, 2, G])
        esk = small("esk", [P, 2, G])
        rsum = small("rsum", [P, 2, G])
        rden = small("rden", [P, 2, G])
        fin_ss = small("fin_ss", [P, 3, 1])
        fin_r = small("fin_r", [P, 3, 1])
        v_st = small("v_st", [P, 2, P])
        smp_t = small("smp_t", [P, DK, NB, NT])
        pool_last = small("pool_last", [P, NG, PAD])
        m_pool = m
        assert m + 8448 + 1216 <= arena_bytes
        R = small("R", [P, T])
        acc = small("acc", [P, T])
        win_a = at("win_a", m_pool, [P, TP])
        win_b = at("win_b", m_pool + 4096, [P, TP])
        win_sa = at("win_sa", m_pool + 8192, [P, NB, PAD + NT])
        win_sb = at("win_sb", m_pool + 8192 + 608, [P, NB, PAD + NT])
        kv_out = at("kv_out", m_pool, [P, 512])
        poolp_out = at("poolp_out", m_pool + 2048, [P, 512])
        pool_tail = at("pool_tail", m_pool + 6144, [P, NG, NB * PAD])
        pools_out = at("pools_out", m_pool + 4096, [P, 512])

        h_hi = at("h_hi", RA, [P, DK, T], F32R)
        h_lo = at("h_lo", RB, [P, DK, T], F32R)
        o_hi = at("o_hi", RA, [P, 4, T], F32R)
        o_lo = at("o_lo", RA + 4 * ROW, [P, 4, T], F32R)
        a_hi = at("a_hi", RB, [P, 4, T], F32R)
        a_lo = at("a_lo", RB + 4 * ROW, [P, 4, T], F32R)
        x1 = at("x1", RA, [P, DK, T])
        ff_hi = at("ff_hi", RB, [P, DK, T], F32R)
        c_row = at("c_row", RB, [P, D])
        c_sil = at("c_sil", RB + 4096, [P, D])
        v_row = at("v_row", RB + 8192, [P, P])
        s_row = at("s_row", RB + 8704, [P, PW])
        diag1 = at("diag1", RB + 12288, [P, 9, P])
        sq_x = at("sq_x", RB + 17408, [P, D])
        xT = at("xT", RC, [P, DK, T])
        z = at("z", RC, [P, 10, T])
        mg_hi = at("mg_hi", RC, [P, DK, T], F32R)
        mg_lo = at("mg_lo", RC + 8 * ROW, [P, DK, T], F32R)
        h2_hi = at("h2_hi", RC, [P, DK, T], F32R)
        h2_lo = at("h2_lo", RC + 8 * ROW, [P, DK, T], F32R)
        x_in = at("x_in", RE, [P, 4, D])
        ada_row = at("ada_row", RE + 16384, [P, 2, 512])
        nrm_t = at("nrm_t", RE + 20480, [P, 2, 512])
        bias_p = at("bias_p", RE, [P, NH, 2 * P])
        pr = at("pr", RE + 8192, [P, 2, G, 2 * P])
        pt_hi = at("pt_hi", RE + 16384, [P, 2, G * P], F32R)
        pt_lo = at("pt_lo", RE + 20480, [P, 2, G * P], F32R)
        ks_hi = at("ks_hi", RE, [P, SK], F32R)
        ks_lo = at("ks_lo", RE + 4224, [P, SK], F32R)
        ps = at("ps", RE + 8448, [P, 2, SK])
        pst_hi = at("pst_hi", RE + 16896, [P, 9, P], F32R)
        ada_w = at("ada_w", RD, [P, 2, DK, 512])
        q_hi = at("q_hi", RD, [P, 4, P], F32R)
        q_lo = at("q_lo", RD + 2048, [P, 4, P], F32R)
        k_hi = at("k_hi", RD + 4096, [P, 2 * P], F32R)
        k_lo = at("k_lo", RD + 5120, [P, 2 * P], F32R)
        v_hi = at("v_hi", RD + 6144, [P, 2, P], F32R)
        v_lo = at("v_lo", RD + 7168, [P, 2, P], F32R)
        g_out = at("g_out", RD + 8192, [P, 2, T])
        kc = at("kc", RD + 16640, [P, NB, P])
        vc = at("vc", RD + 20736, [P, NB, P])
        bias_s = at("bias_s", RD + 24832, [P, NKV, SK])
        vs_hi = at("vs_hi", RD, [P, 9, P], F32R)
        vs_lo = at("vs_lo", RD + 4608, [P, 9, P], F32R)
        pst_lo = at("pst_lo", RD + 9216, [P, 9, P], F32R)
        qs_hi = at("qs_hi", RD + 13824, [P, 4, TS], F32R)
        qs_lo = at("qs_lo", RD + 14336, [P, 4, TS], F32R)
        d_hi = [at(f"d_hi{s}", RD + ROW * (4 + 2 * s), [P, T], F32R) for s in range(2)]
        d_lo = [at(f"d_lo{s}", RD + ROW * (5 + 2 * s), [P, T], F32R) for s in range(2)]
        wp_raw = at("wp_raw", RE + 21504, [P, NG, P])
        wp_hi = at("wp_hi", RC, [P, NG, P], F32R)
        wp_lo = at("wp_lo", RC + 2048, [P, NG, P], F32R)
        a_t = at("a_t", RC + ROW, [P, 2, TM])
        g_in = at("g_in", RD, [P, 2, 2, T])
        mt = at("mt", RD + 4 * ROW, [P, 2, 3, TM])
        x_res = at("x_res", RD, [P, 2, T])
        sq_t = at("sq_t", RD + 2 * ROW, [P, 3, TM])
        nrm_t2 = at("nrm_t2", RD + 4 * ROW, [P, 2, TM])
        diag2 = at("diag2", RD + 5 * ROW, [P, 9, P])
        ff_lo = at("ff_lo", RD, [P, DK, T], F32R)
        r_t = at("r_t", m_pool, [P, 2, TM])
        f_t = at("f_t", m_pool + 8 * TM, [P, 2, TM])
        wd_hi = [w_hi[0]] + [at(f"wd_hi{j}", RC + 8192 * j, [P, DK, P], F32R) for j in range(1, DK)]
        wd_lo = [w_lo[0]] + [at(f"wd_lo{j}", RC + 8192 * j + 4096, [P, DK, P], F32R) for j in range(1, DK)]
        fin_g = at("fin_g", RW + 12288, [P, D])
        y_sq = at("y_sq", RW + 20480, [P, D])
        y_out = [at("y_out0", m_pool, [P, D]), at("y_out1", m_pool + 4096, [P, D]), at("y_out2", RC, [P, D])]

        psum = ctx.enter_context(nc.psum_tensor("psum", [P, 8, 512], F32))

        gates_d = nc.dram_tensor("gates_scratch", [8, P, 2, T], F32, kind="Internal").ap()
        xT_d = nc.dram_tensor("xT_scratch", [P, DK, T], F32, kind="Internal").ap()

        w_in = [sem("w_in0"), sem("w_in1")]
        w_hi_done, w_lo_done = sem("w_hi_done"), sem("w_lo_done")
        ready = [sem(f"ready{t}") for t in range(3)]
        free = [sem(f"free{t}") for t in range(3)]
        readyB = [sem(f"readyB{t}") for t in range(3)]
        freeB = [sem(f"freeB{t}") for t in range(3)]
        c_in, v_in, s_in, tab_in = sem("c_in"), sem("v_in"), sem("s_in"), sem("tab_in")
        x_land = [sem(f"x_land{s}") for s in range(4)]
        x_sq, xt_ready, xt_read, xt_saved = sem("x_sq"), sem("xt_ready"), sem("xt_read"), sem("xt_saved")
        const_done, c_sig, c_silu = sem("const_done"), sem("c_sig"), sem("c_silu")
        cvt_ready, cvt_read, st_ready, st_read = sem("cvt_ready"), sem("cvt_read"), sem("st_ready"), sem("st_read")
        ada_in = [sem("ada_in0"), sem("ada_in1")]
        row_ready, row_read, modt_ready, mod_done = sem("row_ready"), sem("row_read"), sem("modt_ready"), sem("mod_done")
        ms_done, rms_done, diag_done = sem("ms_done"), sem("rms_done"), sem("diag_done")
        n_tmp, n_hi, h_done = sem("n_tmp"), sem("n_hi"), sem("h_done")
        pool_done = sem("pool_done")
        stage_done, vt_ready, v_hi_done, v_lo_done = sem("stage_done"), sem("vt_ready"), sem("v_hi_done"), sem("v_lo_done")
        s_ready, nmax_done, exp_done, p_done = sem("s_ready"), sem("nmax_done"), sem("exp_done"), sem("p_done")
        pt_ready, pt_hi_done, pt_lo_done, o_ready, o_read = sem("pt_ready"), sem("pt_hi_done"), sem("pt_lo_done"), sem("o_ready"), sem("o_read")
        g_saved, kvc_in, bs_in, bp_in = sem("g_saved"), sem("kvc_in"), sem("bs_in"), sem("bp_in")
        out_t_ready, out_t_read, kct_ready, kct_hi, ks_done, vs_done, qs_done = (
            sem("out_t_ready"), sem("out_t_read"), sem("kct_ready"), sem("kct_hi"), sem("ks_done"), sem("vs_done"), sem("qs_done"))
        sst_ready, sst_hi, sst_lo, so_ready, so_read = sem("sst_ready"), sem("sst_hi"), sem("sst_lo"), sem("so_ready"), sem("so_read")
        ss_nmax, ss_exp, ss_p = sem("ss_nmax"), sem("ss_exp"), sem("ss_p")
        d_hi_done, d_lo_done, o_hi_done, o_lo_done = sem("d_hi_done"), sem("d_lo_done"), sem("o_hi_done"), sem("o_lo_done")
        a_hi_done, a_lo_done = sem("a_hi_done"), sem("a_lo_done")
        g_in_sem, sig_done, sum_done, mg_hi_done, mg_lo_done = (
            [sem("g_in0"), sem("g_in1")], sem("sig_done"), sem("sum_done"), sem("mg_hi_done"), sem("mg_lo_done"))
        xr_in, x1_done, sq_done, acc_done = [sem("xr_in0"), sem("xr_in1")], sem("x1_done"), sem("sq_done"), sem("acc_done")
        ff_sq, ff_hi_done, ff_lo_done = sem("ff_sq"), sem("ff_hi_done"), sem("ff_lo_done")
        x_last, yt_ready, yss_done, yms_done, yr_done, y_done, fg_in = (
            sem("x_last"), sem("yt_ready"), sem("yss_done"), sem("yms_done"), sem("yr_done"), sem("y_done"), sem("fg_in"))
        y_sent = [sem("y_sent0"), sem("y_sent1"), sem("y_sent2")]
        n2_tmp, n2_hi, h2_done, h2s_done, ss_ready, diag2_done = (
            sem("n2_tmp"), sem("n2_hi"), sem("h2_done"), sem("h2s_done"), sem("ss_ready"), sem("diag2_done"))
        qk_lo_done = sem("qk_lo_done")
        wp_in, wp_done = sem("wp_in"), sem("wp_done")
        sent = sem("sent")
        act_c, dve_c, pool_c = sem("act_chain"), sem("dve_chain"), sem("pool_chain")

        def cols(t):
            return slice(TC[t], TC[t] + TW[t])

        ada_col = [0, 2, 1, 3] + list(range(4, 12))

        block = ctx.enter_context(nc.Block())

        @block.sync
        def _(sp):
            def load_x(b):
                rows = P if b < BLK else TS
                if b >= 4:
                    sp.wait_ge(x_sq, b - 3)
                    sp.wait_ge(xt_ready, b - 3)
                src = a["x_prompt"][0, b * P:(b + 1) * P, :] if b < BLK else a["x_sample"].rearrange("b t d -> (b t) d")
                sp.dma_start(x_in[0:rows, b % 4, :], src).then_inc(x_land[b % 4], 16)

            def load_ada(n, col):
                wait(sp, row_ready, n - 1)
                sp.dma_start(ada_w[:, n % 2, :, :], a["w_ada"][0, :, col].rearrange("(k p) c -> p k c", p=P))\
                    .then_inc(ada_in[n % 2], 16)

            def load_w(slot, src, free_count):
                wait(sp, w_lo_done, free_count)
                sp.dma_start(w_raw[slot][:, :, :], src.rearrange("(k p) c -> p k c", p=P)).then_inc(w_in[slot], 16)

            w_in_d, z_col = a["w_in"][0], [PW + NH * HD, PW + NH * HD + NKV * HD] + [None] * 4 + [g * P for g in range(NG)]

            def load_z(u):
                if z_col[u] is not None:
                    load_w(u % 2, w_in_d[:, z_col[u]:z_col[u] + P], u - 1)
                    return
                wait(sp, w_lo_done, u - 1)
                c = PW + (u - 2) * HD
                src = w_in_d[:, PW:PW + NH * HD].rearrange("(k p) (v g c) -> p k v g c", p=P, v=NKV, g=G)[:, :, :, u - 2, :]
                sp.dma_start(w_raw[u % 2][:, :, 0:HD], src[:, :, 0, :]).then_inc(w_in[u % 2], 16)
                sp.dma_start(w_raw[u % 2][:, :, HD:P], src[:, :, 1, :]).then_inc(w_in[u % 2], 16)

            for b in range(4):
                load_x(b)
            load_ada(0, slice(ada_col[0] * 512, ada_col[0] * 512 + 512))
            for b in range(4, 9):
                load_x(b)
            load_ada(1, slice(ada_col[1] * 512, ada_col[1] * 512 + 512))
            load_z(0)
            load_z(1)
            for n in (2, 3):
                load_ada(n, slice(ada_col[n] * 512, ada_col[n] * 512 + 512))
            sp.wait_ge(xt_read, 9)
            sp.dma_start(xT_d, xT[:, :, :]).then_inc(xt_saved, 16)
            for p in range(4):
                load_z(2 * p + 2)
                load_ada(4 + 2 * p, slice((4 + 2 * p) * 512, (5 + 2 * p) * 512))
                load_z(2 * p + 3)
                load_ada(5 + 2 * p, slice((5 + 2 * p) * 512, (6 + 2 * p) * 512))
            z0 = 2 * PW + 2 * NKV * HD

            def gate_loads(i, g_from):
                load_w(0, w_in_d[:, bass.ds(z0 + i * P, P)], g_from)
                load_w(1, w_in_d[:, bass.ds(z0 + D + i * P, P)], g_from + 1)

            gate_loads(0, U_G - 1)
            sp.wait_ge(mod_done, 12)
            sp.dma_start(bias_p[:, :, :], a["alibi_prompt"]).then_inc(bp_in, 16)
            sp.dma_start(kc[:, :, :], a["cache_k"][0].rearrange("b w h d -> w b (h d)")).then_inc(kvc_in, 16)
            sp.dma_start(vc[:, :, :], a["cache_v"][0].rearrange("b w h d -> w b (h d)")).then_inc(kvc_in, 16)
            sp.dma_start(bias_s[:, :, :], a["alibi_sample"]).then_inc(bs_in, 16)
            for cache, new in ((a["cache_k"], nk_s), (a["cache_v"], nv_s)):
                sp.dma_start(new[0, :, 0:WIN - NT].rearrange("b w h d -> b w (h d)"),
                             cache[0, :, NT:WIN].rearrange("b w h d -> b w (h d)")).then_inc(sent, 16)
            def gate_store(i):
                for t in range(3):
                    sp.wait_ge(free[t], USE_Z + U_G + 2 * i + 2)
                sp.dma_start(gates_d[bass.ds(i, 1)].rearrange("o p g t -> (o p) g t"), g_out[:, :, :]).then_inc(g_saved, 16)

            with sp.Fori(1, BLK) as i:
                gate_loads(i, U_G - 1 + 2 * i)
                gate_store(i - 1)

            def load_ab(j, slot, free_count):
                wait(sp, w_lo_done, free_count)
                c = bass.ds(j * P, P)
                sp.dma_start(w_raw[slot][:, 0:4, :], a["w_a"][0][:, c].rearrange("(k p) c -> p k c", p=P)).then_inc(w_in[slot], 16)
                w_b = a["w_b"][0][:, c].rearrange("(v g p) c -> v p g c", v=NKV, g=G)
                for v in range(NKV):
                    sp.dma_start(w_raw[slot][v * HD:(v + 1) * HD, 4:8, :], w_b[v]).then_inc(w_in[slot], 16)

            load_ab(0, 0, U_AB - 1)
            load_ab(1, 1, U_AB)
            gate_store(BLK - 1)
            sp.wait_ge(o_ready, 2 * BLK)
            sp.dma_start(wp_raw[:, :, :], a["w_pool"][0].rearrange("g c d -> c g d")).then_inc(wp_in, 16)
            sp.wait_ge(out_t_read, 4)
            sp.dma_start(nk_p[0, 0].rearrange("w h d -> w (h d)"), kv_out[:, 0:P]).then_inc(sent, 16)
            sp.dma_start(nv_p[0, 0].rearrange("w h d -> w (h d)"), kv_out[:, P:2 * P]).then_inc(sent, 16)
            for new, c in ((nk_s, 2 * P), (nv_s, 3 * P)):
                for b in range(NB):
                    sp.dma_start(new[0, b, WIN - NT:WIN].rearrange("w h d -> w (h d)"), kv_out[b * NT:(b + 1) * NT, c:c + P]).then_inc(sent, 16)
            sp.dma_start(npool_p[0, 0], poolp_out[0:PAD, :]).then_inc(sent, 16)
            sp.dma_start(npool_s[0].rearrange("b r c -> (b r) c"), pools_out[0:NB * PAD, :]).then_inc(sent, 16)

            def gates_back(j, slot):
                wait(sp, free[2], USE_AB + j - 1)
                sp.dma_start(g_in[:, slot, :, :], gates_d[bass.ds(j, 1)].rearrange("o p g t -> (o p) g t")).then_inc(g_in_sem[slot], 16)

            sp.wait_ge(g_saved, 16 * BLK)
            sp.wait_ge(so_ready, 2)
            gates_back(0, 0)
            gates_back(1, 1)
            w_out_d = a["w_out"][0]
            with sp.Fori(1, 4) as p:
                load_ab(2 * p, 0, U_AB - 1 + 2 * p)
                gates_back(2 * p, 0)
                load_ab(2 * p + 1, 1, U_AB + 2 * p)
                gates_back(2 * p + 1, 1)
            load_w(0, w_out_d[:, 0:P], U_O - 1)
            load_w(1, w_out_d[:, P:2 * P], U_O)
            sp.wait_ge(xt_saved, 16)

            def load_res(j, slot):
                wait(sp, x1_done, j - 1)
                sp.dma_start(x_res[:, slot, :], xT_d[:, bass.ds(j, 1), :].rearrange("p o t -> p (o t)")).then_inc(xr_in[slot], 16)

            sp.wait_ge(mg_lo_done, 3 * N_AB)
            load_res(0, 0)
            load_res(1, 1)
            with sp.Fori(1, 4) as p:
                load_w(0, w_out_d[:, bass.ds(2 * p * P, P)], U_O - 1 + 2 * p)
                load_res(2 * p, 0)
                load_w(1, w_out_d[:, bass.ds((2 * p + 1) * P, P)], U_O + 2 * p)
                load_res(2 * p + 1, 1)
            w_up_d, w_down_d = a["w_up"][0], a["w_down"][0]
            with sp.Fori(0, 4) as g:
                with sp.Fori(0, 4) as i:
                    for s in range(2):
                        load_w(s, w_up_d[:, bass.ds((8 * g + 2 * i + s) * P, P)], U_F - 1 + 16 * g + 2 * i + s)
                with sp.Fori(0, 4) as i:
                    for s in range(2):
                        load_w(s, w_down_d[bass.ds(g * D, D), bass.ds((2 * i + s) * P, P)], U_F + 7 + 16 * g + 2 * i + s)
            for t in range(3):
                sp.wait_ge(ready[t], USE_F + 56)
            sp.dma_start(fin_g[:, :], a["final_g"].partition_broadcast(P)).then_inc(fg_in, 16)
            for b in range(BLK + 1):
                sp.wait_ge(y_done, b + 1)
                dst = y_p[0, b * P:(b + 1) * P, :] if b < BLK else y_s.rearrange("b t d -> (b t) d")
                sp.dma_start(dst, y_out[b % 3][0:P if b < BLK else TS, :]).then_inc(y_sent[b % 3], 16)
            for s in range(3):
                sp.wait_ge(y_sent[s], 16 * 3)
            sp.wait_ge(sent, 16 * (2 + 2 + 16 + 2))

        @block.tensor
        def _(pe):
            mm = nc.tensor.matmul

            def mm3(out, whi, wlo, rhi, rlo, first, last):
                mm(out, whi, rhi, start=first, stop=False)
                mm(out, whi, rlo, start=False, stop=False)
                return mm(out, wlo, rhi, start=False, stop=last)

            def project(u, use, slot, rhi, rlo, before=None):
                pe.wait_ge(w_lo_done, u + 1)
                for t in range(3):
                    if before:
                        before(t)
                    pe.wait_ge(free[t], use)
                    for k in range(DK):
                        last = mm3(psum[:, t, 0:TW[t]], w_hi[slot][:, k, :], w_lo[slot][:, k, :], rhi[:, k, cols(t)], rlo[:, k, cols(t)], k == 0, k == DK - 1)
                    last.then_inc(ready[t], 1)

            pe.wait_ge(const_done, 4)
            pe.wait_ge(c_silu, 1)
            for j in range(DK):
                nc.tensor.transpose(psum[:, 3, 16 * j:16 * j + NC], c_sil[0:NC, j * P:(j + 1) * P], ident[0:NC, 0:NC])
            pe.wait_ge(v_in, 64)
            nc.tensor.transpose(psum[:, 3, P:P + 68], v_row[0:68, :], ident[0:68, 0:68]).then_inc(cvt_ready, 1)
            pe.wait_ge(s_in, 16)
            for g in range(NG):
                last = nc.tensor.transpose(psum[:, 2, 120 * g:120 * g + 120], s_row[0:120, g * P:(g + 1) * P], ident[0:120, 0:120])
            last.then_inc(st_ready, 1)
            for b in range(BLK + 1):
                rows = P if b < BLK else TS
                pe.wait_ge(x_land[b % 4], 16 * (b // 4 + 1))
                wait(pe, xt_read, b - 1)
                for j in range(DK):
                    bank = 4 + 2 * (b % 2) + j // 4
                    last = nc.tensor.transpose(psum[:, bank, (j % 4) * P:(j % 4) * P + rows], x_in[0:rows, b % 4, j * P:(j + 1) * P], ident[0:rows, 0:rows])
                last.then_inc(xt_ready, 1)

            def ada_rows(n, s):
                pe.wait_ge(ada_in[s], 8 * (n - s) + 16)
                wait(pe, row_read, n - 1)
                for k in range(DK):
                    last = mm(psum[0:NC, 3 + s, :], cT[:, k, :], ada_w[:, s, k, :], start=(k == 0), stop=(k == DK - 1))
                last.then_inc(row_ready, 1)

            def ada_turn(n, s):
                pe.wait_ge(row_read, n + 1)
                wait(pe, mod_done, n - 1)
                for q in range(4):
                    last = mm(psum[:, 5 + s, 16 * q:16 * q + NC], ada_row[:, s, q * P:(q + 1) * P], ident[:, 0:NC], start=True, stop=True)
                last.then_inc(modt_ready, 1)

            pe.wait_ge(cvt_read, 2)
            ada_rows(0, 0)
            pe.wait_ge(st_read, 1)

            def spread_rms(diag, use):
                pe.wait_ge(diag_done, 2)
                for t in range(3):
                    wait(pe, free[t], use)
                for t in range(2):
                    mm(psum[:, t, :], ones[:, :], diag[:, 4 * t:4 * t + 4, :], start=True, stop=True).then_inc(ready[t], 1)
                mm(psum[:, 2, 0:TS], ones[0:TS, :], diag[0:TS, 8, 0:TS], start=True, stop=True).then_inc(ready[2], 1)

            pe.wait_ge(xt_read, 9)
            ada_rows(1, 1)
            spread_rms(diag1, USE_R1)
            ada_turn(0, 0)
            ada_rows(2, 0)
            ada_turn(1, 1)
            ada_rows(3, 1)
            ada_turn(2, 0)
            ada_turn(3, 1)

            def h_there(t):
                pe.wait_ge(h_done, (12, 16, 17)[t])

            project(0, USE_Z, 0, h_hi, h_lo, h_there)
            project(1, USE_Z + 1, 1, h_hi, h_lo)
            with pe.Fori(1, 5) as p:
                project(2 * p, USE_Z + 2 * p, 0, h_hi, h_lo)
                ada_rows(2 * p + 2, 0)
                ada_rows(2 * p + 3, 1)
                project(2 * p + 1, USE_Z + 2 * p + 1, 1, h_hi, h_lo)
                ada_turn(2 * p + 2, 0)
                ada_turn(2 * p + 3, 1)

            def gate_tile(use, slot, t):
                pe.wait_ge(free[t], use)
                for k in range(DK):
                    last = mm3(psum[:, t, 0:TW[t]], w_hi[slot][:, k, :], w_lo[slot][:, k, :], h_hi[:, k, cols(t)], h_lo[:, k, cols(t)], k == 0, k == DK - 1)
                last.then_inc(ready[t], 1)

            def attend(i):
                first = isinstance(i, int)
                kks = [1] if first else [0, 1]
                k0 = P if first else 0
                u = U_G + 2 * i

                def scores(kv):
                    wait(pe, nmax_done, 2 * i + kv)
                    h = slice(kv * HD, (kv + 1) * HD)
                    for c in range(G):
                        last = mm3(psum[:, 3 + c // 2, (c % 2) * 256 + k0:(c % 2) * 256 + 256], q_hi[h, c, :], q_lo[h, c, :],
                                   k_hi[h, k0:256], k_lo[h, k0:256], True, True)
                    last.then_inc(s_ready, 1)

                def turn_probs(kv):
                    pe.wait_ge(p_done, 2 * i + kv + 1)
                    wait(pe, pt_lo_done, 2 * i + kv)
                    for kk in kks:
                        for c in range(G):
                            last = nc.tensor.transpose(psum[:, 5 + kk, c * P:(c + 1) * P], pr[:, kv, c, kk * P:(kk + 1) * P], ident[:, :])
                    last.then_inc(pt_ready, 1)

                def weigh(kv):
                    pe.wait_ge(pt_lo_done, 2 * i + kv + 1)
                    pe.wait_ge(v_lo_done, i + 1)
                    wait(pe, o_read, 2 * i + kv)
                    for kk in kks:
                        last = mm3(psum[:, 7, :], v_hi[:, kk, :], v_lo[:, kk, :], pt_hi[:, kk, :], pt_lo[:, kk, :], kk == kks[0], kk == 1)
                    last.then_inc(o_ready, 1)

                pe.wait_ge(stage_done, i + 1)
                wait(pe, o_read, 2 * i)
                for kk in kks:
                    last = nc.tensor.transpose(psum[:, 7, kk * P:(kk + 1) * P], v_st[:, kk, :], ident[:, :])
                last.then_inc(vt_ready, 1)
                pe.wait_ge(qk_lo_done, i + 1)
                scores(0)
                pe.wait_ge(w_lo_done, u + 1)
                gate_tile(USE_Z + u, 0, 0)
                gate_tile(USE_Z + u, 0, 1)
                turn_probs(0)
                scores(1)
                gate_tile(USE_Z + u, 0, 2)
                weigh(0)
                pe.wait_ge(w_lo_done, u + 2)
                gate_tile(USE_Z + u + 1, 1, 0)
                gate_tile(USE_Z + u + 1, 1, 1)
                turn_probs(1)
                gate_tile(USE_Z + u + 1, 1, 2)
                weigh(1)

            attend(0)
            with pe.Fori(1, BLK) as i:
                attend(i)

            pe.wait_ge(o_read, 2 * BLK)
            pe.wait_ge(pt_lo_done, 2 * BLK)
            for q, (chunk, c0, n) in enumerate(((0, TP - P, P), (1, TP - P, P), (0, TP, TS), (1, TP, TS))):
                last = nc.tensor.transpose(psum[0:n, 5, q * P:(q + 1) * P], z[:, chunk, c0:c0 + n], ident[:, :])
            last.then_inc(out_t_ready, 1)
            pe.wait_ge(pool_done, 1)
            for g in range(NG):
                last = nc.tensor.transpose(psum[0:PAD, 6, g * P:(g + 1) * P], pool_last[:, g, :], ident[:, :])
            last.then_inc(out_t_ready, 1)
            for g in range(NG):
                last = nc.tensor.transpose(psum[0:NB * PAD, 7, g * P:(g + 1) * P], pool_tail[:, g, :], ident[:, :])
            last.then_inc(out_t_ready, 1)
            pe.wait_ge(kvc_in, 32)
            for b in range(NB):
                last = nc.tensor.transpose(psum[:, 3 + b // 4, (b % 4) * P:(b % 4 + 1) * P], kc[:, b, :], ident[:, :])
            last.then_inc(kct_ready, 1)
            pe.wait_ge(ks_done, 1)
            pe.wait_ge(qs_done, 1)
            for kv in range(NKV):
                h = slice(kv * HD, (kv + 1) * HD)
                for t in range(3):
                    pe.wait_ge(free[t], USE_SS + kv)
                    mm3(psum[:, t, 0:TW[t]], qs_hi[h, :, :], qs_lo[h, :, :], ks_hi[h, cols(t)], ks_lo[h, cols(t)], True, True)\
                        .then_inc(ready[t], 1)
            pe.wait_ge(vs_done, 1)
            pe.wait_ge(out_t_read, 4)
            for kv in range(NKV):
                pe.wait_ge(ss_p, kv + 1)
                wait(pe, sst_lo, 2 * kv)
                for cc in range(9):
                    n = P if cc < NB else TS
                    bank = (5, 6, 4)[cc // 4]
                    last = nc.tensor.transpose(psum[0:n, bank, (cc % 4) * P:(cc % 4 + 1) * P], ps[:, kv, cc * P:cc * P + n], ident[:, :])
                last.then_inc(sst_ready, 1)
                pe.wait_ge(sst_lo, 2 * kv + 2)
                wait(pe, so_read, kv)
                for cc in range(9):
                    n = P if cc < NB else TS
                    last = mm3(psum[:, 7, 0:P], vs_hi[0:n, cc, :], vs_lo[0:n, cc, :], pst_hi[0:n, cc, :], pst_lo[0:n, cc, :], cc == 0, cc == 8)
                last.then_inc(so_ready, 1)

            pe.wait_ge(wp_done, 1)
            for g in range(NG):
                pe.wait_ge(d_lo_done, g + 1)
                for t in range(3):
                    pe.wait_ge(free[t], USE_POOL + g)
                    mm3(psum[:, t, 0:TW[t]], wp_hi[:, g, :], wp_lo[:, g, :], d_hi[g % 2][:, cols(t)], d_lo[g % 2][:, cols(t)], True, True)\
                        .then_inc(ready[t], 1)

            def branches(j, slot):
                pe.wait_ge(w_lo_done, U_AB + j + 1)
                for t in range(3):
                    wait(pe, freeB[t], j)
                    for k in range(4):
                        last = mm3(psum[:, 3 + t, 0:TW[t]], w_hi[slot][:, 4 + k, :], w_lo[slot][:, 4 + k, :], o_hi[:, k, cols(t)], o_lo[:, k, cols(t)], k == 0, k == 3)
                    last.then_inc(readyB[t], 1)
                    pe.wait_ge(free[t], USE_AB + j)
                    for k in range(4):
                        last = mm3(psum[:, t, 0:TW[t]], w_hi[slot][:, k, :], w_lo[slot][:, k, :], a_hi[:, k, cols(t)], a_lo[:, k, cols(t)], k == 0, k == 3)
                    last.then_inc(ready[t], 1)

            pe.wait_ge(o_lo_done, 4)
            pe.wait_ge(so_read, 2)
            pe.wait_ge(a_lo_done, 12)
            branches(0, 0)
            branches(1, 1)
            with pe.Fori(1, 4) as p:
                branches(2 * p, 0)
                branches(2 * p + 1, 1)

            def merged_there(t):
                pe.wait_ge(mg_lo_done, 3 * (N_AB - 1) + t + 1)

            with pe.Fori(0, 4) as p:
                for s in range(2):
                    project(U_O + 2 * p + s, USE_O + 2 * p + s, s, mg_hi, mg_lo, merged_there)

            for b in range(BLK + 1):
                n, t = (P if b < BLK else TS), b // 3
                c0 = b * P - TC[t]
                pe.wait_ge(acc_done, 3 * (N_O - 2) + t + 2)
                mm(psum[0:n, 6, b:b + 1], acc[:, b * P:b * P + n], ones[:, 0:1], start=True, stop=False)
                pe.wait_ge(sq_done, 3 * (N_O - 1) + t + 1)
                last = mm(psum[0:n, 6, b:b + 1], sq_t[:, t, c0:c0 + n], ones[:, 0:1], start=False, stop=True)
            last.then_inc(ss_ready, 1)
            for t in range(3):
                pe.wait_ge(diag2_done, t + 1)
                pe.wait_ge(free[t], USE_R2)
                n = min(3, BLK - 3 * t)
                last = mm(psum[:, t, 0:n * P], ones[:, :], diag2[:, 3 * t:3 * t + n, :], start=True, stop=True)
                if t == 2:
                    last = mm(psum[:, t, n * P:TW[t]], ones[0:TS, :], diag2[0:TS, BLK, 0:TS], start=True, stop=True)
                last.then_inc(ready[t], 1)

            pe.wait_ge(w_lo_done, U_F + 2)
            for t in range(3):
                pe.wait_ge(free[t], USE_R2 + 1)
                pe.wait_ge(freeB[t], N_AB)
                if t == 2:
                    pe.wait_ge(h2s_done, 1)
                for k in range(DK):
                    if k % 2 == 0:
                        pe.wait_ge(h2_done, 8 * t + k + 2)
                    for s in range(2):
                        last = mm3(psum[:, 3 * s + t, 0:TW[t]], w_hi[s][:, k, :], w_lo[s][:, k, :], h2_hi[:, k, cols(t)], h2_lo[:, k, cols(t)], k == 0, k == DK - 1)
                        if k == DK - 1:
                            last.then_inc((ready, readyB)[s][t], 1)

            def up(g, i):
                for s in range(2):
                    n = 16 * g + 2 * i + s
                    project(U_F + n, USE_F + n, s, h2_hi, h2_lo)

            def down(g):
                def ff_there(t):
                    pe.wait_ge(ff_lo_done, 24 * g + 22 + t)

                with pe.Fori(0, 4) as i:
                    for s in range(2):
                        n = 16 * g + 8 + 2 * i + s
                        project(U_F + n, USE_F + n, s, ff_hi, ff_lo, ff_there)

            with pe.Fori(1, 4) as i:
                up(0, i)
            down(0)
            with pe.Fori(1, 3) as g:
                with pe.Fori(0, 4) as i:
                    up(g, i)
                down(g)
            with pe.Fori(0, 4) as i:
                up(3, i)

            def turn_back(b, bank):
                n = P if b < BLK else TS
                wait(pe, y_done, b - 1)
                for j in range(DK):
                    last = nc.tensor.transpose(psum[0:n, bank + j // 4, (j % 4) * P:(j % 4 + 1) * P], x1[:, j, b * P:b * P + n], ident[:, :])
                last.then_inc(yt_ready, 1)

            for t in range(3):
                pe.wait_ge(ff_lo_done, 24 * 3 + 22 + t)
                for j in range(DK):
                    n = DK * t + j
                    pe.wait_ge(w_lo_done, U_F + 56 + j + 1)
                    pe.wait_ge(free[n % 3], USE_F + 56 + n // 3)
                    for k in range(DK):
                        last = mm3(psum[:, n % 3, 0:TW[t]], wd_hi[j][:, k, :], wd_lo[j][:, k, :], ff_hi[:, k, cols(t)], ff_lo[:, k, cols(t)], k == 0, k == DK - 1)
                    last.then_inc(ready[n % 3], 1)
                    if t and j in (0, 2, 4):
                        b = 3 * (t - 1) + j // 2
                        if j == 0:
                            for m in range(DK * t - 3, DK * t):
                                pe.wait_ge(free[m % 3], USE_F + 56 + m // 3 + 1)
                        turn_back(b, 3 + 2 * (b % 2))
            pe.wait_ge(x_last, DK)
            turn_back(6, 3)
            turn_back(7, 5)
            for t in range(3):
                pe.wait_ge(free[t], USE_F + 64)
            turn_back(8, 0)

        @block.scalar
        def _(act):
            copy = nc.scalar.copy
            fn = nc.scalar.activation

            act.dma_start(c_row[0:1, :], a["c_prompt"]).then_inc(c_in, 16)
            act.dma_start(c_row[1:NC, :], a["c_sample"]).then_inc(c_in, 16)
            for r0, n, name in ((0, NMOD, "b_ada"), (NMOD, DK, "norm1_g"), (NMOD + DK, DK, "norm2_g"), (NMOD + 2 * DK, NG, "pool_scale")):
                act.dma_start(v_row[r0:r0 + n, :], a[name].rearrange("o (j p) -> (o j) p", p=P)).then_inc(v_in, 16)
            act.dma_start(s_row[0:NB * PAD, :], a["state_pool"][0].rearrange("b r c -> (b r) c")).then_inc(s_in, 16)
            act.dma_start(sink_p[:, :], a["attn_sinks"][0].partition_broadcast(P)).then_inc(tab_in, 16)
            for g in range(G):
                act.dma_start(sink_s[g * TS:(g + 1) * TS, :], a["attn_sinks"][0].rearrange("(v g) -> g v", g=G)[g].partition_broadcast(TS), allow_slow_non_contiguous=True).then_inc(tab_in, 16)
            act.dma_start(inv_cnt[:, :, :].rearrange("p g c -> p (g c)"), a["inv_count"].partition_broadcast(P)).then_inc(tab_in, 16)

            act.wait_ge(c_in, 32)
            fn(c_sil[0:NC, :], c_row[0:NC, :], ACT.Sigmoid).then_inc(c_sig, 1)
            act.wait_ge(cvt_ready, 1)
            fn(cT[:, :, :], psum[:, 3, 0:P].rearrange("p (j c) -> p j c", c=16)[:, :, 0:NC], ACT.Copy).then_inc(cvt_read, 1)
            fn(vec[:, :], psum[:, 3, P:P + 68], ACT.Copy).then_inc(cvt_read, 1)
            act.wait_ge(st_ready, 1)
            fn(pool_s[:, :, :, 0:PAD], psum[:, 2, 0:480].rearrange("p (g b r) -> p g b r", g=NG, b=NB), ACT.Copy).then_inc(st_read, 1)
            for b in range(BLK + 1):
                n = P if b < BLK else TS
                act.wait_ge(xt_ready, b + 1)
                for hf in range(2):
                    last = fn(xT[:, 4 * hf:4 * hf + 4, b * P:b * P + n],
                              psum[:, 4 + 2 * (b % 2) + hf, :].rearrange("p (j c) -> p j c", c=P)[:, :, 0:n], ACT.Copy)
                last.then_inc(xt_read, 1)

            def ada_copy(n, s):
                act.wait_ge(row_ready, n + 1)
                wait(act, modt_ready, n - 1)
                fn(ada_row[0:NC, s, :], psum[0:NC, 3 + s, :], ACT.Copy).then_inc(row_read, 1)

            def split_hi(u, slot, loads, use):
                act.wait_ge(w_in[slot], loads)
                wait(act, ready[2], use)
                fn(w_hi[slot][:, :, :], w_raw[slot][:, :, :], ACT.Copy).then_inc(w_hi_done, 1)

            def rms_copies(use):
                for t in range(2):
                    act.wait_ge(ready[t], use + 1)
                    fn(R[:, 512 * t:512 * t + 512], psum[:, t, :], ACT.Copy).then_inc(free[t], 1)
                act.wait_ge(ready[2], use + 1)
                fn(R[:, TP:T], psum[:, 2, 0:TS], ACT.Copy).then_inc(free[2], 1)

            def norm_hi(m, dst, j, shift, tl, s):
                act.wait_ge(n_tmp, m + 1)
                fn(dst[:, bass.ds(j, 1), 512 * tl:512 * tl + 512].rearrange("p o t -> p (o t)"), (nrm_t if shift == 0 else nrm_t2)[:, s, :],
                   ACT.Identity, bias=mod[:, bass.ds(shift + j, 1), 0:1].rearrange("p o c -> p (o c)")).then_inc(n_hi, 1)

            ada_copy(0, 0)
            ada_copy(1, 1)
            rms_copies(USE_R1)
            for hf in range(2):
                if hf == 1:
                    ada_copy(2, 0)
                    split_hi(1, 1, loads_of(1), 0)
                    ada_copy(3, 1)
                else:
                    split_hi(0, 0, loads_of(0), 0)
                for tl in range(2):
                    act.wait_ge(mod_done, 2 * hf + 2)
                    with act.Fori(0, 2) as q:
                        for s in range(2):
                            norm_hi(8 * hf + 4 * tl + 2 * q + s, h_hi, 4 * hf + 2 * q + s, 0, tl, s)

            def z_tiles(u):
                for t in range(3):
                    act.wait_ge(ready[t], USE_Z + u + 1)
                    fn(z[:, u, cols(t)], psum[:, t, 0:TW[t]], ACT.Copy).then_inc(free[t], 1)

            act.wait_ge(xt_saved, 16)
            for u in range(N_Z):
                if u >= 1:
                    split_hi(u + 1, (u + 1) % 2, loads_of(u + 1), use_of(u - 1) + 1)
                z_tiles(u)
                if u >= 2 and u % 2 == 0:
                    ada_copy(u + 2, 0)
                    ada_copy(u + 3, 1)

            def gate_copy(i, which, t):
                act.wait_ge(ready[t], USE_Z + U_G + 2 * i + which + 1)
                fn(g_out[:, which, cols(t)], psum[:, t, 0:TW[t]], ACT.Copy).then_inc(free[t], 1)

            def attend(i, last_turn=False):
                first = isinstance(i, int) and i == 0
                k0 = P if first else 0
                kks = [1] if first else [0, 1]
                u = U_G + 2 * i

                def exps(kv):
                    act.wait_ge(nmax_done, 2 * i + kv + 1)
                    for c in range(G):
                        fn(pr[:, kv, c, k0:256], pr[:, kv, c, k0:256], ACT.Exp, bias=nmx[:, kv, c:c + 1], accum_out=rsum[:, kv, c:c + 1])
                    fn(esk[:, kv, :], dsk[:, kv, :], ACT.Exp).then_inc(exp_done, 1)

                def pt_halves(kv):
                    act.wait_ge(pt_ready, 2 * i + kv + 1)
                    wait(act, o_ready, 2 * i + kv)
                    fn(pt_hi[:, kks[0]:2, :], psum[:, 5 + kks[0]:7, :], ACT.Copy).then_inc(pt_hi_done, 1)

                def o_copy(kv):
                    act.wait_ge(o_ready, 2 * i + kv + 1)
                    h = slice(kv * HD, (kv + 1) * HD)
                    fn(z[h, 2:6, bass.ds(i * P, P)], psum[h, 7, :].rearrange("p (c t) -> p c t", c=G), ACT.Copy).then_inc(o_read, 1)

                split_hi(u + 1, 1, 16 * (U_G // 2) + 48 + 16 * i, USE_Z + u)
                act.wait_ge(vt_ready, i + 1)
                wait(act, o_ready, 2 * i)
                fn(v_hi[:, kks[0]:2, :], psum[:, 7, kks[0] * P:256].rearrange("p (k c) -> p k c", c=P), ACT.Copy).then_inc(v_hi_done, 1)
                exps(0)
                wait(act, g_saved, 16 * i)
                gate_copy(i, 0, 0)
                gate_copy(i, 0, 1)
                pt_halves(0)
                gate_copy(i, 0, 2)
                split_hi(u + 2, 0, loads_of(U_AB) if last_turn else 16 * (U_G // 2) + 64 + 16 * i, USE_Z + u + 1)
                exps(1)
                o_copy(0)
                gate_copy(i, 1, 0)
                gate_copy(i, 1, 1)
                pt_halves(1)
                gate_copy(i, 1, 2)
                o_copy(1)

            attend(0)
            with act.Fori(1, BLK - 1) as i:
                attend(i)
            attend(BLK - 1, last_turn=True)

            act.wait_ge(out_t_ready, 1)
            fn(kv_out[:, 0:256], psum[:, 5, 0:256], ACT.Copy).then_inc(out_t_read, 1)
            fn(kv_out[0:TS, 256:512], psum[0:TS, 5, 256:512], ACT.Copy).then_inc(out_t_read, 1)
            act.wait_ge(out_t_ready, 2)
            fn(poolp_out[0:PAD, :], psum[0:PAD, 6, :], ACT.Copy).then_inc(out_t_read, 1)
            act.wait_ge(out_t_ready, 3)
            fn(pools_out[0:NB * PAD, :], psum[0:NB * PAD, 7, :], ACT.Copy).then_inc(out_t_read, 1)
            act.wait_ge(kct_ready, 1)
            fn(ks_hi[:, 0:NB * WIN].rearrange("p (b k) -> p b k", b=2), psum[:, 3:5, :], ACT.Copy).then_inc(kct_hi, 1)
            fn(ks_hi[:, NB * WIN:SK], z[:, 0, TP:T], ACT.Copy).then_inc(kct_hi, 1)
            for kv in range(NKV):
                act.wait_ge(ss_nmax, kv + 1)
                fn(ps[:, kv, :], ps[:, kv, :], ACT.Exp, bias=nmx[:, kv, 0:1], accum_out=rsum[:, kv, 0:1])
                fn(esk[:, kv, 0:1], dsk[:, kv, 0:1], ACT.Exp).then_inc(ss_exp, 1)

            def d_half(g):
                act.wait_ge(ready[2], USE_POOL + g - 1 if g >= 2 else USE_SS + 2)
                fn(d_hi[g % 2][:, :], z[:, 6 + g, :], ACT.Copy).then_inc(d_hi_done, 1)

            act.wait_ge(pool_done, 1)
            act.wait_ge(vs_done, 1)
            act.wait_ge(ss_p, 1)
            for kv in range(NKV):
                act.wait_ge(sst_ready, kv + 1)
                wait(act, so_ready, kv)
                fn(pst_hi[:, 0:NB, :].rearrange("p (b k) c -> p b (k c)", b=2), psum[:, 5:7, :], ACT.Copy).then_inc(sst_hi, 1)
                fn(pst_hi[0:TS, NB, :], psum[0:TS, 4, 0:P], ACT.Copy).then_inc(sst_hi, 1)
                d_half(kv)
                act.wait_ge(so_ready, kv + 1)
                h = slice(kv * HD, (kv + 1) * HD)
                fn(z[h, 2:6, TP:T], psum[h, 7, 0:P].rearrange("p (c t) -> p c t", c=G), ACT.Copy).then_inc(so_read, 1)
            act.wait_ge(so_read, 2)
            for g in range(NG):
                fn(o_hi[:, g, :], z[:, 2 + g, :], ACT.Copy).then_inc(o_hi_done, 1)
                if g >= 2:
                    d_half(g)
                for t in range(3):
                    n = 3 * g + t
                    act.wait_ge(ready[t], USE_POOL + g + 1)
                    wait(act, a_lo_done, n - 1)
                    fn(a_t[:, n % 2, 0:TW[t]], psum[:, t, 0:TW[t]], ACT.Identity, scale=vec[:, NMOD + 2 * DK + g:NMOD + 2 * DK + g + 1])\
                        .then_inc(free[t], 1)
                    act.wait_ge(free[t], USE_POOL + g + 1)
                    fn(a_hi[:, g, cols(t)], a_t[:, n % 2, 0:TW[t]], ACT.Copy).then_inc(a_hi_done, 1)

            def gate_halves(j, slot, turn, loads, use):
                act.wait_ge(g_in_sem[slot], 16 * turn + 16)
                fn(g_in[:, slot, :, :], g_in[:, slot, :, :], ACT.Sigmoid).then_inc(sig_done, 1)
                split_hi(0, 1 - slot, loads, use)
                for t in range(3):
                    act.wait_ge(sum_done, 3 * j + t + 1)
                    fn(mg_hi[:, bass.ds(j, 1), cols(t)].rearrange("p o t -> p (o t)"), mt[:, 0, t, 0:TW[t]], ACT.Copy).then_inc(mg_hi_done, 1)

            with act.Fori(0, 3) as p:
                gate_halves(2 * p, 0, p, LOADS_AB + 48 + 48 * p, USE_AB + 2 * p)
                gate_halves(2 * p + 1, 1, p, LOADS_AB + 96 + 48 * p, USE_AB + 1 + 2 * p)
            gate_halves(6, 0, 3, loads_of(U_AB + 7), USE_AB + 6)
            gate_halves(7, 1, 3, loads_of(U_O), USE_AB + 7)

            with act.Fori(0, 4) as p:
                for s in range(2):
                    j = 2 * p + s
                    split_hi(0, 1 - s, LOADS_O + 16 + 16 * (p + s), USE_O + j)
                    for t in range(3):
                        act.wait_ge(free[t], USE_O + j + 1)
                        if t == 2:
                            act.wait_ge(x1_done, j + 1)
                        act.wait_ge(acc_done, 3 * j + 1)
                        fn(sq_t[:, t, 0:TW[t]], x1[:, bass.ds(j, 1), cols(t)].rearrange("p o t -> p (o t)"), ACT.Square).then_inc(sq_done, 1)

            split_hi(0, 1, LOADS_O + 80, USE_O + 8)

            for t in range(3):
                n = min(TW[t], TP - TC[t])
                if t == 0:
                    for r in range(3):
                        act.wait_ge(ready[r], USE_R2 + 1)
                        fn(R[:, cols(r)], psum[:, r, 0:TW[r]], ACT.Copy).then_inc(free[r], 1)
                with act.Fori(0, 4) as q:
                    for s in range(2):
                        j = 2 * q + s
                        act.wait_ge(n2_tmp, 8 * t + j + 1)
                        fn(h2_hi[:, bass.ds(j, 1), TC[t]:TC[t] + n].rearrange("p o t -> p (o t)"), nrm_t2[:, s, 0:n], ACT.Identity,
                           bias=mod[:, bass.ds(3 * DK + j, 1), 0:1].rearrange("p o c -> p (o c)")).then_inc(n2_hi, 1)
            act.wait_ge(h2s_done, 1)
            act.wait_ge(h2_done, 24)

            def ff_tiles(g, j, s):
                side = isinstance(j, int) and g == 0 and j < 2
                for t in range(3):
                    n = 24 * g + 3 * j + t
                    sl = (3 * s + t) % 2
                    done, read, bank, use = ready[t], free[t], t, USE_F + 16 * g + j
                    if side:
                        done, read, bank, use = (ready[t], free[t], t, USE_F + 1) if j == 0 else (readyB[t], freeB[t], 3 + t, N_AB)
                    act.wait_ge(done, use + 1)
                    wait(act, ff_sq, n - 1)
                    wait(act, ff_hi_done, n - 1)
                    fn(r_t[:, sl, 0:TW[t]], psum[:, bank, 0:TW[t]], ACT.Relu).then_inc(read, 1)
                    act.wait_ge(read, use + 1)
                    fn(ff_hi[:, bass.ds(j, 1), cols(t)].rearrange("p o t -> p (o t)"), r_t[:, sl, 0:TW[t]], ACT.Square).then_inc(ff_hi_done, 1)

            def up(g, i):
                for s in range(2):
                    split_hi(0, 1 - s, LOADS_O + 80 + 128 * g + 16 * i + 16 * s, USE_F + 16 * g + 2 * i + s)
                    ff_tiles(g, 2 * i + s, s)

            def down(g):
                with act.Fori(0, 4) as i:
                    for s in range(2):
                        split_hi(0, 1 - s, LOADS_O + 144 + 128 * g + 16 * i + 16 * s, USE_F + 8 + 16 * g + 2 * i + s)

            ff_tiles(0, 0, 0)
            split_hi(0, 0, LOADS_O + 96, USE_F + 2)
            ff_tiles(0, 1, 1)
            act.wait_ge(readyB[2], N_AB + 1)
            split_hi(0, 1, LOADS_O + 96, 0)
            ff_tiles(0, 2, 0)
            split_hi(0, 0, LOADS_O + 112, USE_F + 3)
            ff_tiles(0, 3, 1)
            with act.Fori(2, 4) as i:
                up(0, i)
            down(0)
            with act.Fori(1, 3) as g:
                with act.Fori(0, 4) as i:
                    up(g, i)
                down(g)
            with act.Fori(0, 4) as i:
                up(3, i)
            for j in range(1, DK):
                act.wait_ge(w_in[j % 2], loads_of(U_F + 56 + j))
                for t in range(3):
                    wait(act, ready[t], USE_F + 56)
                fn(wd_hi[j][:, :, :], w_raw[j % 2][:, :, :], ACT.Copy).then_inc(w_hi_done, 1)

            for b in range(BLK + 1):
                n = P if b < BLK else TS
                bank = 0 if b == BLK else 3 + 2 * (b % 2)
                act.wait_ge(yt_ready, b + 1)
                wait(act, yss_done, b)
                wait(act, y_done, b - 2)
                act.wait_ge(w_lo_done, N_U)
                fn(y_sq[0:n, :], psum[0:n, bank:bank + 2, :], ACT.Square, accum_out=fin_ss[0:n, b % 3, :]).then_inc(yss_done, 1)

        @block.vector
        def _(dve):
            tt, ts_, stt = nc.vector.tensor_tensor, nc.vector.tensor_scalar, nc.vector.scalar_tensor_tensor
            ch = Chain(dve, dve_c)

            def f(t):
                return t.bitcast(F32)

            dve.wait_ge(c_sig, 1)
            tt(c_sil[0:NC, :], c_sil[0:NC, :], c_row[0:NC, :], ALU.mult).then_inc(c_silu, 1)
            for b in range(BLK + 1):
                n = P if b < BLK else TS
                dve.wait_ge(x_land[b % 4], 16 * (b // 4 + 1))
                wait(dve, x_sq, b)
                nc.vector.tensor_tensor_reduce(out=sq_x[0:n, :], in0=x_in[0:n, b % 4, :], in1=x_in[0:n, b % 4, :], scale=1.0, scalar=0.0,
                                               op0=ALU.mult, op1=ALU.add, accum_out=ssq[0:n, b:b + 1]).then_inc(x_sq, 1)

            def diagonals(diag):
                dve.wait_ge(rms_done, 2)
                tt(diag[:, 0:BLK, :], ident[:, :].unsqueeze(1).to_broadcast([P, BLK, P]), ssq[:, 0:BLK].unsqueeze(2).to_broadcast([P, BLK, P]), ALU.mult)\
                    .then_inc(diag_done, 1)
                tt(diag[0:TS, BLK, 0:TS], ident[0:TS, 0:TS], ssq[0:TS, BLK:BLK + 1].to_broadcast([TS, TS]), ALU.mult).then_inc(diag_done, 1)

            dve.wait_ge(x_sq, 9)
            ts_(rms[:, 0:BLK], ssq[:, 0:BLK], 1.0 / D, EPS, ALU.mult, ALU.add)
            ts_(rms[0:TS, BLK:BLK + 1], ssq[0:TS, BLK:BLK + 1], 1.0 / D, EPS, ALU.mult, ALU.add).then_inc(ms_done, 1)
            dve.wait_ge(const_done, 4)
            diagonals(diag1)

            def ada_add(n, s, col):
                dve.wait_ge(modt_ready, n + 1)
                tt(mod[:, 4 * col:4 * col + 4, :], psum[:, 5 + s, 0:64].rearrange("p (q c) -> p q c", c=16)[:, :, 0:NC],
                   vec[:, 4 * col:4 * col + 4].unsqueeze(2).to_broadcast([P, 4, NC]), ALU.add).then_inc(mod_done, 1)
                dve.wait_ge(mod_done, n + 1)

            def gains(gain, j0, n, scale_chunk, g_chunk):
                ch.step(stt(gain[:, j0:j0 + n, :], mod[:, scale_chunk + j0:scale_chunk + j0 + n, :], 1.0,
                            vec[:, g_chunk + j0:g_chunk + j0 + n].unsqueeze(2).to_broadcast([P, n, NC]), ALU.add, ALU.mult))

            def split_lo(u, slot):
                dve.wait_ge(w_hi_done, u + 1)
                tt(w_lo[slot][:, :, :], w_raw[slot][:, :, :], f(w_hi[slot][:, :, :]), ALU.subtract).then_inc(w_lo_done, 1)

            def norm_pair(m, src, gain, dst_hi, dst_lo, j, shift, tl, first):
                tile = slice(512 * tl, 512 * tl + 512)
                tmp = nrm_t if shift == 0 else nrm_t2
                for s in range(2):
                    if not first:
                        dve.wait_ge(n_hi, m + s - 1)
                        dve.wait_ge(h_done, m + s - 1 + (0 if shift == 0 else 1))
                    stt(tmp[:, s, :], src[:, bass.ds(j + s, 1), tile].rearrange("p o t -> p (o t)"),
                        gain[:, bass.ds(j + s, 1), 0:1].rearrange("p o c -> p (o c)"), R[:, tile], ALU.mult, ALU.mult).then_inc(n_tmp, 1)
                for s in range(2):
                    dve.wait_ge(n_hi, m + s + 1)
                    stt(dst_lo[:, bass.ds(j + s, 1), tile].rearrange("p o t -> p (o t)"), tmp[:, s, :],
                        mod[:, bass.ds(shift + j + s, 1), 0:1].rearrange("p o c -> p (o c)"),
                        f(dst_hi[:, bass.ds(j + s, 1), tile]).rearrange("p o t -> p (o t)"), ALU.add, ALU.subtract).then_inc(h_done, 1)

            def norm_samples(src, gain, dst_hi, dst_lo, shift):
                def v(t):
                    return t.rearrange("p j (b t) -> p j b t", t=NT)

                ch.step(tt(smp_t[:, :, :, :], v(src[:, :, TP:T]), gain[:, :, 1:NC].unsqueeze(3).to_broadcast([P, DK, NB, NT]), ALU.mult))
                flat = smp_t[:, :, :, :].rearrange("p j b t -> p j (b t)")
                ch.step(tt(flat, flat, R[:, TP:T].unsqueeze(1).to_broadcast([P, DK, TS]), ALU.mult))
                ch.step(tt(smp_t[:, :, :, :], smp_t[:, :, :, :], mod[:, shift:shift + DK, 1:NC].unsqueeze(3).to_broadcast([P, DK, NB, NT]), ALU.add))
                ch.step(nc.vector.tensor_copy(dst_hi[:, :, TP:T], flat))
                tt(dst_lo[:, :, TP:T], flat, f(dst_hi[:, :, TP:T]), ALU.subtract).then_inc(h_done, 1)

            ada_add(0, 0, ada_col[0])
            ada_add(1, 1, ada_col[1])
            gains(gain1, 0, 4, DK, NMOD)
            for t in range(3):
                dve.wait_ge(free[t], USE_R1 + 1)
            dve.wait_ge(xt_read, 9)
            split_lo(0, 0)
            for hf in range(2):
                if hf == 1:
                    split_lo(1, 1)
                    ada_add(2, 0, ada_col[2])
                    ada_add(3, 1, ada_col[3])
                    gains(gain1, 4, 4, DK, NMOD)
                for tl in range(2):
                    if hf == 0 and tl == 0:
                        norm_pair(0, xT, gain1, h_hi, h_lo, 0, 0, 0, True)
                        norm_pair(2, xT, gain1, h_hi, h_lo, 2, 0, 0, False)
                        continue
                    with dve.Fori(0, 2) as q:
                        norm_pair(8 * hf + 4 * tl + 2 * q, xT, gain1, h_hi, h_lo, 4 * hf + 2 * q, 0, tl, False)
            norm_samples(xT, gain1, h_hi, h_lo, 0)

            def pool_group(g):
                w = 2 << g
                u = z[:, 6 + g, :]
                for t in range(3):
                    dve.wait_ge(free[t], USE_Z + 6 + g + 1)
                us = u[:, TP:T].rearrange("p (b t) -> p b t", t=NT)
                ch.step(nc.vector.tensor_copy(pool_last[:, g, :], u[:, TP - PAD:TP]))
                ch.step(nc.vector.tensor_copy(pool_s[:, g, :, PAD:PAD + NT], us))
                cur, cur_s, lag = u[:, 0:TP], pool_s[:, g, :, :], 1
                bufs, bufs_s = [win_a, win_b], [win_sa, win_sb]
                while lag < w:
                    new, new_s = bufs[0][:, :], bufs_s[0][:, :, :]
                    bufs.reverse()
                    bufs_s.reverse()
                    tt(new[:, lag:TP], cur[:, lag:TP], cur[:, 0:TP - lag], ALU.add)
                    nc.vector.tensor_copy(new[:, 0:lag], cur[:, 0:lag])
                    ch.step(tt(new_s[:, :, 2 * lag - 1:], cur_s[:, :, 2 * lag - 1:], cur_s[:, :, lag - 1:PAD + NT - lag], ALU.add))
                    cur, cur_s, lag = new, new_s, 2 * lag
                ch.step(tt(cur[:, 0:16], cur[:, 0:16], inv_cnt[:, g, :], ALU.mult))
                tt(u[:, 0:16], cur[:, 0:16], u[:, 0:16], ALU.subtract)
                stt(u[:, 16:TP], cur[:, 16:TP], 1.0 / w, u[:, 16:TP], ALU.mult, ALU.subtract)
                last = stt(us, cur_s[:, :, PAD:PAD + NT], 1.0 / w, us, ALU.mult, ALU.subtract)
                ch.step(last)

            dve.wait_ge(tab_in, 16 * 6)
            for p in range(5):
                for s in range(2):
                    u = 2 * p + s
                    if u >= 1:
                        split_lo(u + 1, (u + 1) % 2)
                    if u >= 7:
                        pool_group(u - 7)
                if p:
                    ada_add(2 * p + 2, 0, 2 * p + 2)
                    ada_add(2 * p + 3, 1, 2 * p + 3)
            gains(gain2, 0, DK, 4 * DK, NMOD + DK)
            pool_group(3)

            nc.vector.tensor_copy(pool_tail[:, :, :].rearrange("p g (b r) -> p g b r", b=NB), pool_s[:, :, :, NT:PAD + NT]).then_inc(pool_done, 1)

            def attend(i):
                first = isinstance(i, int)
                k0 = P if first else 0
                kks = [1] if first else [0, 1]
                nk = 2 * P - k0
                u = U_G + 2 * i

                def soft_a(kv):
                    dve.wait_ge(s_ready, 2 * i + kv + 1)
                    wait(dve, pt_ready, 2 * i + kv - 1 if not first else 0)
                    s_all = psum[:, 3:5, :].rearrange("p b (c k) -> p (b c) k", k=256)
                    ch.step(stt(pr[:, kv, :, k0:256], s_all[:, :, k0:256], SCALE, bias_p[:, G * kv:G * kv + G, k0:256], ALU.mult, ALU.add))
                    ch.step(nc.vector.tensor_reduce(mx[:, kv, :], pr[:, kv, :, k0:256], AX.X, ALU.max))
                    ch.step(tt(mx[:, kv, :], mx[:, kv, :], sink_p[:, G * kv:G * kv + G], ALU.max))
                    ts_(nmx[:, kv, :], mx[:, kv, :], -1.0, None, ALU.mult)
                    tt(dsk[:, kv, :], sink_p[:, G * kv:G * kv + G], mx[:, kv, :], ALU.subtract).then_inc(nmax_done, 1)

                def soft_b(kv):
                    dve.wait_ge(exp_done, 2 * i + kv + 1)
                    ch.step(tt(rden[:, kv, :], rsum[:, kv, :], esk[:, kv, :], ALU.add))
                    ch.step(nc.vector.reciprocal(rden[:, kv, :], rden[:, kv, :]))
                    tt(pr[:, kv, :, k0:256], pr[:, kv, :, k0:256], rden[:, kv, :].unsqueeze(2).to_broadcast([P, G, nk]), ALU.mult).then_inc(p_done, 1)

                def pt_low(kv):
                    dve.wait_ge(pt_hi_done, 2 * i + kv + 1)
                    tt(pt_lo[:, kks[0]:2, :], psum[:, 5 + kks[0]:7, :], f(pt_hi[:, kks[0]:2, :]), ALU.subtract).then_inc(pt_lo_done, 1)

                dve.wait_ge(stage_done, i + 1)
                keys = slice(0, P) if first else bass.ds(i * P - P, 2 * P)
                tt(q_lo[:, :, :], z[:, 2:6, bass.ds(i * P, P)], f(q_hi[:, :, :]), ALU.subtract)
                tt(k_lo[:, k0:256], z[:, 0, keys], f(k_hi[:, k0:256]), ALU.subtract).then_inc(qk_lo_done, 1)
                split_lo(u + 1, 1)
                dve.wait_ge(v_hi_done, i + 1)
                tt(v_lo[:, kks[0]:2, :], psum[:, 7, kks[0] * P:256].rearrange("p (k c) -> p k c", c=P), f(v_hi[:, kks[0]:2, :]), ALU.subtract)\
                    .then_inc(v_lo_done, 1)
                soft_a(0)
                soft_b(0)
                pt_low(0)
                soft_a(1)
                split_lo(u + 2, 0)
                soft_b(1)
                pt_low(1)

            dve.wait_ge(bp_in, 16)
            attend(0)
            per = 2 * 5
            with dve.Fori(1, BLK) as i:
                ch.enter(i, 1, per)
                attend(i)
            ch.leave(BLK - 1, per)

            dve.wait_ge(kct_hi, 2)
            tt(ks_lo[:, 0:NB * WIN].rearrange("p (b k) -> p b k", b=2), psum[:, 3:5, :], f(ks_hi[:, 0:NB * WIN]).rearrange("p (b k) -> p b k", b=2), ALU.subtract)
            tt(ks_lo[:, NB * WIN:SK], z[:, 0, TP:T], f(ks_hi[:, NB * WIN:SK]), ALU.subtract).then_inc(ks_done, 1)
            dve.wait_ge(bs_in, 16)
            for kv in range(NKV):
                for t in range(3):
                    dve.wait_ge(ready[t], USE_SS + kv + 1)
                    ins = stt(ps[:, kv, cols(t)], psum[:, t, 0:TW[t]], SCALE, bias_s[:, kv, cols(t)], ALU.mult, ALU.add)
                    ins.then_inc(free[t], 1)
                for t in range(3):
                    dve.wait_ge(free[t], USE_SS + kv + 1)
                ch.step(nc.vector.tensor_reduce(mx[:, kv, 0:1], ps[:, kv, :], AX.X, ALU.max))
                ch.step(tt(mx[:, kv, 0:1], mx[:, kv, 0:1], sink_s[:, kv:kv + 1], ALU.max))
                ts_(nmx[:, kv, 0:1], mx[:, kv, 0:1], -1.0, None, ALU.mult)
                tt(dsk[:, kv, 0:1], sink_s[:, kv:kv + 1], mx[:, kv, 0:1], ALU.subtract).then_inc(ss_nmax, 1)
            for kv in range(NKV):
                dve.wait_ge(ss_exp, kv + 1)
                ch.step(tt(rden[:, kv, 0:1], rsum[:, kv, 0:1], esk[:, kv, 0:1], ALU.add))
                ch.step(nc.vector.reciprocal(rden[:, kv, 0:1], rden[:, kv, 0:1]))
                ts_(ps[:, kv, :], ps[:, kv, :], rden[:, kv, 0:1], None, ALU.mult).then_inc(ss_p, 1)

            def d_low(g):
                dve.wait_ge(d_hi_done, g + 1)
                tt(d_lo[g % 2][:, :], z[:, 6 + g, :], f(d_hi[g % 2][:, :]), ALU.subtract).then_inc(d_lo_done, 1)

            for kv in range(NKV):
                dve.wait_ge(sst_hi, 2 * kv + 2)
                tt(pst_lo[:, 0:NB, :].rearrange("p (b k) c -> p b (k c)", b=2), psum[:, 5:7, :], f(pst_hi[:, 0:NB, :]).rearrange("p (b k) c -> p b (k c)", b=2), ALU.subtract)\
                    .then_inc(sst_lo, 1)
                tt(pst_lo[0:TS, NB, :], psum[0:TS, 4, 0:P], f(pst_hi[0:TS, NB, :]), ALU.subtract).then_inc(sst_lo, 1)
                d_low(kv)
            for g in range(NG):
                dve.wait_ge(o_hi_done, g + 1)
                tt(o_lo[:, g, :], z[:, 2 + g, :], f(o_hi[:, g, :]), ALU.subtract).then_inc(o_lo_done, 1)
                if g >= 2:
                    d_low(g)
                for t in range(3):
                    n = 3 * g + t
                    dve.wait_ge(a_hi_done, n + 1)
                    tt(a_lo[:, g, cols(t)], a_t[:, n % 2, 0:TW[t]], f(a_hi[:, g, cols(t)]), ALU.subtract).then_inc(a_lo_done, 1)

            def gated(j, u, slot):
                def lo(t):
                    dve.wait_ge(mg_hi_done, 3 * j + t + 1)
                    tt(mg_lo[:, bass.ds(j, 1), cols(t)].rearrange("p o t -> p (o t)"), mt[:, 0, t, 0:TW[t]],
                       f(mg_hi[:, bass.ds(j, 1), cols(t)]).rearrange("p o t -> p (o t)"), ALU.subtract).then_inc(mg_lo_done, 1)

                split_lo(u + 1, 1 - slot)
                dve.wait_ge(sig_done, j + 1)
                for t in range(3):
                    dve.wait_ge(readyB[t], j + 1)
                    wait(dve, mg_lo_done, 3 * j + t - 2)
                    tt(mt[:, 1, t, 0:TW[t]], psum[:, 3 + t, 0:TW[t]], g_in[:, slot, 1, cols(t)], ALU.mult).then_inc(freeB[t], 1)
                    dve.wait_ge(ready[t], USE_AB + j + 1)
                    tt(mt[:, 0, t, 0:TW[t]], psum[:, t, 0:TW[t]], g_in[:, slot, 0, cols(t)], ALU.mult).then_inc(free[t], 1)
                    if t:
                        lo(t - 1)
                lo(2)

            gated(0, U_AB, 0)
            gated(1, U_AB + 1, 1)
            with dve.Fori(1, 4) as p:
                for s in range(2):
                    gated(2 * p + s, U_AB + 2 * p + s, s)

            def add_gated(j, t, use, gate_chunk, res, count, bank=None, done=None):
                x = x1[:, bass.ds(j, 1), :].rearrange("p o t -> p (o t)")
                gt = mod[:, bass.ds(gate_chunk + j, 1), :].rearrange("p o c -> p (o c)")
                bank = t if bank is None else bank
                dve.wait_ge(ready[bank], use + 1)
                n = min(TW[t], TP - TC[t])
                c0 = TC[t]
                if t == 2:
                    ch.step(tt(smp_t[:, 0, :, :], psum[:, bank, n:TW[2]].rearrange("p (b t) -> p b t", t=NT), gt[:, 1:NC].unsqueeze(2).to_broadcast([P, NB, NT]), ALU.mult))
                last = stt(x[:, c0:c0 + n], psum[:, bank, 0:n], gt[:, 0:1], res[:, c0:c0 + n], ALU.mult, ALU.add)
                last.then_inc(free[bank], 1)
                if done is not None:
                    if t == 2:
                        tt(x[:, TP:T], smp_t[:, 0, :, :].rearrange("p b t -> p (b t)"), res[:, TP:T], ALU.add).then_inc(done, 1)
                        dve.wait_ge(done, count)
                elif t == 2:
                    tt(x[:, TP:T], smp_t[:, 0, :, :].rearrange("p b t -> p (b t)"), res[:, TP:T], ALU.add).then_inc(x1_done, 1)
                    dve.wait_ge(x1_done, count)

            per = 2
            with dve.Fori(0, 4) as p:
                ch.enter(p, 0, per)
                for s in range(2):
                    j = 2 * p + s
                    split_lo(U_O + j + 1, 1 - s)
                    dve.wait_ge(xr_in[s], 16 * p + 16)
                    for t in range(3):
                        add_gated(j, t, USE_O + j, 2 * DK, x_res[:, s, :], j + 1)
            ch.leave(4, per)

            split_lo(U_F + 1, 1)
            dve.wait_ge(ss_ready, 1)
            ts_(rms[:, 0:BLK], psum[:, 6, 0:BLK], 1.0 / D, EPS, ALU.mult, ALU.add)
            ts_(rms[0:TS, BLK:BLK + 1], psum[0:TS, 6, BLK:BLK + 1], 1.0 / D, EPS, ALU.mult, ALU.add).then_inc(ms_done, 1)
            dve.wait_ge(rms_done, 4)
            for t in range(3):
                n = min(3, BLK - 3 * t)
                last = tt(diag2[:, 3 * t:3 * t + n, :], ident[:, :].unsqueeze(1).to_broadcast([P, n, P]), ssq[:, 3 * t:3 * t + n].unsqueeze(2).to_broadcast([P, n, P]), ALU.mult)
                if t == 2:
                    last = tt(diag2[0:TS, BLK, 0:TS], ident[0:TS, 0:TS], ssq[0:TS, BLK:BLK + 1].to_broadcast([TS, TS]), ALU.mult)
                last.then_inc(diag2_done, 1)
            for t in range(3):
                dve.wait_ge(free[t], USE_R2 + 1)
                n = min(TW[t], TP - TC[t])
                tile = slice(TC[t], TC[t] + n)

                def pair(m, j, first):
                    for s in range(2):
                        if not first:
                            dve.wait_ge(h2_done, m + s - 1)
                        stt(nrm_t2[:, s, 0:n], x1[:, bass.ds(j + s, 1), tile].rearrange("p o t -> p (o t)"),
                            gain2[:, bass.ds(j + s, 1), 0:1].rearrange("p o c -> p (o c)"), R[:, tile], ALU.mult, ALU.mult).then_inc(n2_tmp, 1)
                    for s in range(2):
                        dve.wait_ge(n2_hi, m + s + 1)
                        stt(h2_lo[:, bass.ds(j + s, 1), tile].rearrange("p o t -> p (o t)"), nrm_t2[:, s, 0:n],
                            mod[:, bass.ds(3 * DK + j + s, 1), 0:1].rearrange("p o c -> p (o c)"),
                            f(h2_hi[:, bass.ds(j + s, 1), tile]).rearrange("p o t -> p (o t)"), ALU.add, ALU.subtract).then_inc(h2_done, 1)

                if t == 0:
                    pair(0, 0, True)
                    with dve.Fori(1, 4) as q:
                        pair(2 * q, 2 * q, False)
                else:
                    with dve.Fori(0, 4) as q:
                        pair(8 * t + 2 * q, 2 * q, False)

            def ff_tiles(g, j, s):
                side = isinstance(j, int) and g == 0 and j < 2
                for t in range(3):
                    n = 24 * g + 3 * j + t
                    sl = (3 * s + t) % 2
                    read, use = free[t], USE_F + 16 * g + j
                    if side:
                        read, use = (free[t], USE_F + 1) if j == 0 else (freeB[t], N_AB)
                    dve.wait_ge(read, use + 1)
                    wait(dve, ff_lo_done, n - 1)
                    tt(f_t[:, sl, 0:TW[t]], r_t[:, sl, 0:TW[t]], r_t[:, sl, 0:TW[t]], ALU.mult).then_inc(ff_sq, 1)
                    dve.wait_ge(ff_sq, n + 1)
                    dve.wait_ge(ff_hi_done, n + 1)
                    tt(ff_lo[:, bass.ds(j, 1), cols(t)].rearrange("p o t -> p (o t)"), f_t[:, sl, 0:TW[t]],
                       f(ff_hi[:, bass.ds(j, 1), cols(t)]).rearrange("p o t -> p (o t)"), ALU.subtract).then_inc(ff_lo_done, 1)

            def up(g, i):
                for s in range(2):
                    split_lo(U_F + 16 * g + 2 * i + s + 1, 1 - s)
                    ff_tiles(g, 2 * i + s, s)

            def down(g):
                with dve.Fori(0, 4) as i:
                    ch.enter(i, 0, 2)
                    for s in range(2):
                        j = 2 * i + s
                        split_lo(U_F + 16 * g + 8 + j + 1, 1 - s)
                        for t in range(3):
                            add_gated(j, t, USE_F + 16 * g + 8 + j, 5 * DK, x1[:, bass.ds(j, 1), :].rearrange("p o t -> p (o t)"), N_O + 8 * g + j + 1)
                ch.leave(4, 2)

            ff_tiles(0, 0, 0)
            split_lo(U_F + 2, 0)
            ff_tiles(0, 1, 1)
            split_lo(U_F + 3, 1)
            ff_tiles(0, 2, 0)
            split_lo(U_F + 4, 0)
            ff_tiles(0, 3, 1)
            with dve.Fori(2, 4) as i:
                up(0, i)
            down(0)
            outer = ch.base + ch.k
            with dve.Fori(1, 3) as g:
                ch.base, ch.k = outer + (g - 1) * 8, 0
                with dve.Fori(0, 4) as i:
                    up(g, i)
                down(g)
            ch.base, ch.k = outer + 2 * 8, 0
            with dve.Fori(0, 4) as i:
                up(3, i)

            def y_rms(b):
                n = P if b < BLK else TS
                dve.wait_ge(yss_done, b + 1)
                ts_(fin_r[0:n, b % 3, :], fin_ss[0:n, b % 3, :], 1.0 / D, EPS, ALU.mult, ALU.add).then_inc(yms_done, 1)

            def y_block(b):
                n = P if b < BLK else TS
                bank = 0 if b == BLK else 3 + 2 * (b % 2)
                dve.wait_ge(yr_done, b + 1)
                if b >= 3:
                    dve.wait_ge(y_sent[b % 3], 16 * (b // 3))
                stt(y_out[b % 3][0:n, :], psum[0:n, bank:bank + 2, :].rearrange("p b c -> p (b c)"), fin_ss[0:n, b % 3, :], fin_g[0:n, :], ALU.mult, ALU.mult)\
                    .then_inc(y_done, 1)

            for t in range(3):
                for j in range(DK):
                    n = DK * t + j
                    if t == 0 and j + 1 < DK:
                        dve.wait_ge(w_hi_done, U_F + 56 + j + 2)
                        tt(wd_lo[j + 1][:, :, :], w_raw[(j + 1) % 2][:, :, :], f(wd_hi[j + 1][:, :, :]), ALU.subtract).then_inc(w_lo_done, 1)
                    add_gated(j, t, USE_F + 56 + n // 3, 5 * DK, x1[:, j, :], j + 1, bank=n % 3, done=x_last)
                    b = 3 * (t - 1) + (j - 1) // 2
                    if t and j in (1, 3, 5):
                        if b == 0:
                            dve.wait_ge(fg_in, 16)
                        y_rms(b)
                    if t and j in (2, 4, 6):
                        y_block(b)
            for b in (6, 7, 8):
                y_rms(b)
                y_block(b)

        @block.gpsimd
        def _(pool):
            tt = nc.gpsimd.tensor_tensor
            cp = nc.gpsimd.tensor_copy
            ch = Chain(pool, pool_c)

            def f(t):
                return t.bitcast(F32)

            ch.step(nc.gpsimd.memset(ident[:, :], 0.0))
            nc.gpsimd.affine_select(out=ident[:, :], in_=ident[:, :], compare_op=ALU.not_equal, fill=1.0, base=0, pattern=[[-1, P]],
                                    channel_multiplier=1).then_inc(const_done, 1)
            nc.gpsimd.memset(ada_row[:, :, :], 0.0).then_inc(const_done, 1)
            nc.gpsimd.memset(ones[:, :], 1.0).then_inc(const_done, 1)
            nc.gpsimd.memset(half[:, :], -0.5).then_inc(const_done, 1)
            pool.wait_ge(const_done, 4)

            def powers(n):
                pool.wait_ge(ms_done, n + 1)
                tt(ssq[:, 0:BLK], rms[:, 0:BLK], half[:, 0:BLK], ALU.pow).then_inc(rms_done, 1)
                tt(ssq[0:TS, BLK:BLK + 1], rms[0:TS, BLK:BLK + 1], half[0:TS, 0:1], ALU.pow).then_inc(rms_done, 1)

            powers(0)

            def norm_samples(src, gain, dst_hi, dst_lo, shift, done):
                def v(t):
                    return t.rearrange("p j (b t) -> p j b t", t=NT)

                ch.step(tt(smp_t[:, :, :, :], v(src[:, :, TP:T]), gain[:, :, 1:NC].unsqueeze(3).to_broadcast([P, DK, NB, NT]), ALU.mult))
                flat = smp_t[:, :, :, :].rearrange("p j b t -> p j (b t)")
                ch.step(tt(flat, flat, R[:, TP:T].unsqueeze(1).to_broadcast([P, DK, TS]), ALU.mult))
                ch.step(tt(smp_t[:, :, :, :], smp_t[:, :, :, :], mod[:, shift:shift + DK, 1:NC].unsqueeze(3).to_broadcast([P, DK, NB, NT]), ALU.add))
                ch.step(cp(dst_hi[:, :, TP:T], flat))
                tt(dst_lo[:, :, TP:T], flat, f(dst_hi[:, :, TP:T]), ALU.subtract).then_inc(done, 1)

            def stage(i):
                first = isinstance(i, int)
                k0 = P if first else 0
                keys = slice(0, P) if first else bass.ds(i * P - P, 2 * P)
                blk = bass.ds(i * P, P)
                wait(pool, s_ready, 2 * i)
                wait(pool, vt_ready, i)
                cp(q_hi[:, :, :], z[:, 2:6, blk])
                cp(k_hi[:, k0:256], z[:, 0, keys])
                cp(v_st[:, k0 // P:2, :].rearrange("p k c -> p (k c)"), z[:, 1, keys]).then_inc(stage_done, 1)

            for t in range(3):
                pool.wait_ge(free[t], USE_Z + 6)
            pool.wait_ge(mod_done, 12)
            stage(0)
            with pool.Fori(1, BLK) as i:
                stage(i)

            pool.wait_ge(g_saved, 16 * BLK)
            pool.wait_ge(o_ready, 2 * BLK)
            ch.step(cp(qs_hi[:, :, :], z[:, 2:6, TP:T]))
            tt(qs_lo[:, :, :], z[:, 2:6, TP:T], f(qs_hi[:, :, :]), ALU.subtract).then_inc(qs_done, 1)
            pool.wait_ge(kvc_in, 32)
            ch.step(cp(vs_hi[:, 0:NB, :], vc[:, :, :]))
            tt(vs_lo[:, 0:NB, :], vc[:, :, :], f(vs_hi[:, 0:NB, :]), ALU.subtract)
            pool.wait_ge(out_t_read, 2)
            ch.step(cp(vs_hi[0:TS, NB, :], kv_out[0:TS, 3 * P:4 * P]))
            tt(vs_lo[0:TS, NB, :], kv_out[0:TS, 3 * P:4 * P], f(vs_hi[0:TS, NB, :]), ALU.subtract).then_inc(vs_done, 1)
            pool.wait_ge(ks_done, 1)
            pool.wait_ge(wp_in, 16)
            ch.step(cp(wp_hi[:, :, :], wp_raw[:, :, :]))
            tt(wp_lo[:, :, :], wp_raw[:, :, :], f(wp_hi[:, :, :]), ALU.subtract).then_inc(wp_done, 1)

            with pool.Fori(0, N_AB) as j:
                for t in range(3):
                    pool.wait_ge(free[t], USE_AB + j + 1)
                    tt(mt[:, 0, t, 0:TW[t]], mt[:, 0, t, 0:TW[t]], mt[:, 1, t, 0:TW[t]], ALU.add).then_inc(sum_done, 1)

            pool.wait_ge(sent, 16 * 22)
            nc.gpsimd.memset(acc[:, :], 0.0).then_inc(acc_done, 1)
            with pool.Fori(0, N_O - 1) as j:
                for t in range(3):
                    pool.wait_ge(sq_done, 3 * j + t + 1)
                    pool.wait_ge(acc_done, 3 * j + t + 1)
                    tt(acc[:, cols(t)], acc[:, cols(t)], sq_t[:, t, 0:TW[t]], ALU.add).then_inc(acc_done, 1)
            powers(1)
            pool.wait_ge(free[2], USE_R2 + 1)
            norm_samples(x1, gain2, h2_hi, h2_lo, 3 * DK, h2s_done)
            for b in range(BLK + 1):
                n = P if b < BLK else TS
                pool.wait_ge(yms_done, b + 1)
                tt(fin_ss[0:n, b % 3, :], fin_r[0:n, b % 3, :], half[0:n, 0:1], ALU.pow).then_inc(yr_done, 1)


_INS = ["x_prompt", "x_sample", "cache_k", "cache_v", "state_pool", "c_prompt", "c_sample", "w_ada", "b_ada", "norm1_g", "w_in", "w_pool",
        "pool_scale", "attn_sinks", "w_a", "w_b", "w_out", "norm2_g", "w_up", "w_down", "final_g"]
_OUTS = [(1, TP, D), (NB, NT, D), (1, 1, WIN, NKV, HD), (1, 1, WIN, NKV, HD), (1, 1, PAD, PW),
         (1, NB, WIN, NKV, HD), (1, NB, WIN, NKV, HD), (1, NB, PAD, PW)]


def _shape_tables(np):
    slopes = 2.0 ** (-8.0 * (np.arange(NH) + 1) / NH)
    dist = np.arange(P)[:, None] + P - np.arange(2 * P)[None, :]
    seen = (dist >= 0) & (dist < WIN)
    prompt = np.where(seen[:, None, :], -slopes[None, :, None] * dist[:, None, :], -1e30).astype(np.float32)
    row = np.arange(P)
    g, seq, tok = row // TS, (row % TS) // NT, row % NT
    key = np.arange(SK)
    new = key >= NB * WIN
    key_seq = np.where(new, (key - NB * WIN) // NT, key // WIN)
    key_pos = np.where(new, (key - NB * WIN) % NT, key % WIN - WIN)
    dist = tok[:, None] - key_pos[None, :]
    seen = (dist >= 0) & (dist < WIN) & (seq[:, None] == key_seq[None, :])
    sample = np.stack([np.where(seen, -slopes[v * G + g][:, None] * dist, -1e30) for v in range(NKV)], axis=1).astype(np.float32)
    pos = np.arange(16)
    inv = np.stack([1.0 / np.minimum(2 << n, pos + 1) for n in range(NG)]).astype(np.float32).reshape(-1)
    return {"alibi_prompt": prompt, "alibi_sample": sample, "inv_count": inv}


def kernel(**inputs):
    import numpy as _np
    import concourse.bacc as _bacc
    from concourse import mybir as _mybir
    from concourse.bass_utils import run_bass_kernel_spmd as _run

    nc = _bacc.Bacc("TRN2", target_bir_lowering=False, num_devices=1)
    arrays, args = {}, {}
    given = {name: _np.ascontiguousarray(inputs[name]) for name in _INS}
    given.update(_shape_tables(_np))
    for name, x in given.items():
        arrays[f"in_{name}_dram"] = x
        args[name] = nc.dram_tensor(f"in_{name}_dram", x.shape, _mybir.dt.from_np(x.dtype), kind="ExternalInput").ap()
    outs = [nc.dram_tensor(f"out_{i}_dram", shape, _mybir.dt.float32, kind="ExternalOutput").ap() for i, shape in enumerate(_OUTS)]
    hybrid_decoder_step(nc, args, outs)
    r = _run(nc, [arrays], core_ids=[0])
    return tuple(r.results[0][f"out_{i}_dram"] for i in range(len(_OUTS)))
```

```python
import concourse.bass as bass
from concourse import mybir
from contextlib import ExitStack

F32 = mybir.dt.float32
F32R = mybir.dt.float32r
ALU = mybir.AluOpType
ACT = mybir.ActivationFunctionType
AX = mybir.AxisListType

P = 128
D = 1024
DK = D // P
TP = 1024
NB, NT = 8, 4
TS = NB * NT
T = TP + TS
TW = (384, 384, 288)
TC = (0, 384, 768)
TM = max(TW)
BLK = TP // P
HD, NH, NKV = 64, 8, 2
G = NH // NKV
WIN = 128
DFF = 4 * D
PW = D // 2
NG = 4
PAD = 15
NMOD = 6 * DK
NC = 1 + NB
SK = NB * WIN + TS
EPS = 1e-6
SCALE = HD ** -0.5

Q0, U0, KZ, VZ = 0, 4, 8, 9
Z_ROW = (KZ, VZ, 0, 1, 2, 3, 4, 5, 6, 7)

U_Z, N_Z = 0, 10
U_G, N_G = 10, 16
U_AB, N_AB = 26, 8
U_O, N_O = 34, 8
U_F = 42
N_U = U_F + 64
USE_R1 = 0
USE_Z = 0
USE_SS = 26
USE_POOL = 28
USE_AB = 32
USE_O = 40
USE_R2 = 48
USE_F = 48
USE_B = 1


LOADS_AB = 16 * (U_AB // 2) + 32
LOADS_O = LOADS_AB + 48 * (N_AB // 2)


def use_of(u):
    if u < U_AB:
        return USE_Z + u
    return USE_AB + (u - U_AB) if u < U_F else USE_F + (u - U_F)


def loads_of(u):
    if u < U_AB:
        return 16 * (u // 2 + 1) + 16 * min(u // 2, 2)
    if u < U_O:
        return LOADS_AB + 48 * ((u - U_AB) // 2 + 1)
    return LOADS_O + 16 * ((u - U_O) // 2 + 1)


def wait(eng, sem, value):
    if isinstance(value, int) and value <= 0:
        return
    eng.wait_ge(sem, value)


class Chain:

    def __init__(self, eng, sem):
        self.eng, self.sem, self.base, self.k = eng, sem, 0, 0

    def step(self, ins):
        self.k += 1
        ins.then_inc(self.sem, 1)
        self.eng.wait_ge(self.sem, self.base + self.k)

    def enter(self, i, first, per):
        self.start = self.base + self.k
        self.base = self.start + (i - first) * per
        self.k = 0

    def leave(self, turns, per):
        assert self.k == per, (self.k, per)
        self.base, self.k = self.start + turns * per, 0


def hybrid_decoder_step(nc, a, outs):
    y_p, y_s, nk_p, nv_p, npool_p, nk_s, nv_s, npool_s = outs
    ctx = ExitStack()
    with ctx:
        def sem(name):
            return ctx.enter_context(nc.semaphore(name))

        arena_bytes = 212800
        arena = ctx.enter_context(nc.sbuf_tensor("arena", [P, arena_bytes // 4], F32))
        arena_at = 16512

        def at(name, offset, shape, dt=F32):
            size = 4
            for s in shape[1:]:
                size *= s
            assert offset % 32 == 0 and offset + size <= arena_bytes, (name, offset, size)
            return nc.alloc_sbuf_tensor_at(name, shape, dt, offset=arena_at + offset)

        ROW = 4 * T
        RA, RB, RC, RD = 0, 8 * ROW, 16 * ROW, 32 * ROW
        RE = RC + 10 * ROW
        RW = RD + 8 * ROW
        RM = RW + 6 * 4096

        w_raw = [at(f"w_raw{s}", RW + 4096 * s, [P, DK, P]) for s in range(2)]
        w_hi = [at(f"w_hi{s}", RW + 8192 + 4096 * s, [P, DK, P], F32R) for s in range(2)]
        w_lo = [at(f"w_lo{s}", RW + 16384 + 4096 * s, [P, DK, P], F32R) for s in range(2)]
        m = RM

        def small(name, shape, dt=F32):
            nonlocal m
            size = 4
            for s in shape[1:]:
                size *= s
            t = at(name, m, shape, dt)
            m += (size + 31) // 32 * 32
            return t

        mod = small("mod", [P, NMOD, NC])
        vec = small("vec", [P, 68])
        ident = small("ident", [P, P])
        ones = small("ones", [P, P])
        gain1 = small("gain1", [P, DK, NC])
        gain2 = small("gain2", [P, DK, NC])
        cT = small("cT", [P, DK, NC])
        pool_s = small("pool_s", [P, NG, NB, PAD + NT])
        inv_cnt = small("inv_cnt", [P, NG, 16])
        sink_p = small("sink_p", [P, NH])
        sink_s = small("sink_s", [P, NKV])
        ssq = small("ssq", [P, 9])
        rms = small("rms", [P, 9])
        half = small("half", [P, 9])
        mx = small("mx", [P, 2, G])
        nmx = small("nmx", [P, 2, G])
        dsk = small("dsk", [P, 2, G])
        esk = small("esk", [P, 2, G])
        rsum = small("rsum", [P, 2, G])
        rden = small("rden", [P, 2, G])
        fin_ss = small("fin_ss", [P, 3, 1])
        fin_r = small("fin_r", [P, 3, 1])
        v_st = small("v_st", [P, 2, P])
        smp_t = small("smp_t", [P, DK, NB, NT])
        pool_last = small("pool_last", [P, NG, PAD])
        m_pool = m
        assert m + 8448 + 1216 <= arena_bytes
        R = small("R", [P, T])
        acc = small("acc", [P, T])
        win_a = at("win_a", m_pool, [P, TP])
        win_b = at("win_b", m_pool + 4096, [P, TP])
        win_sa = at("win_sa", m_pool + 8192, [P, NB, PAD + NT])
        win_sb = at("win_sb", m_pool + 8192 + 608, [P, NB, PAD + NT])
        kv_out = at("kv_out", m_pool, [P, 512])
        poolp_out = at("poolp_out", m_pool + 2048, [P, 512])
        pool_tail = at("pool_tail", m_pool + 6144, [P, NG, NB * PAD])
        pools_out = at("pools_out", m_pool + 4096, [P, 512])

        h_hi = at("h_hi", RA, [P, DK, T], F32R)
        h_lo = at("h_lo", RB, [P, DK, T], F32R)
        o_hi = at("o_hi", RA, [P, 4, T], F32R)
        o_lo = at("o_lo", RA + 4 * ROW, [P, 4, T], F32R)
        a_hi = at("a_hi", RB, [P, 4, T], F32R)
        a_lo = at("a_lo", RB + 4 * ROW, [P, 4, T], F32R)
        x1 = at("x1", RA, [P, DK, T])
        ff_hi = at("ff_hi", RB, [P, DK, T], F32R)
        xn = at("xn", RA, [P, DK, T])
        h_t = at("h_t", RB, [P, DK, T])
        c_row = at("c_row", RB, [P, D])
        c_sil = at("c_sil", RB + 4096, [P, D])
        v_row = at("v_row", RB + 8192, [P, P])
        s_row = at("s_row", RB + 8704, [P, PW])
        diag1 = at("diag1", RB + 12288, [P, 9, P])
        sq_x = at("sq_x", RB + 17408, [P, D])
        xT = at("xT", RC, [P, DK, T])
        z = at("z", RC, [P, 10, T])
        mg_hi = at("mg_hi", RC, [P, DK, T], F32R)
        mg_lo = at("mg_lo", RC + 8 * ROW, [P, DK, T], F32R)
        h2_hi = at("h2_hi", RC, [P, DK, T], F32R)
        h2_lo = at("h2_lo", RC + 8 * ROW, [P, DK, T], F32R)
        x_in = at("x_in", RE, [P, 4, D])
        c2 = at("c2", RE + 20480, [P, DK, 2 * NC], F32R)
        fold = at("fold", RE + 21056, [P, NC])
        ada_row = at("ada_row", RE + 16384, [P, 2, 512])
        bias_p = at("bias_p", RE, [P, NH, 2 * P])
        pr = at("pr", RE + 8192, [P, 2, G, 2 * P])
        pt_hi = at("pt_hi", RE + 16384, [P, 2, G * P], F32R)
        pt_lo = at("pt_lo", RE + 20480, [P, 2, G * P], F32R)
        ks_hi = at("ks_hi", RE, [P, SK], F32R)
        ks_lo = at("ks_lo", RE + 4224, [P, SK], F32R)
        ps = at("ps", RE + 8448, [P, 2, SK])
        pst_hi = at("pst_hi", RE + 16896, [P, 9, P], F32R)
        ada_w = at("ada_w", RD, [P, 2, DK, 512])
        ada_lo = at("ada_lo", RD, [P, 2, DK, 512], F32R)
        ada_hi = [at(f"ada_hi{q}", o, [P, DK // 2, 512], F32R) for q, o in
                  enumerate((RE, RE + 8192, RC + U0 * ROW, RC + U0 * ROW + 8192))]
        q_hi = at("q_hi", RD, [P, 4, P], F32R)
        q_lo = at("q_lo", RD + 2048, [P, 4, P], F32R)
        k_hi = at("k_hi", RD + 4096, [P, 2 * P], F32R)
        k_lo = at("k_lo", RD + 5120, [P, 2 * P], F32R)
        v_hi = at("v_hi", RD + 6144, [P, 2, P], F32R)
        v_lo = at("v_lo", RD + 7168, [P, 2, P], F32R)
        g_out = at("g_out", RD + 8192, [P, 2, T])
        kc = at("kc", RD + 16640, [P, NB, P])
        vc = at("vc", RD + 20736, [P, NB, P])
        bias_s = at("bias_s", RD + 24832, [P, NKV, SK])
        vs_hi = at("vs_hi", RD, [P, 9, P], F32R)
        vs_lo = at("vs_lo", RD + 4608, [P, 9, P], F32R)
        pst_lo = at("pst_lo", RD + 9216, [P, 9, P], F32R)
        qs_hi = at("qs_hi", RD + 13824, [P, 4, TS], F32R)
        qs_lo = at("qs_lo", RD + 14336, [P, 4, TS], F32R)
        d_hi = [at(f"d_hi{s}", RD + ROW * (4 + 2 * s), [P, T], F32R) for s in range(2)]
        d_lo = [at(f"d_lo{s}", RD + ROW * (5 + 2 * s), [P, T], F32R) for s in range(2)]
        wp_raw = at("wp_raw", RE + 21504, [P, NG, P])
        wp_hi = at("wp_hi", RC + KZ * ROW, [P, NG, P], F32R)
        wp_lo = at("wp_lo", RC + KZ * ROW + 2048, [P, NG, P], F32R)
        a_t = at("a_t", RC + VZ * ROW, [P, 2, TM])
        g_in = at("g_in", RD, [P, 2, 2, T])
        mt = at("mt", RD + 4 * ROW, [P, 2, 3, TM])
        x_res = at("x_res", RD, [P, 2, T])
        sq_t = at("sq_t", RD + 2 * ROW, [P, 3, TM])
        nrm_t2 = at("nrm_t2", RD + 4 * ROW, [P, 2, TM])
        diag2 = at("diag2", RD + 5 * ROW, [P, 9, P])
        ff_lo = at("ff_lo", RD, [P, DK, T], F32R)
        r_t = at("r_t", m_pool, [P, 2, TM])
        f_t = at("f_t", m_pool + 8 * TM, [P, 2, TM])
        wd_hi = [w_hi[0]] + [at(f"wd_hi{j}", RC + 8192 * j, [P, DK, P], F32R) for j in range(1, DK)]
        wd_lo = [w_lo[0]] + [at(f"wd_lo{j}", RC + 8192 * j + 4096, [P, DK, P], F32R) for j in range(1, DK)]
        fin_g = at("fin_g", RW + 12288, [P, D])
        y_sq = at("y_sq", RW + 20480, [P, D])
        y_out = [at("y_out0", m_pool, [P, D]), at("y_out1", m_pool + 4096, [P, D]), at("y_out2", RC, [P, D])]

        psum = ctx.enter_context(nc.psum_tensor("psum", [P, 8, 512], F32))

        gates_d = nc.dram_tensor("gates_scratch", [8, P, 2, T], F32, kind="Internal").ap()
        xT_d = nc.dram_tensor("xT_scratch", [P, DK, T], F32, kind="Internal").ap()

        w_in = [sem("w_in0"), sem("w_in1")]
        w_hi_done, w_lo_done = sem("w_hi_done"), sem("w_lo_done")
        ready = [sem(f"ready{t}") for t in range(3)]
        free = [sem(f"free{t}") for t in range(3)]
        readyB = [sem(f"readyB{t}") for t in range(3)]
        freeB = [sem(f"freeB{t}") for t in range(3)]
        c_in, v_in, s_in, tab_in = sem("c_in"), sem("v_in"), sem("s_in"), sem("tab_in")
        x_land = [sem(f"x_land{s}") for s in range(4)]
        x_sq, xt_ready, xt_read, xt_saved = sem("x_sq"), sem("xt_ready"), sem("xt_read"), sem("xt_saved")
        const_done, c_sig, c_silu = sem("const_done"), sem("c_sig"), sem("c_silu")
        cvt_ready, cvt_read, st_ready, st_read = sem("cvt_ready"), sem("cvt_read"), sem("st_ready"), sem("st_read")
        ada_in = [[sem(f"ada_in{s}{hf}") for hf in range(2)] for s in range(2)]
        row_ready, row_read, modt_ready, mod_done = sem("row_ready"), sem("row_read"), sem("modt_ready"), sem("mod_done")
        ms_done, rms_done, diag_done = sem("ms_done"), sem("rms_done"), sem("diag_done")
        gain_done, xn_done, t_dve, t_act, n_hi, h_done, hs_done = (
            sem("gain_done"), sem("xn_done"), sem("t_dve"), sem("t_act"), sem("n_hi"), sem("h_done"), sem("hs_done"))
        c2_hi_done, c2_done, fold_done = sem("c2_hi_done"), sem("c2_done"), sem("fold_done")
        ada_hi_done, ada_lo_done, ada_used = sem("ada_hi_done"), sem("ada_lo_done"), sem("ada_used")
        pool_done = sem("pool_done")
        stage_done, vt_ready, v_hi_done, v_lo_done = sem("stage_done"), sem("vt_ready"), sem("v_hi_done"), sem("v_lo_done")
        s_ready, nmax_done, exp_done, p_done = sem("s_ready"), sem("nmax_done"), sem("exp_done"), sem("p_done")
        pt_ready, pt_hi_done, pt_lo_done, o_ready, o_read = sem("pt_ready"), sem("pt_hi_done"), sem("pt_lo_done"), sem("o_ready"), sem("o_read")
        g_saved, kvc_in, bs_in, bp_in = sem("g_saved"), sem("kvc_in"), sem("bs_in"), sem("bp_in")
        out_t_ready, out_t_read, kct_ready, kct_hi, ks_done, vs_done, qs_done = (
            sem("out_t_ready"), sem("out_t_read"), sem("kct_ready"), sem("kct_hi"), sem("ks_done"), sem("vs_done"), sem("qs_done"))
        sst_ready, sst_hi, sst_lo, so_ready, so_read = sem("sst_ready"), sem("sst_hi"), sem("sst_lo"), sem("so_ready"), sem("so_read")
        ss_nmax, ss_exp, ss_p = sem("ss_nmax"), sem("ss_exp"), sem("ss_p")
        d_hi_done, d_lo_done, o_hi_done, o_lo_done = sem("d_hi_done"), sem("d_lo_done"), sem("o_hi_done"), sem("o_lo_done")
        a_hi_done, a_lo_done = sem("a_hi_done"), sem("a_lo_done")
        g_in_sem, sig_done, sum_done, mg_hi_done, mg_lo_done = (
            [sem("g_in0"), sem("g_in1")], sem("sig_done"), sem("sum_done"), sem("mg_hi_done"), sem("mg_lo_done"))
        xr_in, x1_done, sq_done, acc_done = [sem("xr_in0"), sem("xr_in1")], sem("x1_done"), sem("sq_done"), sem("acc_done")
        ff_sq, ff_hi_done, ff_lo_done = sem("ff_sq"), sem("ff_hi_done"), sem("ff_lo_done")
        x_last, yt_ready, yss_done, yms_done, yr_done, y_done, fg_in = (
            sem("x_last"), sem("yt_ready"), sem("yss_done"), sem("yms_done"), sem("yr_done"), sem("y_done"), sem("fg_in"))
        y_sent = [sem("y_sent0"), sem("y_sent1"), sem("y_sent2")]
        n2_tmp, n2_hi, h2_done, h2s_done, ss_ready, diag2_done = (
            sem("n2_tmp"), sem("n2_hi"), sem("h2_done"), sem("h2s_done"), sem("ss_ready"), sem("diag2_done"))
        qk_lo_done = sem("qk_lo_done")
        wp_in, wp_done = sem("wp_in"), sem("wp_done")
        sent = sem("sent")
        act_c, dve_c, pool_c = sem("act_chain"), sem("dve_chain"), sem("pool_chain")

        def cols(t):
            return slice(TC[t], TC[t] + TW[t])

        ada_col = [0, 2, 1, 3] + list(range(4, 12))

        block = ctx.enter_context(nc.Block())

        @block.sync
        def _(sp):
            def load_x(b):
                rows = P if b < BLK else TS
                if b >= 4:
                    sp.wait_ge(x_sq, b - 3)
                    sp.wait_ge(xt_ready, b - 3)
                src = a["x_prompt"][0, b * P:(b + 1) * P, :] if b < BLK else a["x_sample"].rearrange("b t d -> (b t) d")
                sp.dma_start(x_in[0:rows, b % 4, :], src).then_inc(x_land[b % 4], 16)

            def load_ada(n, col):
                wait(sp, row_ready, n - 1)
                for hf in range(2):
                    k = slice(hf * DK // 2, (hf + 1) * DK // 2)
                    sp.dma_start(ada_w[:, n % 2, k, :], a["w_ada"][0, :, col].rearrange("(k p) c -> p k c", p=P)[:, k, :]).then_inc(ada_in[n % 2][hf], 16)

            def col(n):
                return slice(ada_col[n] * 512, ada_col[n] * 512 + 512)

            def load_w(slot, src, free_count):
                wait(sp, w_lo_done, free_count)
                sp.dma_start(w_raw[slot][:, :, :], src.rearrange("(k p) c -> p k c", p=P)).then_inc(w_in[slot], 16)

            w_in_d, z_col = a["w_in"][0], [PW + NH * HD, PW + NH * HD + NKV * HD] + [None] * 4 + [g * P for g in range(NG)]

            def load_z(u):
                if z_col[u] is not None:
                    load_w(u % 2, w_in_d[:, z_col[u]:z_col[u] + P], u - 1)
                    return
                wait(sp, w_lo_done, u - 1)
                c = PW + (u - 2) * HD
                src = w_in_d[:, PW:PW + NH * HD].rearrange("(k p) (v g c) -> p k v g c", p=P, v=NKV, g=G)[:, :, :, u - 2, :]
                sp.dma_start(w_raw[u % 2][:, :, 0:HD], src[:, :, 0, :]).then_inc(w_in[u % 2], 16)
                sp.dma_start(w_raw[u % 2][:, :, HD:P], src[:, :, 1, :]).then_inc(w_in[u % 2], 16)

            for b in range(9):
                load_x(b)
            load_ada(0, col(0))
            load_ada(1, col(1))
            load_z(0)
            load_z(1)
            load_ada(2, col(2))
            load_ada(3, col(3))
            load_z(2)
            load_ada(4, col(4))
            sp.wait_ge(xt_read, 9)
            sp.dma_start(xT_d, xT[:, :, :]).then_inc(xt_saved, 16)
            load_ada(5, col(5))
            for u in range(3, 6):
                load_z(u)
                load_ada(2 * u, col(2 * u))
                load_ada(2 * u + 1, col(2 * u + 1))
            for u in range(6, N_Z):
                load_z(u)
            z0 = 2 * PW + 2 * NKV * HD

            def gate_loads(i, g_from):
                load_w(0, w_in_d[:, bass.ds(z0 + i * P, P)], g_from)
                load_w(1, w_in_d[:, bass.ds(z0 + D + i * P, P)], g_from + 1)

            gate_loads(0, U_G - 1)
            sp.wait_ge(mod_done, 12)
            sp.dma_start(bias_p[:, :, :], a["alibi_prompt"]).then_inc(bp_in, 16)
            sp.dma_start(kc[:, :, :], a["cache_k"][0].rearrange("b w h d -> w b (h d)")).then_inc(kvc_in, 16)
            sp.dma_start(vc[:, :, :], a["cache_v"][0].rearrange("b w h d -> w b (h d)")).then_inc(kvc_in, 16)
            sp.dma_start(bias_s[:, :, :], a["alibi_sample"]).then_inc(bs_in, 16)
            for cache, new in ((a["cache_k"], nk_s), (a["cache_v"], nv_s)):
                sp.dma_start(new[0, :, 0:WIN - NT].rearrange("b w h d -> b w (h d)"),
                             cache[0, :, NT:WIN].rearrange("b w h d -> b w (h d)")).then_inc(sent, 16)
            def gate_store(i):
                for t in range(3):
                    sp.wait_ge(free[t], USE_Z + U_G + 2 * i + 2)
                sp.dma_start(gates_d[bass.ds(i, 1)].rearrange("o p g t -> (o p) g t"), g_out[:, :, :]).then_inc(g_saved, 16)

            with sp.Fori(1, BLK) as i:
                gate_loads(i, U_G - 1 + 2 * i)
                gate_store(i - 1)

            def load_ab(j, slot, free_count):
                wait(sp, w_lo_done, free_count)
                c = bass.ds(j * P, P)
                sp.dma_start(w_raw[slot][:, 0:4, :], a["w_a"][0][:, c].rearrange("(k p) c -> p k c", p=P)).then_inc(w_in[slot], 16)
                w_b = a["w_b"][0][:, c].rearrange("(v g p) c -> v p g c", v=NKV, g=G)
                for v in range(NKV):
                    sp.dma_start(w_raw[slot][v * HD:(v + 1) * HD, 4:8, :], w_b[v]).then_inc(w_in[slot], 16)

            load_ab(0, 0, U_AB - 1)
            load_ab(1, 1, U_AB)
            gate_store(BLK - 1)
            sp.wait_ge(o_ready, 2 * BLK)
            sp.dma_start(wp_raw[:, :, :], a["w_pool"][0].rearrange("g c d -> c g d")).then_inc(wp_in, 16)
            sp.wait_ge(out_t_read, 4)
            sp.dma_start(nk_p[0, 0].rearrange("w h d -> w (h d)"), kv_out[:, 0:P]).then_inc(sent, 16)
            sp.dma_start(nv_p[0, 0].rearrange("w h d -> w (h d)"), kv_out[:, P:2 * P]).then_inc(sent, 16)
            for new, c in ((nk_s, 2 * P), (nv_s, 3 * P)):
                for b in range(NB):
                    sp.dma_start(new[0, b, WIN - NT:WIN].rearrange("w h d -> w (h d)"), kv_out[b * NT:(b + 1) * NT, c:c + P]).then_inc(sent, 16)
            sp.dma_start(npool_p[0, 0], poolp_out[0:PAD, :]).then_inc(sent, 16)
            sp.dma_start(npool_s[0].rearrange("b r c -> (b r) c"), pools_out[0:NB * PAD, :]).then_inc(sent, 16)

            def gates_back(j, slot):
                wait(sp, free[2], USE_AB + j - 1)
                sp.dma_start(g_in[:, slot, :, :], gates_d[bass.ds(j, 1)].rearrange("o p g t -> (o p) g t")).then_inc(g_in_sem[slot], 16)

            sp.wait_ge(g_saved, 16 * BLK)
            sp.wait_ge(so_ready, 2)
            gates_back(0, 0)
            gates_back(1, 1)
            w_out_d = a["w_out"][0]
            with sp.Fori(1, 4) as p:
                load_ab(2 * p, 0, U_AB - 1 + 2 * p)
                gates_back(2 * p, 0)
                load_ab(2 * p + 1, 1, U_AB + 2 * p)
                gates_back(2 * p + 1, 1)
            load_w(0, w_out_d[:, 0:P], U_O - 1)
            load_w(1, w_out_d[:, P:2 * P], U_O)
            sp.wait_ge(xt_saved, 16)

            def load_res(j, slot):
                wait(sp, x1_done, j - 1)
                sp.dma_start(x_res[:, slot, :], xT_d[:, bass.ds(j, 1), :].rearrange("p o t -> p (o t)")).then_inc(xr_in[slot], 16)

            sp.wait_ge(mg_lo_done, 3 * N_AB)
            load_res(0, 0)
            load_res(1, 1)
            with sp.Fori(1, 4) as p:
                load_w(0, w_out_d[:, bass.ds(2 * p * P, P)], U_O - 1 + 2 * p)
                load_res(2 * p, 0)
                load_w(1, w_out_d[:, bass.ds((2 * p + 1) * P, P)], U_O + 2 * p)
                load_res(2 * p + 1, 1)
            w_up_d, w_down_d = a["w_up"][0], a["w_down"][0]
            with sp.Fori(0, 4) as g:
                with sp.Fori(0, 4) as i:
                    for s in range(2):
                        load_w(s, w_up_d[:, bass.ds((8 * g + 2 * i + s) * P, P)], U_F - 1 + 16 * g + 2 * i + s)
                with sp.Fori(0, 4) as i:
                    for s in range(2):
                        load_w(s, w_down_d[bass.ds(g * D, D), bass.ds((2 * i + s) * P, P)], U_F + 7 + 16 * g + 2 * i + s)
            for t in range(3):
                sp.wait_ge(ready[t], USE_F + 56)
            sp.dma_start(fin_g[:, :], a["final_g"].partition_broadcast(P)).then_inc(fg_in, 16)
            for b in range(BLK + 1):
                sp.wait_ge(y_done, b + 1)
                dst = y_p[0, b * P:(b + 1) * P, :] if b < BLK else y_s.rearrange("b t d -> (b t) d")
                sp.dma_start(dst, y_out[b % 3][0:P if b < BLK else TS, :]).then_inc(y_sent[b % 3], 16)
            for s in range(3):
                sp.wait_ge(y_sent[s], 16 * 3)
            sp.wait_ge(sent, 16 * (2 + 2 + 16 + 2))

        @block.tensor
        def _(pe):
            mm = nc.tensor.matmul

            def mm3(out, whi, wlo, rhi, rlo, first, last):
                mm(out, whi, rhi, start=first, stop=False)
                mm(out, whi, rlo, start=False, stop=False)
                return mm(out, wlo, rhi, start=False, stop=last)

            def project(u, use, slot, rhi, rlo, before=None, tiles=(0, 1, 2)):
                pe.wait_ge(w_lo_done, u + 1)
                for t in tiles:
                    if before:
                        before(t)
                    pe.wait_ge(free[t], use)
                    for k in range(DK):
                        last = mm3(psum[:, t, 0:TW[t]], w_hi[slot][:, k, :], w_lo[slot][:, k, :], rhi[:, k, cols(t)], rlo[:, k, cols(t)], k == 0, k == DK - 1)
                    last.then_inc(ready[t], 1)

            pe.wait_ge(const_done, 4)
            pe.wait_ge(c_silu, 1)
            for j in range(DK):
                nc.tensor.transpose(psum[:, 3, 16 * j:16 * j + NC], c_sil[0:NC, j * P:(j + 1) * P], ident[0:NC, 0:NC])
            pe.wait_ge(v_in, 64)
            nc.tensor.transpose(psum[:, 3, P:P + 68], v_row[0:68, :], ident[0:68, 0:68]).then_inc(cvt_ready, 1)
            pe.wait_ge(s_in, 16)
            for g in range(NG):
                last = nc.tensor.transpose(psum[:, 2, 120 * g:120 * g + 120], s_row[0:120, g * P:(g + 1) * P], ident[0:120, 0:120])
            last.then_inc(st_ready, 1)
            for b in range(BLK + 1):
                rows = P if b < BLK else TS
                pe.wait_ge(x_land[b % 4], 16 * (b // 4 + 1))
                wait(pe, xt_read, b - 1)
                for j in range(DK):
                    bank = 4 + 2 * (b % 2) + j // 4
                    last = nc.tensor.transpose(psum[:, bank, (j % 4) * P:(j % 4) * P + rows], x_in[0:rows, b % 4, j * P:(j + 1) * P], ident[0:rows, 0:rows])
                last.then_inc(xt_ready, 1)

            def ada_rows(n, s):
                wait(pe, row_read, n - 1)
                for k in range(DK):
                    if k % 4 == 0:
                        pe.wait_ge(ada_in[s][k // 4], 16 * (n // 2) + 16)
                    last = mm(psum[0:NC, 3 + s, :], cT[:, k, :], ada_w[:, s, k, :], start=(k == 0), stop=(k == DK - 1))
                last.then_inc(row_ready, 1)

            def ada_row_halves(n, s):
                pe.wait_ge(row_read, n - 1)
                for hf in range(2):
                    pe.wait_ge(ada_lo_done, 2 * (n - 4) + hf + 1)
                    for k in range(DK // 2):
                        kk = hf * DK // 2 + k
                        mm(psum[0:2 * NC, 3 + s, :], c2[:, kk, :], ada_hi[2 * s + hf][:, k, :], start=(kk == 0), stop=False)
                        last = mm(psum[0:2 * NC, 3 + s, :], c2[:, kk, :], ada_lo[:, s, kk, :], start=False, stop=(kk == DK - 1))
                    if hf == 0:
                        last.then_inc(ada_used, 1)
                last.then_inc(row_ready, 1)

            def ada_turn(n, s):
                pe.wait_ge(row_read, n + 1)
                wait(pe, mod_done, n - 1)
                for q in range(4):
                    last = mm(psum[:, 5 + s, 16 * q:16 * q + NC], ada_row[:, s, q * P:(q + 1) * P], (ident[:, 0:NC] if n < 4 else fold[:, :]), start=True, stop=True)
                last.then_inc(modt_ready, 1)

            pe.wait_ge(cvt_read, 2)
            ada_rows(0, 0)
            pe.wait_ge(st_read, 1)

            def spread_rms(diag, use):
                pe.wait_ge(diag_done, 2)
                for t in range(3):
                    wait(pe, free[t], use)
                for t in range(2):
                    mm(psum[:, t, :], ones[:, :], diag[:, 4 * t:4 * t + 4, :], start=True, stop=True).then_inc(ready[t], 1)
                mm(psum[:, 2, 0:TS], ones[0:TS, :], diag[0:TS, 8, 0:TS], start=True, stop=True).then_inc(ready[2], 1)

            pe.wait_ge(xt_read, 9)
            spread_rms(diag1, USE_R1)
            ada_rows(1, 1)
            ada_rows(2, 0)
            ada_turn(0, 0)
            ada_turn(1, 1)
            ada_rows(3, 1)
            ada_turn(2, 0)
            ada_turn(3, 1)

            pe.wait_ge(w_lo_done, 2)
            for t in range(3):
                pe.wait_ge(free[t], 1)
            pe.wait_ge(row_read, 4)
            pe.wait_ge(mod_done, 3)
            for k in range(DK):
                pe.wait_ge(h_done, k + 1)
                if k % 4 == 0:
                    pe.wait_ge(hs_done, k // 4 + 1)
                for t in range(3):
                    for s in range(2):
                        last = mm3(psum[:, 3 * s + t, 0:TW[t]], w_hi[s][:, k, :], w_lo[s][:, k, :], h_hi[:, k, cols(t)], h_lo[:, k, cols(t)], k == 0, k == DK - 1)
                        if k == DK - 1:
                            last.then_inc((ready, readyB)[s][t], 1)
            for t in range(3):
                pe.wait_ge(freeB[t], 1)
            pe.wait_ge(c2_done, 1)
            pe.wait_ge(fold_done, 1)
            for u in range(2, 6):
                project(u, u, u % 2, h_hi, h_lo, tiles=(0,))
                if u > 2:
                    ada_turn(2 * u - 1, 1)
                ada_row_halves(2 * u, 0)
                project(u, u, u % 2, h_hi, h_lo, tiles=(1,))
                ada_turn(2 * u, 0)
                project(u, u, u % 2, h_hi, h_lo, tiles=(2,))
                ada_row_halves(2 * u + 1, 1)
            ada_turn(11, 1)
            for u in range(6, N_Z):
                project(u, u, u % 2, h_hi, h_lo)

            def gate_tile(use, slot, t):
                pe.wait_ge(free[t], use)
                for k in range(DK):
                    last = mm3(psum[:, t, 0:TW[t]], w_hi[slot][:, k, :], w_lo[slot][:, k, :], h_hi[:, k, cols(t)], h_lo[:, k, cols(t)], k == 0, k == DK - 1)
                last.then_inc(ready[t], 1)

            def attend(i):
                first = isinstance(i, int)
                kks = [1] if first else [0, 1]
                k0 = P if first else 0
                u = U_G + 2 * i

                def scores(kv):
                    wait(pe, nmax_done, 2 * i + kv)
                    h = slice(kv * HD, (kv + 1) * HD)
                    for c in range(G):
                        last = mm3(psum[:, 3 + c // 2, (c % 2) * 256 + k0:(c % 2) * 256 + 256], q_hi[h, c, :], q_lo[h, c, :],
                                   k_hi[h, k0:256], k_lo[h, k0:256], True, True)
                    last.then_inc(s_ready, 1)

                def turn_probs(kv):
                    pe.wait_ge(p_done, 2 * i + kv + 1)
                    wait(pe, pt_lo_done, 2 * i + kv)
                    for kk in kks:
                        for c in range(G):
                            last = nc.tensor.transpose(psum[:, 5 + kk, c * P:(c + 1) * P], pr[:, kv, c, kk * P:(kk + 1) * P], ident[:, :])
                    last.then_inc(pt_ready, 1)

                def weigh(kv):
                    pe.wait_ge(pt_lo_done, 2 * i + kv + 1)
                    pe.wait_ge(v_lo_done, i + 1)
                    wait(pe, o_read, 2 * i + kv)
                    for kk in kks:
                        last = mm3(psum[:, 7, :], v_hi[:, kk, :], v_lo[:, kk, :], pt_hi[:, kk, :], pt_lo[:, kk, :], kk == kks[0], kk == 1)
                    last.then_inc(o_ready, 1)

                pe.wait_ge(stage_done, i + 1)
                wait(pe, o_read, 2 * i)
                for kk in kks:
                    last = nc.tensor.transpose(psum[:, 7, kk * P:(kk + 1) * P], v_st[:, kk, :], ident[:, :])
                last.then_inc(vt_ready, 1)
                pe.wait_ge(qk_lo_done, i + 1)
                scores(0)
                pe.wait_ge(w_lo_done, u + 1)
                gate_tile(USE_Z + u, 0, 0)
                gate_tile(USE_Z + u, 0, 1)
                turn_probs(0)
                scores(1)
                gate_tile(USE_Z + u, 0, 2)
                weigh(0)
                pe.wait_ge(w_lo_done, u + 2)
                gate_tile(USE_Z + u + 1, 1, 0)
                gate_tile(USE_Z + u + 1, 1, 1)
                turn_probs(1)
                gate_tile(USE_Z + u + 1, 1, 2)
                weigh(1)

            attend(0)
            with pe.Fori(1, BLK) as i:
                attend(i)

            pe.wait_ge(o_read, 2 * BLK)
            pe.wait_ge(pt_lo_done, 2 * BLK)
            for q, (chunk, c0, n) in enumerate(((KZ, TP - P, P), (VZ, TP - P, P), (KZ, TP, TS), (VZ, TP, TS))):
                last = nc.tensor.transpose(psum[0:n, 5, q * P:(q + 1) * P], z[:, chunk, c0:c0 + n], ident[:, :])
            last.then_inc(out_t_ready, 1)
            pe.wait_ge(pool_done, 1)
            for g in range(NG):
                last = nc.tensor.transpose(psum[0:PAD, 6, g * P:(g + 1) * P], pool_last[:, g, :], ident[:, :])
            last.then_inc(out_t_ready, 1)
            for g in range(NG):
                last = nc.tensor.transpose(psum[0:NB * PAD, 7, g * P:(g + 1) * P], pool_tail[:, g, :], ident[:, :])
            last.then_inc(out_t_ready, 1)
            pe.wait_ge(kvc_in, 32)
            for b in range(NB):
                last = nc.tensor.transpose(psum[:, 3 + b // 4, (b % 4) * P:(b % 4 + 1) * P], kc[:, b, :], ident[:, :])
            last.then_inc(kct_ready, 1)
            pe.wait_ge(ks_done, 1)
            pe.wait_ge(qs_done, 1)
            for kv in range(NKV):
                h = slice(kv * HD, (kv + 1) * HD)
                for t in range(3):
                    pe.wait_ge(free[t], USE_SS + kv)
                    mm3(psum[:, t, 0:TW[t]], qs_hi[h, :, :], qs_lo[h, :, :], ks_hi[h, cols(t)], ks_lo[h, cols(t)], True, True)\
                        .then_inc(ready[t], 1)
            pe.wait_ge(vs_done, 1)
            pe.wait_ge(out_t_read, 4)
            for kv in range(NKV):
                pe.wait_ge(ss_p, kv + 1)
                wait(pe, sst_lo, 2 * kv)
                for cc in range(9):
                    n = P if cc < NB else TS
                    bank = (5, 6, 4)[cc // 4]
                    last = nc.tensor.transpose(psum[0:n, bank, (cc % 4) * P:(cc % 4 + 1) * P], ps[:, kv, cc * P:cc * P + n], ident[:, :])
                last.then_inc(sst_ready, 1)
                pe.wait_ge(sst_lo, 2 * kv + 2)
                wait(pe, so_read, kv)
                for cc in range(9):
                    n = P if cc < NB else TS
                    last = mm3(psum[:, 7, 0:P], vs_hi[0:n, cc, :], vs_lo[0:n, cc, :], pst_hi[0:n, cc, :], pst_lo[0:n, cc, :], cc == 0, cc == 8)
                last.then_inc(so_ready, 1)

            pe.wait_ge(wp_done, 1)
            for g in range(NG):
                pe.wait_ge(d_lo_done, g + 1)
                for t in range(3):
                    pe.wait_ge(free[t], USE_POOL + g)
                    mm3(psum[:, t, 0:TW[t]], wp_hi[:, g, :], wp_lo[:, g, :], d_hi[g % 2][:, cols(t)], d_lo[g % 2][:, cols(t)], True, True)\
                        .then_inc(ready[t], 1)

            def branches(j, slot):
                pe.wait_ge(w_lo_done, U_AB + j + 1)
                for t in range(3):
                    wait(pe, freeB[t], USE_B + j)
                    for k in range(4):
                        last = mm3(psum[:, 3 + t, 0:TW[t]], w_hi[slot][:, 4 + k, :], w_lo[slot][:, 4 + k, :], o_hi[:, k, cols(t)], o_lo[:, k, cols(t)], k == 0, k == 3)
                    last.then_inc(readyB[t], 1)
                    pe.wait_ge(free[t], USE_AB + j)
                    for k in range(4):
                        last = mm3(psum[:, t, 0:TW[t]], w_hi[slot][:, k, :], w_lo[slot][:, k, :], a_hi[:, k, cols(t)], a_lo[:, k, cols(t)], k == 0, k == 3)
                    last.then_inc(ready[t], 1)

            pe.wait_ge(o_lo_done, 4)
            pe.wait_ge(so_read, 2)
            pe.wait_ge(a_lo_done, 12)
            branches(0, 0)
            branches(1, 1)
            with pe.Fori(1, 4) as p:
                branches(2 * p, 0)
                branches(2 * p + 1, 1)

            def merged_there(t):
                pe.wait_ge(mg_lo_done, 3 * (N_AB - 1) + t + 1)

            with pe.Fori(0, 4) as p:
                for s in range(2):
                    project(U_O + 2 * p + s, USE_O + 2 * p + s, s, mg_hi, mg_lo, merged_there)

            for b in range(BLK + 1):
                n, t = (P if b < BLK else TS), b // 3
                c0 = b * P - TC[t]
                pe.wait_ge(acc_done, 3 * (N_O - 2) + t + 2)
                mm(psum[0:n, 6, b:b + 1], acc[:, b * P:b * P + n], ones[:, 0:1], start=True, stop=False)
                pe.wait_ge(sq_done, 3 * (N_O - 1) + t + 1)
                last = mm(psum[0:n, 6, b:b + 1], sq_t[:, t, c0:c0 + n], ones[:, 0:1], start=False, stop=True)
            last.then_inc(ss_ready, 1)
            for t in range(3):
                pe.wait_ge(diag2_done, t + 1)
                pe.wait_ge(free[t], USE_R2)
                n = min(3, BLK - 3 * t)
                last = mm(psum[:, t, 0:n * P], ones[:, :], diag2[:, 3 * t:3 * t + n, :], start=True, stop=True)
                if t == 2:
                    last = mm(psum[:, t, n * P:TW[t]], ones[0:TS, :], diag2[0:TS, BLK, 0:TS], start=True, stop=True)
                last.then_inc(ready[t], 1)

            pe.wait_ge(w_lo_done, U_F + 2)
            for t in range(3):
                pe.wait_ge(free[t], USE_R2 + 1)
                pe.wait_ge(freeB[t], USE_B + N_AB)
                if t == 2:
                    pe.wait_ge(h2s_done, 1)
                for k in range(DK):
                    if k % 2 == 0:
                        pe.wait_ge(h2_done, 8 * t + k + 2)
                    for s in range(2):
                        last = mm3(psum[:, 3 * s + t, 0:TW[t]], w_hi[s][:, k, :], w_lo[s][:, k, :], h2_hi[:, k, cols(t)], h2_lo[:, k, cols(t)], k == 0, k == DK - 1)
                        if k == DK - 1:
                            last.then_inc((ready, readyB)[s][t], 1)

            def up(g, i):
                for s in range(2):
                    n = 16 * g + 2 * i + s
                    project(U_F + n, USE_F + n, s, h2_hi, h2_lo)

            def down(g):
                def ff_there(t):
                    pe.wait_ge(ff_lo_done, 24 * g + 22 + t)

                with pe.Fori(0, 4) as i:
                    for s in range(2):
                        n = 16 * g + 8 + 2 * i + s
                        project(U_F + n, USE_F + n, s, ff_hi, ff_lo, ff_there)

            with pe.Fori(1, 4) as i:
                up(0, i)
            down(0)
            with pe.Fori(1, 3) as g:
                with pe.Fori(0, 4) as i:
                    up(g, i)
                down(g)
            with pe.Fori(0, 4) as i:
                up(3, i)

            def turn_back(b, bank):
                n = P if b < BLK else TS
                wait(pe, y_done, b - 1)
                for j in range(DK):
                    last = nc.tensor.transpose(psum[0:n, bank + j // 4, (j % 4) * P:(j % 4 + 1) * P], x1[:, j, b * P:b * P + n], ident[:, :])
                last.then_inc(yt_ready, 1)

            for t in range(3):
                pe.wait_ge(ff_lo_done, 24 * 3 + 22 + t)
                for j in range(DK):
                    n = DK * t + j
                    pe.wait_ge(w_lo_done, U_F + 56 + j + 1)
                    pe.wait_ge(free[n % 3], USE_F + 56 + n // 3)
                    for k in range(DK):
                        last = mm3(psum[:, n % 3, 0:TW[t]], wd_hi[j][:, k, :], wd_lo[j][:, k, :], ff_hi[:, k, cols(t)], ff_lo[:, k, cols(t)], k == 0, k == DK - 1)
                    last.then_inc(ready[n % 3], 1)
                    if t and j in (0, 2, 4):
                        b = 3 * (t - 1) + j // 2
                        if j == 0:
                            for m in range(DK * t - 3, DK * t):
                                pe.wait_ge(free[m % 3], USE_F + 56 + m // 3 + 1)
                        turn_back(b, 3 + 2 * (b % 2))
            pe.wait_ge(x_last, DK)
            turn_back(6, 3)
            turn_back(7, 5)
            for t in range(3):
                pe.wait_ge(free[t], USE_F + 64)
            turn_back(8, 0)

        @block.scalar
        def _(act):
            copy = nc.scalar.copy
            fn = nc.scalar.activation

            act.dma_start(c_row[0:1, :], a["c_prompt"]).then_inc(c_in, 16)
            act.dma_start(c_row[1:NC, :], a["c_sample"]).then_inc(c_in, 16)
            for r0, n, name in ((0, NMOD, "b_ada"), (NMOD, DK, "norm1_g"), (NMOD + DK, DK, "norm2_g"), (NMOD + 2 * DK, NG, "pool_scale")):
                act.dma_start(v_row[r0:r0 + n, :], a[name].rearrange("o (j p) -> (o j) p", p=P)).then_inc(v_in, 16)
            act.dma_start(s_row[0:NB * PAD, :], a["state_pool"][0].rearrange("b r c -> (b r) c")).then_inc(s_in, 16)
            act.dma_start(sink_p[:, :], a["attn_sinks"][0].partition_broadcast(P)).then_inc(tab_in, 16)
            for g in range(G):
                act.dma_start(sink_s[g * TS:(g + 1) * TS, :], a["attn_sinks"][0].rearrange("(v g) -> g v", g=G)[g].partition_broadcast(TS), allow_slow_non_contiguous=True).then_inc(tab_in, 16)
            act.dma_start(inv_cnt[:, :, :].rearrange("p g c -> p (g c)"), a["inv_count"].partition_broadcast(P)).then_inc(tab_in, 16)

            act.wait_ge(c_in, 32)
            fn(c_sil[0:NC, :], c_row[0:NC, :], ACT.Sigmoid).then_inc(c_sig, 1)
            act.wait_ge(cvt_ready, 1)
            fn(cT[:, :, :], psum[:, 3, 0:P].rearrange("p (j c) -> p j c", c=16)[:, :, 0:NC], ACT.Copy).then_inc(cvt_read, 1)
            fn(vec[:, :], psum[:, 3, P:P + 68], ACT.Copy).then_inc(cvt_read, 1)
            act.wait_ge(cvt_read, 1)
            fn(c2[:, :, 0:NC], cT[:, :, :], ACT.Copy).then_inc(c2_hi_done, 1)
            act.wait_ge(st_ready, 1)
            fn(pool_s[:, :, :, 0:PAD], psum[:, 2, 0:480].rearrange("p (g b r) -> p g b r", g=NG, b=NB), ACT.Copy).then_inc(st_read, 1)
            for b in range(BLK + 1):
                n = P if b < BLK else TS
                act.wait_ge(xt_ready, b + 1)
                for hf in range(2):
                    last = fn(xT[:, 4 * hf:4 * hf + 4, b * P:b * P + n],
                              psum[:, 4 + 2 * (b % 2) + hf, :].rearrange("p (j c) -> p j c", c=P)[:, :, 0:n], ACT.Copy)
                last.then_inc(xt_read, 1)

            def ada_copy(n, s):
                act.wait_ge(row_ready, n + 1)
                wait(act, modt_ready, n - 1)
                rows = NC if n < 4 else 2 * NC
                fn(ada_row[0:rows, s, :], psum[0:rows, 3 + s, :], ACT.Copy).then_inc(row_read, 1)

            def split_hi(u, slot, loads, use):
                act.wait_ge(w_in[slot], loads)
                wait(act, ready[2], use)
                fn(w_hi[slot][:, :, :], w_raw[slot][:, :, :], ACT.Copy).then_inc(w_hi_done, 1)

            def rms_copies(use):
                for t in range(2):
                    act.wait_ge(ready[t], use + 1)
                    fn(R[:, 512 * t:512 * t + 512], psum[:, t, :], ACT.Copy).then_inc(free[t], 1)
                act.wait_ge(ready[2], use + 1)
                fn(R[:, TP:T], psum[:, 2, 0:TS], ACT.Copy).then_inc(free[2], 1)

            ada_copy(0, 0)
            rms_copies(USE_R1)
            split_hi(0, 0, loads_of(0), 0)
            split_hi(1, 1, loads_of(1), 0)
            ada_copy(1, 1)
            ada_copy(2, 0)
            for hf in range(2):
                act.wait_ge(gain_done, hf + 1)
                for p in range(2):
                    j = 4 * hf + 2 * p
                    act.wait_ge(xn_done, j + 2)
                    fn(h_t[:, j + 1, 0:TP], xn[:, j + 1, 0:TP], ACT.Identity, scale=gain1[:, j + 1, 0:1], bias=mod[:, j + 1, 0:1]).then_inc(t_act, 1)
                    act.wait_ge(t_dve, 2 * hf + p + 1)
                    fn(h_hi[:, j, 0:TP], xn[:, j, 0:TP], ACT.Identity, scale=gain1[:, j, 0:1], bias=mod[:, j, 0:1]).then_inc(n_hi, 1)
                    act.wait_ge(t_act, 2 * hf + p + 1)
                    fn(h_hi[:, j + 1, 0:TP], xn[:, j + 1, 0:TP], ACT.Identity, scale=gain1[:, j + 1, 0:1], bias=mod[:, j + 1, 0:1]).then_inc(n_hi, 1)
                if hf == 0:
                    ada_copy(3, 1)

            def z_tiles(u, tiles=(0, 1, 2)):
                for t in tiles:
                    bank, done, read = (3 + t, readyB[t], freeB[t]) if u == 1 else (t, ready[t], free[t])
                    act.wait_ge(done, (2, 1)[u] if u < 2 else u + 1)
                    fn(z[:, Z_ROW[u], cols(t)], psum[:, bank, 0:TW[t]], ACT.Copy).then_inc(read, 1)

            def ada_high(n, s):
                for hf in range(2):
                    act.wait_ge(ada_in[s][hf], 16 * (n // 2) + 16)
                    if n >= 6:
                        act.wait_ge(row_ready, n - 1)
                    fn(ada_hi[2 * s + hf][:, :, :], ada_w[:, s, hf * DK // 2:(hf + 1) * DK // 2, :], ACT.Copy).then_inc(ada_hi_done, 1)

            act.wait_ge(row_ready, 4)
            ada_high(4, 0)
            z_tiles(0)
            act.wait_ge(xt_saved, 16)
            act.wait_ge(hs_done, 2)
            split_hi(2, 0, loads_of(2), 2)
            z_tiles(1)
            act.wait_ge(readyB[2], 1)
            split_hi(3, 1, loads_of(3), 0)
            for u in range(2, N_Z):
                if u >= 3:
                    split_hi(u + 1, (u + 1) % 2, loads_of(u + 1), u)
                if u < 6:
                    z_tiles(u, (0,))
                    ada_copy(2 * u, 0)
                    ada_high(2 * u + 1, 1)
                    z_tiles(u, (1, 2))
                    if u < 5:
                        ada_high(2 * u + 2, 0)
                    ada_copy(2 * u + 1, 1)
                else:
                    z_tiles(u)

            def gate_copy(i, which, t):
                act.wait_ge(ready[t], USE_Z + U_G + 2 * i + which + 1)
                fn(g_out[:, which, cols(t)], psum[:, t, 0:TW[t]], ACT.Copy).then_inc(free[t], 1)

            def attend(i, last_turn=False):
                first = isinstance(i, int) and i == 0
                k0 = P if first else 0
                kks = [1] if first else [0, 1]
                u = U_G + 2 * i

                def exps(kv):
                    act.wait_ge(nmax_done, 2 * i + kv + 1)
                    for c in range(G):
                        fn(pr[:, kv, c, k0:256], pr[:, kv, c, k0:256], ACT.Exp, bias=nmx[:, kv, c:c + 1], accum_out=rsum[:, kv, c:c + 1])
                    fn(esk[:, kv, :], dsk[:, kv, :], ACT.Exp).then_inc(exp_done, 1)

                def pt_halves(kv):
                    act.wait_ge(pt_ready, 2 * i + kv + 1)
                    wait(act, o_ready, 2 * i + kv)
                    fn(pt_hi[:, kks[0]:2, :], psum[:, 5 + kks[0]:7, :], ACT.Copy).then_inc(pt_hi_done, 1)

                def o_copy(kv):
                    act.wait_ge(o_ready, 2 * i + kv + 1)
                    h = slice(kv * HD, (kv + 1) * HD)
                    fn(z[h, Q0:Q0 + G, bass.ds(i * P, P)], psum[h, 7, :].rearrange("p (c t) -> p c t", c=G), ACT.Copy).then_inc(o_read, 1)

                split_hi(u + 1, 1, 16 * (U_G // 2) + 48 + 16 * i, USE_Z + u)
                act.wait_ge(vt_ready, i + 1)
                wait(act, o_ready, 2 * i)
                fn(v_hi[:, kks[0]:2, :], psum[:, 7, kks[0] * P:256].rearrange("p (k c) -> p k c", c=P), ACT.Copy).then_inc(v_hi_done, 1)
                exps(0)
                wait(act, g_saved, 16 * i)
                gate_copy(i, 0, 0)
                gate_copy(i, 0, 1)
                pt_halves(0)
                gate_copy(i, 0, 2)
                split_hi(u + 2, 0, loads_of(U_AB) if last_turn else 16 * (U_G // 2) + 64 + 16 * i, USE_Z + u + 1)
                exps(1)
                o_copy(0)
                gate_copy(i, 1, 0)
                gate_copy(i, 1, 1)
                pt_halves(1)
                gate_copy(i, 1, 2)
                o_copy(1)

            attend(0)
            with act.Fori(1, BLK - 1) as i:
                attend(i)
            attend(BLK - 1, last_turn=True)

            act.wait_ge(out_t_ready, 1)
            fn(kv_out[:, 0:256], psum[:, 5, 0:256], ACT.Copy).then_inc(out_t_read, 1)
            fn(kv_out[0:TS, 256:512], psum[0:TS, 5, 256:512], ACT.Copy).then_inc(out_t_read, 1)
            act.wait_ge(out_t_ready, 2)
            fn(poolp_out[0:PAD, :], psum[0:PAD, 6, :], ACT.Copy).then_inc(out_t_read, 1)
            act.wait_ge(out_t_ready, 3)
            fn(pools_out[0:NB * PAD, :], psum[0:NB * PAD, 7, :], ACT.Copy).then_inc(out_t_read, 1)
            act.wait_ge(kct_ready, 1)
            fn(ks_hi[:, 0:NB * WIN].rearrange("p (b k) -> p b k", b=2), psum[:, 3:5, :], ACT.Copy).then_inc(kct_hi, 1)
            fn(ks_hi[:, NB * WIN:SK], z[:, KZ, TP:T], ACT.Copy).then_inc(kct_hi, 1)
            for kv in range(NKV):
                act.wait_ge(ss_nmax, kv + 1)
                fn(ps[:, kv, :], ps[:, kv, :], ACT.Exp, bias=nmx[:, kv, 0:1], accum_out=rsum[:, kv, 0:1])
                fn(esk[:, kv, 0:1], dsk[:, kv, 0:1], ACT.Exp).then_inc(ss_exp, 1)

            def d_half(g):
                act.wait_ge(ready[2], USE_POOL + g - 1 if g >= 2 else USE_SS + 2)
                fn(d_hi[g % 2][:, :], z[:, U0 + g, :], ACT.Copy).then_inc(d_hi_done, 1)

            act.wait_ge(pool_done, 1)
            act.wait_ge(vs_done, 1)
            act.wait_ge(ss_p, 1)
            for kv in range(NKV):
                act.wait_ge(sst_ready, kv + 1)
                wait(act, so_ready, kv)
                fn(pst_hi[:, 0:NB, :].rearrange("p (b k) c -> p b (k c)", b=2), psum[:, 5:7, :], ACT.Copy).then_inc(sst_hi, 1)
                fn(pst_hi[0:TS, NB, :], psum[0:TS, 4, 0:P], ACT.Copy).then_inc(sst_hi, 1)
                d_half(kv)
                act.wait_ge(so_ready, kv + 1)
                h = slice(kv * HD, (kv + 1) * HD)
                fn(z[h, Q0:Q0 + G, TP:T], psum[h, 7, 0:P].rearrange("p (c t) -> p c t", c=G), ACT.Copy).then_inc(so_read, 1)
            act.wait_ge(so_read, 2)
            for g in range(NG):
                fn(o_hi[:, g, :], z[:, Q0 + g, :], ACT.Copy).then_inc(o_hi_done, 1)
                if g >= 2:
                    d_half(g)
                for t in range(3):
                    n = 3 * g + t
                    act.wait_ge(ready[t], USE_POOL + g + 1)
                    wait(act, a_lo_done, n - 1)
                    fn(a_t[:, n % 2, 0:TW[t]], psum[:, t, 0:TW[t]], ACT.Identity, scale=vec[:, NMOD + 2 * DK + g:NMOD + 2 * DK + g + 1])\
                        .then_inc(free[t], 1)
                    act.wait_ge(free[t], USE_POOL + g + 1)
                    fn(a_hi[:, g, cols(t)], a_t[:, n % 2, 0:TW[t]], ACT.Copy).then_inc(a_hi_done, 1)

            def gate_halves(j, slot, turn, loads, use):
                act.wait_ge(g_in_sem[slot], 16 * turn + 16)
                fn(g_in[:, slot, :, :], g_in[:, slot, :, :], ACT.Sigmoid).then_inc(sig_done, 1)
                split_hi(0, 1 - slot, loads, use)
                for t in range(3):
                    act.wait_ge(sum_done, 3 * j + t + 1)
                    fn(mg_hi[:, bass.ds(j, 1), cols(t)].rearrange("p o t -> p (o t)"), mt[:, 0, t, 0:TW[t]], ACT.Copy).then_inc(mg_hi_done, 1)

            with act.Fori(0, 3) as p:
                gate_halves(2 * p, 0, p, LOADS_AB + 48 + 48 * p, USE_AB + 2 * p)
                gate_halves(2 * p + 1, 1, p, LOADS_AB + 96 + 48 * p, USE_AB + 1 + 2 * p)
            gate_halves(6, 0, 3, loads_of(U_AB + 7), USE_AB + 6)
            gate_halves(7, 1, 3, loads_of(U_O), USE_AB + 7)

            with act.Fori(0, 4) as p:
                for s in range(2):
                    j = 2 * p + s
                    split_hi(0, 1 - s, LOADS_O + 16 + 16 * (p + s), USE_O + j)
                    for t in range(3):
                        act.wait_ge(free[t], USE_O + j + 1)
                        if t == 2:
                            act.wait_ge(x1_done, j + 1)
                        act.wait_ge(acc_done, 3 * j + 1)
                        fn(sq_t[:, t, 0:TW[t]], x1[:, bass.ds(j, 1), cols(t)].rearrange("p o t -> p (o t)"), ACT.Square).then_inc(sq_done, 1)

            split_hi(0, 1, LOADS_O + 80, USE_O + 8)

            for t in range(3):
                n = min(TW[t], TP - TC[t])
                if t == 0:
                    for r in range(3):
                        act.wait_ge(ready[r], USE_R2 + 1)
                        fn(R[:, cols(r)], psum[:, r, 0:TW[r]], ACT.Copy).then_inc(free[r], 1)
                with act.Fori(0, 4) as q:
                    for s in range(2):
                        j = 2 * q + s
                        act.wait_ge(n2_tmp, 8 * t + j + 1)
                        fn(h2_hi[:, bass.ds(j, 1), TC[t]:TC[t] + n].rearrange("p o t -> p (o t)"), nrm_t2[:, s, 0:n], ACT.Identity,
                           bias=mod[:, bass.ds(3 * DK + j, 1), 0:1].rearrange("p o c -> p (o c)")).then_inc(n2_hi, 1)
            act.wait_ge(h2s_done, 1)
            act.wait_ge(h2_done, 24)

            def ff_tiles(g, j, s):
                side = isinstance(j, int) and g == 0 and j < 2
                for t in range(3):
                    n = 24 * g + 3 * j + t
                    sl = (3 * s + t) % 2
                    done, read, bank, use = ready[t], free[t], t, USE_F + 16 * g + j
                    if side:
                        done, read, bank, use = (ready[t], free[t], t, USE_F + 1) if j == 0 else (readyB[t], freeB[t], 3 + t, USE_B + N_AB)
                    act.wait_ge(done, use + 1)
                    wait(act, ff_sq, n - 1)
                    wait(act, ff_hi_done, n - 1)
                    fn(r_t[:, sl, 0:TW[t]], psum[:, bank, 0:TW[t]], ACT.Relu).then_inc(read, 1)
                    act.wait_ge(read, use + 1)
                    fn(ff_hi[:, bass.ds(j, 1), cols(t)].rearrange("p o t -> p (o t)"), r_t[:, sl, 0:TW[t]], ACT.Square).then_inc(ff_hi_done, 1)

            def up(g, i):
                for s in range(2):
                    split_hi(0, 1 - s, LOADS_O + 80 + 128 * g + 16 * i + 16 * s, USE_F + 16 * g + 2 * i + s)
                    ff_tiles(g, 2 * i + s, s)

            def down(g):
                with act.Fori(0, 4) as i:
                    for s in range(2):
                        split_hi(0, 1 - s, LOADS_O + 144 + 128 * g + 16 * i + 16 * s, USE_F + 8 + 16 * g + 2 * i + s)

            ff_tiles(0, 0, 0)
            split_hi(0, 0, LOADS_O + 96, USE_F + 2)
            ff_tiles(0, 1, 1)
            act.wait_ge(readyB[2], USE_B + N_AB + 1)
            split_hi(0, 1, LOADS_O + 96, 0)
            ff_tiles(0, 2, 0)
            split_hi(0, 0, LOADS_O + 112, USE_F + 3)
            ff_tiles(0, 3, 1)
            with act.Fori(2, 4) as i:
                up(0, i)
            down(0)
            with act.Fori(1, 3) as g:
                with act.Fori(0, 4) as i:
                    up(g, i)
                down(g)
            with act.Fori(0, 4) as i:
                up(3, i)
            for j in range(1, DK):
                act.wait_ge(w_in[j % 2], loads_of(U_F + 56 + j))
                for t in range(3):
                    wait(act, ready[t], USE_F + 56)
                fn(wd_hi[j][:, :, :], w_raw[j % 2][:, :, :], ACT.Copy).then_inc(w_hi_done, 1)

            for b in range(BLK + 1):
                n = P if b < BLK else TS
                bank = 0 if b == BLK else 3 + 2 * (b % 2)
                act.wait_ge(yt_ready, b + 1)
                wait(act, yss_done, b)
                wait(act, y_done, b - 2)
                act.wait_ge(w_lo_done, N_U)
                fn(y_sq[0:n, :], psum[0:n, bank:bank + 2, :], ACT.Square, accum_out=fin_ss[0:n, b % 3, :]).then_inc(yss_done, 1)

        @block.vector
        def _(dve):
            tt, ts_, stt = nc.vector.tensor_tensor, nc.vector.tensor_scalar, nc.vector.scalar_tensor_tensor
            ch = Chain(dve, dve_c)

            def f(t):
                return t.bitcast(F32)

            dve.wait_ge(c_sig, 1)
            tt(c_sil[0:NC, :], c_sil[0:NC, :], c_row[0:NC, :], ALU.mult).then_inc(c_silu, 1)
            for b in range(BLK + 1):
                n = P if b < BLK else TS
                dve.wait_ge(x_land[b % 4], 16 * (b // 4 + 1))
                wait(dve, x_sq, b)
                nc.vector.tensor_tensor_reduce(out=sq_x[0:n, :], in0=x_in[0:n, b % 4, :], in1=x_in[0:n, b % 4, :], scale=1.0, scalar=0.0,
                                               op0=ALU.mult, op1=ALU.add, accum_out=ssq[0:n, b:b + 1]).then_inc(x_sq, 1)

            def diagonals(diag):
                dve.wait_ge(rms_done, 2)
                tt(diag[:, 0:BLK, :], ident[:, :].unsqueeze(1).to_broadcast([P, BLK, P]), ssq[:, 0:BLK].unsqueeze(2).to_broadcast([P, BLK, P]), ALU.mult)\
                    .then_inc(diag_done, 1)
                tt(diag[0:TS, BLK, 0:TS], ident[0:TS, 0:TS], ssq[0:TS, BLK:BLK + 1].to_broadcast([TS, TS]), ALU.mult).then_inc(diag_done, 1)

            dve.wait_ge(x_sq, 9)
            ts_(rms[:, 0:BLK], ssq[:, 0:BLK], 1.0 / D, EPS, ALU.mult, ALU.add)
            ts_(rms[0:TS, BLK:BLK + 1], ssq[0:TS, BLK:BLK + 1], 1.0 / D, EPS, ALU.mult, ALU.add).then_inc(ms_done, 1)
            dve.wait_ge(const_done, 4)
            diagonals(diag1)

            def ada_add(n, s, col):
                dve.wait_ge(modt_ready, n + 1)
                tt(mod[:, 4 * col:4 * col + 4, :], psum[:, 5 + s, 0:64].rearrange("p (q c) -> p q c", c=16)[:, :, 0:NC],
                   vec[:, 4 * col:4 * col + 4].unsqueeze(2).to_broadcast([P, 4, NC]), ALU.add).then_inc(mod_done, 1)
                dve.wait_ge(mod_done, n + 1)

            def gains(gain, j0, n, scale_chunk, g_chunk):
                stt(gain[:, j0:j0 + n, :], mod[:, scale_chunk + j0:scale_chunk + j0 + n, :], 1.0,
                    vec[:, g_chunk + j0:g_chunk + j0 + n].unsqueeze(2).to_broadcast([P, n, NC]), ALU.add, ALU.mult).then_inc(gain_done, 1)
                dve.wait_ge(gain_done, {0: 1, 4: 2}[j0] if n == 4 else 3)

            def split_lo(u, slot):
                dve.wait_ge(w_hi_done, u + 1)
                tt(w_lo[slot][:, :, :], w_raw[slot][:, :, :], f(w_hi[slot][:, :, :]), ALU.subtract).then_inc(w_lo_done, 1)

            dve.wait_ge(c2_hi_done, 1)
            tt(c2[:, :, NC:2 * NC], cT[:, :, :], f(c2[:, :, 0:NC]), ALU.subtract).then_inc(c2_done, 1)
            for t in range(3):
                dve.wait_ge(free[t], USE_R1 + 1)
            dve.wait_ge(xt_read, 9)
            for j in range(DK):
                tt(xn[:, j, 0:TP], xT[:, j, 0:TP], R[:, 0:TP], ALU.mult).then_inc(xn_done, 1)
            split_lo(0, 0)
            split_lo(1, 1)
            for hf in range(2):
                ada_add(2 * hf, 0, ada_col[2 * hf])
                ada_add(2 * hf + 1, 1, ada_col[2 * hf + 1])
                gains(gain1, 4 * hf, 4, DK, NMOD)
                for p in range(2):
                    j = 4 * hf + 2 * p
                    if p == 0:
                        dve.wait_ge(xn_done, j + 3)
                    ts_(h_t[:, j, 0:TP], xn[:, j, 0:TP], gain1[:, j, 0:1], mod[:, j, 0:1], ALU.mult, ALU.add).then_inc(t_dve, 1)
                for q in range(4):
                    j = 4 * hf + q
                    dve.wait_ge(n_hi, j + 1)
                    if q == 0:
                        dve.wait_ge(t_dve, 2 * hf + 2)
                    tt(h_lo[:, j, 0:TP], h_t[:, j, 0:TP], f(h_hi[:, j, 0:TP]), ALU.subtract).then_inc(h_done, 1)

            def ada_low(n, s):
                for hf in range(2):
                    dve.wait_ge(ada_hi_done, 2 * (n - 4) + hf + 1)
                    k = slice(hf * DK // 2, (hf + 1) * DK // 2)
                    tt(ada_lo[:, s, k, :], ada_w[:, s, k, :], f(ada_hi[2 * s + hf][:, :, :]), ALU.subtract).then_inc(ada_lo_done, 1)

            def pool_group(g):
                w = 2 << g
                u = z[:, U0 + g, :]
                for t in range(3):
                    dve.wait_ge(free[t], USE_Z + 6 + g + 1)
                us = u[:, TP:T].rearrange("p (b t) -> p b t", t=NT)
                ch.step(nc.vector.tensor_copy(pool_last[:, g, :], u[:, TP - PAD:TP]))
                ch.step(nc.vector.tensor_copy(pool_s[:, g, :, PAD:PAD + NT], us))
                cur, cur_s, lag = u[:, 0:TP], pool_s[:, g, :, :], 1
                bufs, bufs_s = [win_a, win_b], [win_sa, win_sb]
                while lag < w:
                    new, new_s = bufs[0][:, :], bufs_s[0][:, :, :]
                    bufs.reverse()
                    bufs_s.reverse()
                    tt(new[:, lag:TP], cur[:, lag:TP], cur[:, 0:TP - lag], ALU.add)
                    nc.vector.tensor_copy(new[:, 0:lag], cur[:, 0:lag])
                    ch.step(tt(new_s[:, :, 2 * lag - 1:], cur_s[:, :, 2 * lag - 1:], cur_s[:, :, lag - 1:PAD + NT - lag], ALU.add))
                    cur, cur_s, lag = new, new_s, 2 * lag
                ch.step(tt(cur[:, 0:16], cur[:, 0:16], inv_cnt[:, g, :], ALU.mult))
                tt(u[:, 0:16], cur[:, 0:16], u[:, 0:16], ALU.subtract)
                stt(u[:, 16:TP], cur[:, 16:TP], 1.0 / w, u[:, 16:TP], ALU.mult, ALU.subtract)
                last = stt(us, cur_s[:, :, PAD:PAD + NT], 1.0 / w, us, ALU.mult, ALU.subtract)
                ch.step(last)

            dve.wait_ge(tab_in, 16 * 6)
            ada_low(4, 0)
            split_lo(2, 0)
            split_lo(3, 1)
            for u in range(2, N_Z):
                if u >= 3:
                    split_lo(u + 1, (u + 1) % 2)
                if u < 6:
                    ada_low(2 * u + 1, 1)
                    ada_add(2 * u, 0, 2 * u)
                    if u < 5:
                        ada_low(2 * u + 2, 0)
                    ada_add(2 * u + 1, 1, 2 * u + 1)
                if u >= 7:
                    pool_group(u - 7)
            gains(gain2, 0, DK, 4 * DK, NMOD + DK)
            pool_group(3)

            nc.vector.tensor_copy(pool_tail[:, :, :].rearrange("p g (b r) -> p g b r", b=NB), pool_s[:, :, :, NT:PAD + NT]).then_inc(pool_done, 1)

            def attend(i):
                first = isinstance(i, int)
                k0 = P if first else 0
                kks = [1] if first else [0, 1]
                nk = 2 * P - k0
                u = U_G + 2 * i

                def soft_a(kv):
                    dve.wait_ge(s_ready, 2 * i + kv + 1)
                    wait(dve, pt_ready, 2 * i + kv - 1 if not first else 0)
                    s_all = psum[:, 3:5, :].rearrange("p b (c k) -> p (b c) k", k=256)
                    ch.step(stt(pr[:, kv, :, k0:256], s_all[:, :, k0:256], SCALE, bias_p[:, G * kv:G * kv + G, k0:256], ALU.mult, ALU.add))
                    ch.step(nc.vector.tensor_reduce(mx[:, kv, :], pr[:, kv, :, k0:256], AX.X, ALU.max))
                    ch.step(tt(mx[:, kv, :], mx[:, kv, :], sink_p[:, G * kv:G * kv + G], ALU.max))
                    ts_(nmx[:, kv, :], mx[:, kv, :], -1.0, None, ALU.mult)
                    tt(dsk[:, kv, :], sink_p[:, G * kv:G * kv + G], mx[:, kv, :], ALU.subtract).then_inc(nmax_done, 1)

                def soft_b(kv):
                    dve.wait_ge(exp_done, 2 * i + kv + 1)
                    ch.step(tt(rden[:, kv, :], rsum[:, kv, :], esk[:, kv, :], ALU.add))
                    ch.step(nc.vector.reciprocal(rden[:, kv, :], rden[:, kv, :]))
                    tt(pr[:, kv, :, k0:256], pr[:, kv, :, k0:256], rden[:, kv, :].unsqueeze(2).to_broadcast([P, G, nk]), ALU.mult).then_inc(p_done, 1)

                def pt_low(kv):
                    dve.wait_ge(pt_hi_done, 2 * i + kv + 1)
                    tt(pt_lo[:, kks[0]:2, :], psum[:, 5 + kks[0]:7, :], f(pt_hi[:, kks[0]:2, :]), ALU.subtract).then_inc(pt_lo_done, 1)

                dve.wait_ge(stage_done, i + 1)
                keys = slice(0, P) if first else bass.ds(i * P - P, 2 * P)
                tt(q_lo[:, :, :], z[:, Q0:Q0 + G, bass.ds(i * P, P)], f(q_hi[:, :, :]), ALU.subtract)
                tt(k_lo[:, k0:256], z[:, KZ, keys], f(k_hi[:, k0:256]), ALU.subtract).then_inc(qk_lo_done, 1)
                split_lo(u + 1, 1)
                dve.wait_ge(v_hi_done, i + 1)
                tt(v_lo[:, kks[0]:2, :], psum[:, 7, kks[0] * P:256].rearrange("p (k c) -> p k c", c=P), f(v_hi[:, kks[0]:2, :]), ALU.subtract)\
                    .then_inc(v_lo_done, 1)
                soft_a(0)
                soft_b(0)
                pt_low(0)
                soft_a(1)
                split_lo(u + 2, 0)
                soft_b(1)
                pt_low(1)

            dve.wait_ge(bp_in, 16)
            attend(0)
            per = 2 * 5
            with dve.Fori(1, BLK) as i:
                ch.enter(i, 1, per)
                attend(i)
            ch.leave(BLK - 1, per)

            dve.wait_ge(kct_hi, 2)
            tt(ks_lo[:, 0:NB * WIN].rearrange("p (b k) -> p b k", b=2), psum[:, 3:5, :], f(ks_hi[:, 0:NB * WIN]).rearrange("p (b k) -> p b k", b=2), ALU.subtract)
            tt(ks_lo[:, NB * WIN:SK], z[:, KZ, TP:T], f(ks_hi[:, NB * WIN:SK]), ALU.subtract).then_inc(ks_done, 1)
            dve.wait_ge(bs_in, 16)
            for kv in range(NKV):
                for t in range(3):
                    dve.wait_ge(ready[t], USE_SS + kv + 1)
                    ins = stt(ps[:, kv, cols(t)], psum[:, t, 0:TW[t]], SCALE, bias_s[:, kv, cols(t)], ALU.mult, ALU.add)
                    ins.then_inc(free[t], 1)
                for t in range(3):
                    dve.wait_ge(free[t], USE_SS + kv + 1)
                ch.step(nc.vector.tensor_reduce(mx[:, kv, 0:1], ps[:, kv, :], AX.X, ALU.max))
                ch.step(tt(mx[:, kv, 0:1], mx[:, kv, 0:1], sink_s[:, kv:kv + 1], ALU.max))
                ts_(nmx[:, kv, 0:1], mx[:, kv, 0:1], -1.0, None, ALU.mult)
                tt(dsk[:, kv, 0:1], sink_s[:, kv:kv + 1], mx[:, kv, 0:1], ALU.subtract).then_inc(ss_nmax, 1)
            for kv in range(NKV):
                dve.wait_ge(ss_exp, kv + 1)
                ch.step(tt(rden[:, kv, 0:1], rsum[:, kv, 0:1], esk[:, kv, 0:1], ALU.add))
                ch.step(nc.vector.reciprocal(rden[:, kv, 0:1], rden[:, kv, 0:1]))
                ts_(ps[:, kv, :], ps[:, kv, :], rden[:, kv, 0:1], None, ALU.mult).then_inc(ss_p, 1)

            def d_low(g):
                dve.wait_ge(d_hi_done, g + 1)
                tt(d_lo[g % 2][:, :], z[:, U0 + g, :], f(d_hi[g % 2][:, :]), ALU.subtract).then_inc(d_lo_done, 1)

            for kv in range(NKV):
                dve.wait_ge(sst_hi, 2 * kv + 2)
                tt(pst_lo[:, 0:NB, :].rearrange("p (b k) c -> p b (k c)", b=2), psum[:, 5:7, :], f(pst_hi[:, 0:NB, :]).rearrange("p (b k) c -> p b (k c)", b=2), ALU.subtract)\
                    .then_inc(sst_lo, 1)
                tt(pst_lo[0:TS, NB, :], psum[0:TS, 4, 0:P], f(pst_hi[0:TS, NB, :]), ALU.subtract).then_inc(sst_lo, 1)
                d_low(kv)
            for g in range(NG):
                dve.wait_ge(o_hi_done, g + 1)
                tt(o_lo[:, g, :], z[:, Q0 + g, :], f(o_hi[:, g, :]), ALU.subtract).then_inc(o_lo_done, 1)
                if g >= 2:
                    d_low(g)
                for t in range(3):
                    n = 3 * g + t
                    dve.wait_ge(a_hi_done, n + 1)
                    tt(a_lo[:, g, cols(t)], a_t[:, n % 2, 0:TW[t]], f(a_hi[:, g, cols(t)]), ALU.subtract).then_inc(a_lo_done, 1)

            def gated(j, u, slot):
                def lo(t):
                    dve.wait_ge(mg_hi_done, 3 * j + t + 1)
                    tt(mg_lo[:, bass.ds(j, 1), cols(t)].rearrange("p o t -> p (o t)"), mt[:, 0, t, 0:TW[t]],
                       f(mg_hi[:, bass.ds(j, 1), cols(t)]).rearrange("p o t -> p (o t)"), ALU.subtract).then_inc(mg_lo_done, 1)

                split_lo(u + 1, 1 - slot)
                dve.wait_ge(sig_done, j + 1)
                for t in range(3):
                    dve.wait_ge(readyB[t], USE_B + j + 1)
                    wait(dve, mg_lo_done, 3 * j + t - 2)
                    tt(mt[:, 1, t, 0:TW[t]], psum[:, 3 + t, 0:TW[t]], g_in[:, slot, 1, cols(t)], ALU.mult).then_inc(freeB[t], 1)
                    dve.wait_ge(ready[t], USE_AB + j + 1)
                    tt(mt[:, 0, t, 0:TW[t]], psum[:, t, 0:TW[t]], g_in[:, slot, 0, cols(t)], ALU.mult).then_inc(free[t], 1)
                    if t:
                        lo(t - 1)
                lo(2)

            gated(0, U_AB, 0)
            gated(1, U_AB + 1, 1)
            with dve.Fori(1, 4) as p:
                for s in range(2):
                    gated(2 * p + s, U_AB + 2 * p + s, s)

            def add_gated(j, t, use, gate_chunk, res, count, bank=None, done=None):
                x = x1[:, bass.ds(j, 1), :].rearrange("p o t -> p (o t)")
                gt = mod[:, bass.ds(gate_chunk + j, 1), :].rearrange("p o c -> p (o c)")
                bank = t if bank is None else bank
                dve.wait_ge(ready[bank], use + 1)
                n = min(TW[t], TP - TC[t])
                c0 = TC[t]
                if t == 2:
                    ch.step(tt(smp_t[:, 0, :, :], psum[:, bank, n:TW[2]].rearrange("p (b t) -> p b t", t=NT), gt[:, 1:NC].unsqueeze(2).to_broadcast([P, NB, NT]), ALU.mult))
                last = stt(x[:, c0:c0 + n], psum[:, bank, 0:n], gt[:, 0:1], res[:, c0:c0 + n], ALU.mult, ALU.add)
                last.then_inc(free[bank], 1)
                if done is not None:
                    if t == 2:
                        tt(x[:, TP:T], smp_t[:, 0, :, :].rearrange("p b t -> p (b t)"), res[:, TP:T], ALU.add).then_inc(done, 1)
                        dve.wait_ge(done, count)
                elif t == 2:
                    tt(x[:, TP:T], smp_t[:, 0, :, :].rearrange("p b t -> p (b t)"), res[:, TP:T], ALU.add).then_inc(x1_done, 1)
                    dve.wait_ge(x1_done, count)

            per = 2
            with dve.Fori(0, 4) as p:
                ch.enter(p, 0, per)
                for s in range(2):
                    j = 2 * p + s
                    split_lo(U_O + j + 1, 1 - s)
                    dve.wait_ge(xr_in[s], 16 * p + 16)
                    for t in range(3):
                        add_gated(j, t, USE_O + j, 2 * DK, x_res[:, s, :], j + 1)
            ch.leave(4, per)

            split_lo(U_F + 1, 1)
            dve.wait_ge(ss_ready, 1)
            ts_(rms[:, 0:BLK], psum[:, 6, 0:BLK], 1.0 / D, EPS, ALU.mult, ALU.add)
            ts_(rms[0:TS, BLK:BLK + 1], psum[0:TS, 6, BLK:BLK + 1], 1.0 / D, EPS, ALU.mult, ALU.add).then_inc(ms_done, 1)
            dve.wait_ge(rms_done, 4)
            for t in range(3):
                n = min(3, BLK - 3 * t)
                last = tt(diag2[:, 3 * t:3 * t + n, :], ident[:, :].unsqueeze(1).to_broadcast([P, n, P]), ssq[:, 3 * t:3 * t + n].unsqueeze(2).to_broadcast([P, n, P]), ALU.mult)
                if t == 2:
                    last = tt(diag2[0:TS, BLK, 0:TS], ident[0:TS, 0:TS], ssq[0:TS, BLK:BLK + 1].to_broadcast([TS, TS]), ALU.mult)
                last.then_inc(diag2_done, 1)
            for t in range(3):
                dve.wait_ge(free[t], USE_R2 + 1)
                n = min(TW[t], TP - TC[t])
                tile = slice(TC[t], TC[t] + n)

                def pair(m, j, first):
                    for s in range(2):
                        if not first:
                            dve.wait_ge(h2_done, m + s - 1)
                        stt(nrm_t2[:, s, 0:n], x1[:, bass.ds(j + s, 1), tile].rearrange("p o t -> p (o t)"),
                            gain2[:, bass.ds(j + s, 1), 0:1].rearrange("p o c -> p (o c)"), R[:, tile], ALU.mult, ALU.mult).then_inc(n2_tmp, 1)
                    for s in range(2):
                        dve.wait_ge(n2_hi, m + s + 1)
                        stt(h2_lo[:, bass.ds(j + s, 1), tile].rearrange("p o t -> p (o t)"), nrm_t2[:, s, 0:n],
                            mod[:, bass.ds(3 * DK + j + s, 1), 0:1].rearrange("p o c -> p (o c)"),
                            f(h2_hi[:, bass.ds(j + s, 1), tile]).rearrange("p o t -> p (o t)"), ALU.add, ALU.subtract).then_inc(h2_done, 1)

                if t == 0:
                    pair(0, 0, True)
                    with dve.Fori(1, 4) as q:
                        pair(2 * q, 2 * q, False)
                else:
                    with dve.Fori(0, 4) as q:
                        pair(8 * t + 2 * q, 2 * q, False)

            def ff_tiles(g, j, s):
                side = isinstance(j, int) and g == 0 and j < 2
                for t in range(3):
                    n = 24 * g + 3 * j + t
                    sl = (3 * s + t) % 2
                    read, use = free[t], USE_F + 16 * g + j
                    if side:
                        read, use = (free[t], USE_F + 1) if j == 0 else (freeB[t], USE_B + N_AB)
                    dve.wait_ge(read, use + 1)
                    wait(dve, ff_lo_done, n - 1)
                    tt(f_t[:, sl, 0:TW[t]], r_t[:, sl, 0:TW[t]], r_t[:, sl, 0:TW[t]], ALU.mult).then_inc(ff_sq, 1)
                    dve.wait_ge(ff_sq, n + 1)
                    dve.wait_ge(ff_hi_done, n + 1)
                    tt(ff_lo[:, bass.ds(j, 1), cols(t)].rearrange("p o t -> p (o t)"), f_t[:, sl, 0:TW[t]],
                       f(ff_hi[:, bass.ds(j, 1), cols(t)]).rearrange("p o t -> p (o t)"), ALU.subtract).then_inc(ff_lo_done, 1)

            def up(g, i):
                for s in range(2):
                    split_lo(U_F + 16 * g + 2 * i + s + 1, 1 - s)
                    ff_tiles(g, 2 * i + s, s)

            def down(g):
                with dve.Fori(0, 4) as i:
                    ch.enter(i, 0, 2)
                    for s in range(2):
                        j = 2 * i + s
                        split_lo(U_F + 16 * g + 8 + j + 1, 1 - s)
                        for t in range(3):
                            add_gated(j, t, USE_F + 16 * g + 8 + j, 5 * DK, x1[:, bass.ds(j, 1), :].rearrange("p o t -> p (o t)"), N_O + 8 * g + j + 1)
                ch.leave(4, 2)

            ff_tiles(0, 0, 0)
            split_lo(U_F + 2, 0)
            ff_tiles(0, 1, 1)
            split_lo(U_F + 3, 1)
            ff_tiles(0, 2, 0)
            split_lo(U_F + 4, 0)
            ff_tiles(0, 3, 1)
            with dve.Fori(2, 4) as i:
                up(0, i)
            down(0)
            outer = ch.base + ch.k
            with dve.Fori(1, 3) as g:
                ch.base, ch.k = outer + (g - 1) * 8, 0
                with dve.Fori(0, 4) as i:
                    up(g, i)
                down(g)
            ch.base, ch.k = outer + 2 * 8, 0
            with dve.Fori(0, 4) as i:
                up(3, i)

            def y_rms(b):
                n = P if b < BLK else TS
                dve.wait_ge(yss_done, b + 1)
                ts_(fin_r[0:n, b % 3, :], fin_ss[0:n, b % 3, :], 1.0 / D, EPS, ALU.mult, ALU.add).then_inc(yms_done, 1)

            def y_block(b):
                n = P if b < BLK else TS
                bank = 0 if b == BLK else 3 + 2 * (b % 2)
                dve.wait_ge(yr_done, b + 1)
                if b >= 3:
                    dve.wait_ge(y_sent[b % 3], 16 * (b // 3))
                stt(y_out[b % 3][0:n, :], psum[0:n, bank:bank + 2, :].rearrange("p b c -> p (b c)"), fin_ss[0:n, b % 3, :], fin_g[0:n, :], ALU.mult, ALU.mult)\
                    .then_inc(y_done, 1)

            for t in range(3):
                for j in range(DK):
                    n = DK * t + j
                    if t == 0 and j + 1 < DK:
                        dve.wait_ge(w_hi_done, U_F + 56 + j + 2)
                        tt(wd_lo[j + 1][:, :, :], w_raw[(j + 1) % 2][:, :, :], f(wd_hi[j + 1][:, :, :]), ALU.subtract).then_inc(w_lo_done, 1)
                    add_gated(j, t, USE_F + 56 + n // 3, 5 * DK, x1[:, j, :], j + 1, bank=n % 3, done=x_last)
                    b = 3 * (t - 1) + (j - 1) // 2
                    if t and j in (1, 3, 5):
                        if b == 0:
                            dve.wait_ge(fg_in, 16)
                        y_rms(b)
                    if t and j in (2, 4, 6):
                        y_block(b)
            for b in (6, 7, 8):
                y_rms(b)
                y_block(b)

        @block.gpsimd
        def _(pool):
            tt = nc.gpsimd.tensor_tensor
            cp = nc.gpsimd.tensor_copy
            ch = Chain(pool, pool_c)

            def f(t):
                return t.bitcast(F32)

            ch.step(nc.gpsimd.memset(ident[:, :], 0.0))
            nc.gpsimd.affine_select(out=ident[:, :], in_=ident[:, :], compare_op=ALU.not_equal, fill=1.0, base=0, pattern=[[-1, P]],
                                    channel_multiplier=1).then_inc(const_done, 1)
            nc.gpsimd.memset(ada_row[:, :, :], 0.0).then_inc(const_done, 1)
            nc.gpsimd.memset(ones[:, :], 1.0).then_inc(const_done, 1)
            nc.gpsimd.memset(half[:, :], -0.5).then_inc(const_done, 1)
            pool.wait_ge(const_done, 4)
            tt(fold[:, :], ident[:, 0:NC], ident[:, NC:2 * NC], ALU.add).then_inc(fold_done, 1)

            def powers(n):
                pool.wait_ge(ms_done, n + 1)
                tt(ssq[:, 0:BLK], rms[:, 0:BLK], half[:, 0:BLK], ALU.pow).then_inc(rms_done, 1)
                tt(ssq[0:TS, BLK:BLK + 1], rms[0:TS, BLK:BLK + 1], half[0:TS, 0:1], ALU.pow).then_inc(rms_done, 1)

            powers(0)

            def norm_samples(src, gain, dst_hi, dst_lo, shift, j0, j1, done):
                def v(t):
                    return t.rearrange("p j (b t) -> p j b t", t=NT)

                j, n = slice(j0, j1), j1 - j0
                smp, flat = smp_t[:, j, :, :], smp_t[:, j, :, :].rearrange("p j b t -> p j (b t)")
                ch.step(tt(smp, v(src[:, j, TP:T]), gain[:, j, 1:NC].unsqueeze(3).to_broadcast([P, n, NB, NT]), ALU.mult))
                ch.step(tt(flat, flat, R[:, TP:T].unsqueeze(1).to_broadcast([P, n, TS]), ALU.mult))
                ch.step(tt(smp, smp, mod[:, shift + j0:shift + j1, 1:NC].unsqueeze(3).to_broadcast([P, n, NB, NT]), ALU.add))
                ch.step(cp(dst_hi[:, j, TP:T], flat))
                tt(dst_lo[:, j, TP:T], flat, f(dst_hi[:, j, TP:T]), ALU.subtract).then_inc(done, 1)

            for hf in range(2):
                pool.wait_ge(gain_done, hf + 1)
                norm_samples(xT, gain1, h_hi, h_lo, 0, 4 * hf, 4 * hf + 4, hs_done)

            def stage(i):
                first = isinstance(i, int)
                k0 = P if first else 0
                keys = slice(0, P) if first else bass.ds(i * P - P, 2 * P)
                blk = bass.ds(i * P, P)
                wait(pool, s_ready, 2 * i)
                wait(pool, vt_ready, i)
                cp(q_hi[:, :, :], z[:, Q0:Q0 + G, blk])
                cp(k_hi[:, k0:256], z[:, KZ, keys])
                cp(v_st[:, k0 // P:2, :].rearrange("p k c -> p (k c)"), z[:, VZ, keys]).then_inc(stage_done, 1)

            for t in range(3):
                pool.wait_ge(free[t], USE_Z + 6)
            pool.wait_ge(mod_done, 12)
            stage(0)
            with pool.Fori(1, BLK) as i:
                stage(i)

            pool.wait_ge(g_saved, 16 * BLK)
            pool.wait_ge(o_ready, 2 * BLK)
            ch.step(cp(qs_hi[:, :, :], z[:, Q0:Q0 + G, TP:T]))
            tt(qs_lo[:, :, :], z[:, Q0:Q0 + G, TP:T], f(qs_hi[:, :, :]), ALU.subtract).then_inc(qs_done, 1)
            pool.wait_ge(kvc_in, 32)
            ch.step(cp(vs_hi[:, 0:NB, :], vc[:, :, :]))
            tt(vs_lo[:, 0:NB, :], vc[:, :, :], f(vs_hi[:, 0:NB, :]), ALU.subtract)
            pool.wait_ge(out_t_read, 2)
            ch.step(cp(vs_hi[0:TS, NB, :], kv_out[0:TS, 3 * P:4 * P]))
            tt(vs_lo[0:TS, NB, :], kv_out[0:TS, 3 * P:4 * P], f(vs_hi[0:TS, NB, :]), ALU.subtract).then_inc(vs_done, 1)
            pool.wait_ge(ks_done, 1)
            pool.wait_ge(wp_in, 16)
            ch.step(cp(wp_hi[:, :, :], wp_raw[:, :, :]))
            tt(wp_lo[:, :, :], wp_raw[:, :, :], f(wp_hi[:, :, :]), ALU.subtract).then_inc(wp_done, 1)

            with pool.Fori(0, N_AB) as j:
                for t in range(3):
                    pool.wait_ge(free[t], USE_AB + j + 1)
                    tt(mt[:, 0, t, 0:TW[t]], mt[:, 0, t, 0:TW[t]], mt[:, 1, t, 0:TW[t]], ALU.add).then_inc(sum_done, 1)

            pool.wait_ge(sent, 16 * 22)
            nc.gpsimd.memset(acc[:, :], 0.0).then_inc(acc_done, 1)
            with pool.Fori(0, N_O - 1) as j:
                for t in range(3):
                    pool.wait_ge(sq_done, 3 * j + t + 1)
                    pool.wait_ge(acc_done, 3 * j + t + 1)
                    tt(acc[:, cols(t)], acc[:, cols(t)], sq_t[:, t, 0:TW[t]], ALU.add).then_inc(acc_done, 1)
            powers(1)
            pool.wait_ge(free[2], USE_R2 + 1)
            norm_samples(x1, gain2, h2_hi, h2_lo, 3 * DK, 0, DK, h2s_done)
            for b in range(BLK + 1):
                n = P if b < BLK else TS
                pool.wait_ge(yms_done, b + 1)
                tt(fin_ss[0:n, b % 3, :], fin_r[0:n, b % 3, :], half[0:n, 0:1], ALU.pow).then_inc(yr_done, 1)


_INS = ["x_prompt", "x_sample", "cache_k", "cache_v", "state_pool", "c_prompt", "c_sample", "w_ada", "b_ada", "norm1_g", "w_in", "w_pool",
        "pool_scale", "attn_sinks", "w_a", "w_b", "w_out", "norm2_g", "w_up", "w_down", "final_g"]
_OUTS = [(1, TP, D), (NB, NT, D), (1, 1, WIN, NKV, HD), (1, 1, WIN, NKV, HD), (1, 1, PAD, PW),
         (1, NB, WIN, NKV, HD), (1, NB, WIN, NKV, HD), (1, NB, PAD, PW)]


def _shape_tables(np):
    slopes = 2.0 ** (-8.0 * (np.arange(NH) + 1) / NH)
    dist = np.arange(P)[:, None] + P - np.arange(2 * P)[None, :]
    seen = (dist >= 0) & (dist < WIN)
    prompt = np.where(seen[:, None, :], -slopes[None, :, None] * dist[:, None, :], -1e30).astype(np.float32)
    row = np.arange(P)
    g, seq, tok = row // TS, (row % TS) // NT, row % NT
    key = np.arange(SK)
    new = key >= NB * WIN
    key_seq = np.where(new, (key - NB * WIN) // NT, key // WIN)
    key_pos = np.where(new, (key - NB * WIN) % NT, key % WIN - WIN)
    dist = tok[:, None] - key_pos[None, :]
    seen = (dist >= 0) & (dist < WIN) & (seq[:, None] == key_seq[None, :])
    sample = np.stack([np.where(seen, -slopes[v * G + g][:, None] * dist, -1e30) for v in range(NKV)], axis=1).astype(np.float32)
    pos = np.arange(16)
    inv = np.stack([1.0 / np.minimum(2 << n, pos + 1) for n in range(NG)]).astype(np.float32).reshape(-1)
    return {"alibi_prompt": prompt, "alibi_sample": sample, "inv_count": inv}


def kernel(**inputs):
    import numpy as _np
    import concourse.bacc as _bacc
    from concourse import mybir as _mybir
    from concourse.bass_utils import run_bass_kernel_spmd as _run

    nc = _bacc.Bacc("TRN2", target_bir_lowering=False, num_devices=1)
    arrays, args = {}, {}
    given = {name: _np.ascontiguousarray(inputs[name]) for name in _INS}
    given.update(_shape_tables(_np))
    for name, x in given.items():
        arrays[f"in_{name}_dram"] = x
        args[name] = nc.dram_tensor(f"in_{name}_dram", x.shape, _mybir.dt.from_np(x.dtype), kind="ExternalInput").ap()
    outs = [nc.dram_tensor(f"out_{i}_dram", shape, _mybir.dt.float32, kind="ExternalOutput").ap() for i, shape in enumerate(_OUTS)]
    hybrid_decoder_step(nc, args, outs)
    r = _run(nc, [arrays], core_ids=[0])
    return tuple(r.results[0][f"out_{i}_dram"] for i in range(len(_OUTS)))
```
